# Optimizing a Trainium2 kernel written in Bass

```python
import math
import jax
import jax.numpy as jnp
from jax import lax
import numpy as np

D_MODEL = 1024
BATCH = 1
SEQ = 512
DEPTH = 2

HEAD_DIM = 64
MIX_GROUP_WIDTH = D_MODEL // 2

NSA_HEADS = MIX_GROUP_WIDTH // HEAD_DIM
NSA_KV_GROUPS = 2
NSA_HEADS_PER_GROUP = NSA_HEADS // NSA_KV_GROUPS
NSA_BRANCHES = 3
NSA_CMP_LEN = 32
NSA_CMP_STRIDE = 16
NSA_SEL_LEN = 64
NSA_TOP_N = 16
NSA_WINDOW = 512
NSA_PHI_HIDDEN = 4 * HEAD_DIM
NSA_QBLOCK = 64
NSA_FORCE_SCORE = 1e6

CONV_CH = MIX_GROUP_WIDTH
CONV_WIDTH = 31

DIFF_HEADS = MIX_GROUP_WIDTH // (2 * HEAD_DIM)
DIFF_DH = HEAD_DIM

DIL_HEADS = MIX_GROUP_WIDTH // HEAD_DIM
DIL_PAIRS = ((128, 1), (512, 4), (2048, 16))

D_FF = 256 * ((8 * D_MODEL // 3 + 255) // 256)
FFN_CONV_WIDTH = 3

REL_BUCKETS = 32
REL_MAX_DIST = 2048
REL_COL_NSA = 0
REL_COL_DIFF = NSA_HEADS
REL_COL_DIL = NSA_HEADS + DIFF_HEADS
REL_HEADS = NSA_HEADS + DIFF_HEADS + DIL_HEADS

ATTN_QBLOCK = 128
NORM_EPS = 1e-6
NEG_INF = -1e30

EV_Q = NSA_HEADS * HEAD_DIM
EV_KV = NSA_BRANCHES * 2 * NSA_KV_GROUPS * HEAD_DIM
EV_GATE = NSA_HEADS * NSA_BRANCHES
EV_GLU = 2 * CONV_CH
EV_IN = EV_Q + EV_KV + EV_GATE + EV_GLU
OD_C = DIFF_HEADS * 2 * DIFF_DH
OD_D = DIL_HEADS * HEAD_DIM
OD_IN = 3 * OD_C + 3 * OD_D
MIX_OUT = 2 * MIX_GROUP_WIDTH
N_EVEN = (DEPTH + 1) // 2
N_ODD = DEPTH // 2

kernel_name = 'hybrid_nsa_conformer_diff_dilated_trunk'

def rmsnorm(x, g):
    xf = x.astype(jnp.float32)
    y = xf * lax.rsqrt(jnp.mean(xf * xf, axis=-1, keepdims=True) + NORM_EPS)
    return (y * g.astype(jnp.float32)).astype(x.dtype)

def layernorm(x, g, b):
    xf = x.astype(jnp.float32)
    mu = jnp.mean(xf, axis=-1, keepdims=True)
    var = jnp.mean(jnp.square(xf - mu), axis=-1, keepdims=True)
    y = (xf - mu) * lax.rsqrt(var + NORM_EPS) * g.astype(jnp.float32) + b.astype(jnp.float32)
    return y.astype(x.dtype)

def rel_bucket(dist):
    n = jnp.maximum(dist, 0)
    max_exact = REL_BUCKETS // 2
    nf = jnp.maximum(n, 1).astype(jnp.float32)
    large = max_exact + (jnp.log(nf / max_exact) / math.log(REL_MAX_DIST / max_exact)
                         * (REL_BUCKETS - max_exact)).astype(jnp.int32)
    large = jnp.minimum(large, REL_BUCKETS - 1)
    return jnp.where(n < max_exact, n, large)

def rel_bias(table, dist, col0, n_heads):
    return table[rel_bucket(dist), col0:col0 + n_heads].astype(jnp.float32)

def causal_dwconv(x, w, b):
    k = w.shape[0]
    y = lax.conv_general_dilated(x, w[:, None, :], window_strides=(1,), padding=[(k - 1, 0)],
                                 dimension_numbers=('NWC', 'WIO', 'NWC'),
                                 feature_group_count=x.shape[-1])
    return y + b

def nsa_attention(q, kv, gates, phi_pos, phi_w1, phi_w2, rel_table):
    B, S = q.shape[0], q.shape[1]
    G, HPG, DH, QB = NSA_KV_GROUPS, NSA_HEADS_PER_GROUP, HEAD_DIM, NSA_QBLOCK
    scale = DH ** -0.5
    f32 = jnp.float32
    n_cmp = (S - NSA_CMP_LEN) // NSA_CMP_STRIDE + 1
    cmp_idx = np.arange(n_cmp)[:, None] * NSA_CMP_STRIDE + np.arange(NSA_CMP_LEN)[None, :]
    cmp_end = jnp.asarray(cmp_idx[:, -1], jnp.int32)
    kv_c = kv[:, :, 0]
    blocks = kv_c[:, cmp_idx] + phi_pos.transpose(1, 0, 2)[:, :, None, :]
    flat = blocks.transpose(0, 1, 3, 4, 2, 5).reshape(B, n_cmp, 2, G, NSA_CMP_LEN * DH)
    hid = jax.nn.silu(jnp.einsum('bnegf,efh->bnegh', flat, phi_w1))
    cmp = jnp.einsum('bnegh,ehd->bnegd', hid, phi_w2)
    k_cmp, v_cmp = cmp[:, :, 0], cmp[:, :, 1]
    n_sel = S // NSA_SEL_LEN
    n_top = min(NSA_TOP_N, n_sel)
    overlap = (cmp_idx[:, :, None] // NSA_SEL_LEN == np.arange(n_sel)[None, None, :]).mean(axis=1).astype(np.float32)
    k_sel = kv[:, :, 1, 0].reshape(B, n_sel, NSA_SEL_LEN, G, DH).transpose(0, 3, 1, 2, 4)
    v_sel = kv[:, :, 1, 1].reshape(B, n_sel, NSA_SEL_LEN, G, DH).transpose(0, 3, 1, 2, 4)
    sel_tab = rel_table[:, REL_COL_NSA:REL_COL_NSA + NSA_HEADS].astype(f32).reshape(REL_BUCKETS, G, HPG)
    pad_w = ((0, 0), (NSA_WINDOW, 0), (0, 0), (0, 0))
    k_win = jnp.pad(kv[:, :, 2, 0], pad_w)
    v_win = jnp.pad(kv[:, :, 2, 1], pad_w)
    w_dist = NSA_WINDOW + np.arange(QB)[:, None] - np.arange(NSA_WINDOW + QB)[None, :]
    w_band = (w_dist >= 0) & (w_dist < NSA_WINDOW)
    w_bias = rel_bias(rel_table, jnp.asarray(w_dist), REL_COL_NSA, NSA_HEADS)
    w_bias = w_bias.transpose(2, 0, 1).reshape(G, HPG, QB, NSA_WINDOW + QB)

    n_qb = S // QB
    q_blocks = q.reshape(B, n_qb, QB, G, HPG, DH).transpose(1, 0, 2, 3, 4, 5)
    g_blocks = gates.reshape(B, n_qb, QB, G, HPG, 3).transpose(1, 0, 2, 3, 4, 5)
    starts = jnp.arange(n_qb, dtype=jnp.int32) * QB
    bi = jnp.arange(B)[:, None, None, None]
    gi = jnp.arange(G)[None, :, None, None]
    j_sel = jnp.arange(n_sel)

    def one_block(args):
        qb, gb, s0 = args
        t = s0 + jnp.arange(QB)
        s_c = jnp.einsum('bqghd,bngd->bghqn', qb, k_cmp).astype(f32) * scale
        valid_c = cmp_end[None, :] <= t[:, None]
        p_c = jax.nn.softmax(jnp.where(valid_c, s_c, NEG_INF), axis=-1) * jnp.any(valid_c, axis=-1)[:, None]
        o_c = jnp.einsum('bghqn,bngd->bqghd', p_c, v_cmp.astype(f32))
        imp = jnp.einsum('bghqn,nj->bgqj', p_c, overlap)
        cur = t // NSA_SEL_LEN
        forced = (j_sel[None, :] == 0) | (j_sel[None, :] == cur[:, None]) | (j_sel[None, :] == cur[:, None] - 1)
        imp = jnp.where(forced, NSA_FORCE_SCORE, imp)
        imp = jnp.where(j_sel[None, :] * NSA_SEL_LEN <= t[:, None], imp, NEG_INF)
        _, sel = lax.top_k(imp, n_top)
        kg = k_sel[bi, gi, sel]
        vg = v_sel[bi, gi, sel]
        pos = sel[..., None] * NSA_SEL_LEN + jnp.arange(NSA_SEL_LEN)
        dist = t[None, None, :, None, None] - pos
        bias_s = sel_tab[rel_bucket(dist), gi[..., None]].transpose(0, 1, 5, 2, 3, 4)
        s_s = jnp.einsum('bqghd,bgqnkd->bghqnk', qb, kg).astype(f32) * scale + bias_s
        s_s = jnp.where((dist >= 0)[:, :, None], s_s, NEG_INF)
        p_s = jax.nn.softmax(s_s.reshape(B, G, HPG, QB, n_top * NSA_SEL_LEN), axis=-1).reshape(s_s.shape)
        o_s = jnp.einsum('bghqnk,bgqnkd->bqghd', p_s, vg.astype(f32))
        kw = lax.dynamic_slice_in_dim(k_win, s0, NSA_WINDOW + QB, axis=1)
        vw = lax.dynamic_slice_in_dim(v_win, s0, NSA_WINDOW + QB, axis=1)
        kpos = s0 - NSA_WINDOW + jnp.arange(NSA_WINDOW + QB)
        valid_w = w_band & (kpos >= 0)[None, :]
        s_w = jnp.einsum('bqghd,bkgd->bghqk', qb, kw).astype(f32) * scale + w_bias
        p_w = jax.nn.softmax(jnp.where(valid_w, s_w, NEG_INF), axis=-1)
        o_w = jnp.einsum('bghqk,bkgd->bqghd', p_w, vw.astype(f32))
        o = gb[..., 0:1] * o_c + gb[..., 1:2] * o_s + gb[..., 2:3] * o_w
        return o.reshape(B, QB, G * HPG * DH)

    out = lax.map(one_block, (q_blocks, g_blocks, starts))
    return out.transpose(1, 0, 2, 3).reshape(B, S, NSA_HEADS * HEAD_DIM)

def nsa_conformer_mixer(h, w_in, w_out, phi_pos, phi_w1, phi_w2, dw_w, dw_b, ln_g, ln_b, rel_table):
    B, S, _ = h.shape
    proj = h @ w_in
    q, kv, gate_logits, glu = jnp.split(proj, [EV_Q, EV_Q + EV_KV, EV_Q + EV_KV + EV_GATE], axis=-1)
    q = q.reshape(B, S, NSA_KV_GROUPS, NSA_HEADS_PER_GROUP, HEAD_DIM)
    kv = kv.reshape(B, S, NSA_BRANCHES, 2, NSA_KV_GROUPS, HEAD_DIM)
    gates = jax.nn.sigmoid(gate_logits.astype(jnp.float32)).reshape(
        B, S, NSA_KV_GROUPS, NSA_HEADS_PER_GROUP, NSA_BRANCHES)
    o_a = nsa_attention(q, kv, gates, phi_pos, phi_w1, phi_w2, rel_table)
    a, g = jnp.split(glu, 2, axis=-1)
    u = causal_dwconv(a * jax.nn.sigmoid(g), dw_w, dw_b)
    u = jax.nn.silu(layernorm(u, ln_g, ln_b))
    return jnp.concatenate([o_a.astype(h.dtype), u], axis=-1) @ w_out

def diff_attention(q, k, v, lam_params, norm_g, lam_init, rel_table):
    B, S = q.shape[0], q.shape[1]
    f32 = jnp.float32
    QB = ATTN_QBLOCK
    lp = lam_params.astype(f32)
    lam = jnp.exp(jnp.sum(lp[0] * lp[1])) - jnp.exp(jnp.sum(lp[2] * lp[3])) + lam_init
    scale = DIFF_DH ** -0.5
    n_qb = S // QB
    q_blocks = q.reshape(B, n_qb, QB, DIFF_HEADS, 2, DIFF_DH).transpose(1, 0, 2, 3, 4, 5)
    starts = jnp.arange(n_qb, dtype=jnp.int32) * QB
    kpos = jnp.arange(S)
    v32 = v.astype(f32)

    def one_block(args):
        qb, s0 = args
        t = s0 + jnp.arange(QB)
        dist = t[:, None] - kpos[None, :]
        bias = rel_bias(rel_table, dist, REL_COL_DIFF, DIFF_HEADS).transpose(2, 0, 1)
        s = jnp.einsum('bqhmd,bkhmd->bhmqk', qb, k).astype(f32) * scale + bias[None, :, None]
        p = jax.nn.softmax(jnp.where(dist >= 0, s, NEG_INF), axis=-1)
        a = p[:, :, 0] - lam * p[:, :, 1]
        return jnp.einsum('bhqk,bkhe->bqhe', a, v32)

    o = lax.map(one_block, (q_blocks, starts))
    o = o.transpose(1, 0, 2, 3, 4).reshape(B, S, DIFF_HEADS, 2 * DIFF_DH)
    o = rmsnorm(o, norm_g) * (1.0 - lam_init)
    return o.reshape(B, S, DIFF_HEADS * 2 * DIFF_DH)

def dilated_attention(q, k, v, rel_table):
    B, S = q.shape[0], q.shape[1]
    f32 = jnp.float32
    HD, DH = DIL_HEADS, HEAD_DIM
    scale = DH ** -0.5
    outs, lses = [], []
    for window, dil in DIL_PAIRS:
        blk = window // dil
        span = blk * dil
        s_pad = -(-S // span) * span
        L = s_pad // dil
        nb = L // blk

        def to_blocks(a):
            a = jnp.pad(a, ((0, 0), (0, s_pad - S), (0, 0), (0, 0)))
            return a.reshape(B, L, dil, HD, DH).transpose(0, 2, 1, 3, 4).reshape(B, dil, nb, blk, HD, DH)

        def with_prev(a):
            prev = jnp.pad(a, ((0, 0), (0, 0), (1, 0), (0, 0), (0, 0), (0, 0)))[:, :, :-1]
            return jnp.concatenate([prev, a], axis=3)

        qb = to_blocks(q)
        kc = with_prev(to_blocks(k))
        vc = with_prev(to_blocks(v))
        ik = np.arange(2 * blk)
        sub_dist = blk + np.arange(blk)[:, None] - ik[None, :]
        band = (sub_dist >= 0) & (sub_dist <= blk)
        valid = band[None] & ~((np.arange(nb) == 0)[:, None, None] & (ik < blk)[None, None, :])
        bias = rel_bias(rel_table, jnp.asarray(sub_dist * dil), REL_COL_DIL, HD).transpose(2, 0, 1)
        s = jnp.einsum('brnqhd,brnkhd->brnhqk', qb, kc).astype(f32) * scale + bias
        s = jnp.where(valid[:, None], s, NEG_INF)
        lse = jax.nn.logsumexp(s, axis=-1, keepdims=True)
        o = jnp.einsum('brnhqk,brnkhd->brnqhd', jnp.exp(s - lse), vc.astype(f32))
        o = o.reshape(B, dil, L, HD, DH).transpose(0, 2, 1, 3, 4).reshape(B, s_pad, HD, DH)[:, :S]
        lse = lse[..., 0].transpose(0, 1, 2, 4, 3).reshape(B, dil, L, HD)
        lse = lse.transpose(0, 2, 1, 3).reshape(B, s_pad, HD)[:, :S]
        outs.append(o)
        lses.append(lse)
    w = jax.nn.softmax(jnp.stack(lses, axis=0), axis=0)
    o = jnp.sum(w[..., None] * jnp.stack(outs, axis=0), axis=0)
    return o.reshape(B, S, HD * DH)

def diff_dilated_mixer(h, w_in, w_out, lam_params, diff_g, lam_init, rel_table):
    B, S, _ = h.shape
    proj = h @ w_in
    cq, ck, cv, dq, dk, dv = jnp.split(
        proj, [OD_C, 2 * OD_C, 3 * OD_C, 3 * OD_C + OD_D, 3 * OD_C + 2 * OD_D], axis=-1)
    o_c = diff_attention(cq.reshape(B, S, DIFF_HEADS, 2, DIFF_DH),
                         ck.reshape(B, S, DIFF_HEADS, 2, DIFF_DH),
                         cv.reshape(B, S, DIFF_HEADS, 2 * DIFF_DH),
                         lam_params, diff_g, lam_init, rel_table)
    o_d = dilated_attention(dq.reshape(B, S, DIL_HEADS, HEAD_DIM),
                            dk.reshape(B, S, DIL_HEADS, HEAD_DIM),
                            dv.reshape(B, S, DIL_HEADS, HEAD_DIM), rel_table)
    return jnp.concatenate([o_c.astype(h.dtype), o_d.astype(h.dtype)], axis=-1) @ w_out

def conv_glu_ffn(h, w_gate, w_up, conv_w, conv_b, w_down):
    g = causal_dwconv(h @ w_gate, conv_w, conv_b)
    return (jax.nn.gelu(g, approximate=False) * (h @ w_up)) @ w_down

def setup_inputs(seed: int = 0) -> dict:
    key = jax.random.key(seed)
    ks = jax.random.split(key, 24)
    f32 = jnp.float32

    def nrm(k, shape, s):
        return jax.random.normal(k, shape, f32) * s

    NE, NO = N_EVEN, N_ODD
    return {
        'x': nrm(ks[0], (BATCH, SEQ, D_MODEL), 1.0),
        'rel_bias_table': nrm(ks[1], (REL_BUCKETS, REL_HEADS), 0.5),
        'mix_norm_g': 1.0 + nrm(ks[2], (DEPTH, D_MODEL), 0.02),
        'ffn_norm_g': 1.0 + nrm(ks[3], (DEPTH, D_MODEL), 0.02),
        'ffn_w_gate': nrm(ks[4], (DEPTH, D_MODEL, D_FF), D_MODEL ** -0.5),
        'ffn_w_up': nrm(ks[5], (DEPTH, D_MODEL, D_FF), D_MODEL ** -0.5),
        'ffn_conv_w': nrm(ks[6], (DEPTH, FFN_CONV_WIDTH, D_FF), FFN_CONV_WIDTH ** -0.5),
        'ffn_conv_b': nrm(ks[7], (DEPTH, D_FF), 0.01),
        'ffn_w_down': nrm(ks[8], (DEPTH, D_FF, D_MODEL), D_FF ** -0.5),
        'ev_w_in': nrm(ks[9], (NE, D_MODEL, EV_IN), D_MODEL ** -0.5),
        'ev_w_out': nrm(ks[10], (NE, MIX_OUT, D_MODEL), MIX_OUT ** -0.5),
        'nsa_phi_pos': nrm(ks[11], (NE, 2, NSA_CMP_LEN, HEAD_DIM), 0.1),
        'nsa_phi_w1': nrm(ks[12], (NE, 2, NSA_CMP_LEN * HEAD_DIM, NSA_PHI_HIDDEN), (NSA_CMP_LEN * HEAD_DIM) ** -0.5),
        'nsa_phi_w2': nrm(ks[13], (NE, 2, NSA_PHI_HIDDEN, HEAD_DIM), NSA_PHI_HIDDEN ** -0.5),
        'conv_dw_w': nrm(ks[14], (NE, CONV_WIDTH, CONV_CH), CONV_WIDTH ** -0.5),
        'conv_dw_b': nrm(ks[15], (NE, CONV_CH), 0.01),
        'conv_ln_g': 1.0 + nrm(ks[16], (NE, CONV_CH), 0.02),
        'conv_ln_b': nrm(ks[17], (NE, CONV_CH), 0.01),
        'od_w_in': nrm(ks[18], (NO, D_MODEL, OD_IN), D_MODEL ** -0.5),
        'od_w_out': nrm(ks[19], (NO, MIX_OUT, D_MODEL), MIX_OUT ** -0.5),
        'diff_lambda': nrm(ks[20], (NO, 4, DIFF_DH), 0.1),
        'diff_norm_g': 1.0 + nrm(ks[21], (NO, 2 * DIFF_DH), 0.02),
        'final_norm_g': 1.0 + nrm(ks[22], (D_MODEL,), 0.02),
    }

def reference(x, rel_bias_table, mix_norm_g, ffn_norm_g, ffn_w_gate, ffn_w_up, ffn_conv_w, ffn_conv_b,
              ffn_w_down, ev_w_in, ev_w_out, nsa_phi_pos, nsa_phi_w1, nsa_phi_w2, conv_dw_w, conv_dw_b,
              conv_ln_g, conv_ln_b, od_w_in, od_w_out, diff_lambda, diff_norm_g, final_norm_g):
    for layer in range(DEPTH):
        h = rmsnorm(x, mix_norm_g[layer])
        if layer % 2 == 0:
            e = layer // 2
            x = x + nsa_conformer_mixer(h, ev_w_in[e], ev_w_out[e], nsa_phi_pos[e], nsa_phi_w1[e],
                                        nsa_phi_w2[e], conv_dw_w[e], conv_dw_b[e], conv_ln_g[e],
                                        conv_ln_b[e], rel_bias_table)
        else:
            o = layer // 2
            lam_init = 0.8 - 0.6 * math.exp(-0.3 * layer)
            x = x + diff_dilated_mixer(h, od_w_in[o], od_w_out[o], diff_lambda[o], diff_norm_g[o],
                                       lam_init, rel_bias_table)
        h = rmsnorm(x, ffn_norm_g[layer])
        x = x + conv_glu_ffn(h, ffn_w_gate[layer], ffn_w_up[layer], ffn_conv_w[layer],
                             ffn_conv_b[layer], ffn_w_down[layer])
    return rmsnorm(x, final_norm_g)


_drawn_inputs = setup_inputs


def setup_inputs(seed=0):
    import zlib

    import numpy as np

    out = dict(_drawn_inputs(seed))
    spreads = {}
    factors = {'mix_norm_g': 3.052,
     'ffn_norm_g': 2.741,
     'ffn_conv_b': 7.547,
     'conv_dw_b': 4.064,
     'conv_ln_g': 4.18,
     'conv_ln_b': 8.0,
     'diff_norm_g': 7.49,
     'final_norm_g': 2.832}
    for name, (base, spread) in spreads.items():
        noise = np.random.default_rng([zlib.crc32(name.encode()), seed]).standard_normal(out[name].shape)
        drawn = base * np.exp(spread * noise) if base else spread * noise
        out[name] = jnp.asarray(drawn.astype(out[name].dtype))
    for name, factor in factors.items():
        out[name] = (out[name] * factor).astype(out[name].dtype)
    return out
```

```python
import math
from contextlib import ExitStack

import concourse.bass as bass
from concourse import mybir

F32 = mybir.dt.float32
F32R = mybir.dt.float32r
ALU = mybir.AluOpType
ACT = mybir.ActivationFunctionType
AXX = mybir.AxisListType.X

P = 128
D = 1024
S = 512
KC = D // P
QT = S // P
HD = 64
F = 2816
FC = F // P
EPS = 1e-6
NEG = -1e30
EV_IN = 2328
CONV_W = 31
PAD = CONV_W - 1
NCMP = 31
NPAIR = 16
BUCKETS = 32
FROW = 640
LAM_INIT = 0.8 - 0.6 * math.exp(-0.3)
DOWN = (8, 8, 6)

U_IN0 = 0
N_IN0 = 19
U_OUT0 = U_IN0 + N_IN0
U_GU = [U_OUT0 + KC, 0]
U_DN = [U_GU[0] + 2 * FC, 0]
U_IN1 = U_DN[0] + 3 * KC
N_IN1 = 24
U_OUT1 = U_IN1 + N_IN1
U_GU[1] = U_OUT1 + KC
U_DN[1] = U_GU[1] + 2 * FC
U_END = U_DN[1] + 3 * KC
O_IN0 = 0
O_OUT0 = O_IN0 + N_IN0
O_GU = [O_OUT0 + KC, 0]
O_DN = [O_GU[0] + 2 * FC, 0]
O_IN1 = O_DN[0] + KC
O_OUT1 = O_IN1 + N_IN1
O_GU[1] = O_OUT1 + KC
O_DN[1] = O_GU[1] + 2 * FC
RAW = 4
SPL = 2
NACC = 4

PR_MIX, PR_FFN, PR_FIN = 0, 16, 32
PR_DWB, PR_LNG, PR_LNB, PR_POS = 40, 44, 48, 52
PR_A = 84
PR_DWW = PR_A
PR_FF = [PR_DWW + CONV_W * 4, PR_DWW + CONV_W * 4 + 4 * FC]
PR_N = PR_FF[1] + 4 * FC

N_MEMSETS = 6
JOBS = 64
PER = JOBS // QT


def in0_units():
    kv = 512
    glu = 512 + 768 + 24
    units = []
    for c in range(4):
        units += [("g", c, glu + 512 + c * P, P), ("a", c, glu + c * P, P)]
    units += [("kc", 0, kv, P), ("kc", 1, kv + P, P)]
    units += [("q", c, c * HD, P) for c in range(4)]
    units += [("k", 0, kv + 256, P), ("k", 1, kv + 512, P)]
    units += [("v", 0, kv + 384, P), ("v", 1, kv + 640, P), ("gate", 0, kv + 768, 24)]
    return units


def in1_units():
    kinds = ["q"] * 4 + ["k"] * 4 + ["cv"] * 4 + ["q"] * 4 + ["k"] * 4 + ["dv"] * 4
    index = list(range(4)) * 3 + list(range(4, 8)) * 2 + list(range(4))
    return [(k, n, u * P, P) for u, (k, n) in enumerate(zip(kinds, index))]


def build(nc, x, rel_bias_table, mix_norm_g, ffn_norm_g, ffn_w_gate, ffn_w_up, ffn_conv_w, ffn_conv_b,
          ffn_w_down, ev_w_in, ev_w_out, nsa_phi_pos, nsa_phi_w1, nsa_phi_w2, conv_dw_w, conv_dw_b,
          conv_ln_g, conv_ln_b, od_w_in, od_w_out, diff_lambda, diff_norm_g, final_norm_g,
          c_onehot, c_ident, c_cmpmask, bias_rows, out):
    ctx = ExitStack()
    with ctx:
        top = [16896]

        def at(name, shape, dt=F32, offset=None):
            size = 4
            for n in shape[1:]:
                size *= n
            size = -(-size // 32) * 32
            where = top[0] if offset is None else offset
            if offset is None:
                top[0] += size
            t = nc.alloc_sbuf_tensor_at(name, shape, dt, offset=where)
            return t, where + size

        def sb(name, shape, dt=F32):
            return at(name, shape, dt)[0]

        def sem(name):
            return ctx.enter_context(nc.semaphore(name))

        XT = sb("XT", [P, KC, S])
        Hh = sb("Hh", [P, KC, S], F32R)
        Hl = sb("Hl", [P, KC, S], F32R)
        raw = sb("raw", [P, RAW, 8, P])
        Wh = sb("Wh", [P, SPL, 8, P], F32R)
        Wl = sb("Wl", [P, SPL, 8, P], F32R)
        ident = sb("ident", [P, P])
        ones = sb("ones", [P, P])
        prm = sb("prm", [P, PR_N])
        kcT = sb("kcT", [P, 32])
        vbd = sb("vbd", [P, 2, 4 * HD])
        cmask = sb("cmask", [P, QT, 33])
        gate = sb("gate", [P, QT, 24])
        Ls = sb("Ls", [P, 2, 24])
        Rs = sb("Rs", [P, 24])
        Cs = sb("Cs", [P, 24])
        nmx = sb("nmx", [P, 4])
        cmx = sb("cmx", [P, 8])
        Sm = sb("Sm", [P, 8, 32])
        Pc = sb("Pc", [P, 8, 32])
        PcT = sb("PcT", [P, 2, P])
        lamb = sb("lamb", [P, 8])
        eps = sb("eps", [P, 8])
        lamp = sb("lamp", [P, 4, HD])
        dng = sb("dng", [P, 2 * HD])
        tab = sb("tab", [BUCKETS + 1, 20])
        w2s = sb("w2s", [P, 2, 2, HD])
        hid = sb("hid", [P, 2, 2, 2 * NCMP])

        g0 = top[0]
        sq, e = at("sq", [P, 2, S], F32, g0)
        hf, e = at("hf", [P, 2, S], F32, e)
        rs, e = at("rs", [P, S], F32, e)
        yb, e = at("yb", [P, 2, S], F32, e)
        ab, e_work = at("ab", [P, 2, S], F32, e)
        S2, e = at("S2", [P, 2, S], F32, g0)
        Pb, e = at("Pb", [P, 3, S], F32, e)
        PTs, e = at("PTs", [P, 2, S], F32, e)
        KK, e = at("KK", [P, 2, 2, S], F32, g0)
        FT, e = at("FT", [P, 2, NPAIR, 2 * NCMP], F32, e)
        assert e <= e_work
        a0 = e_work
        Ah, e = at("Ah", [P, FC, S], F32R, a0)
        Al, e_top = at("Al", [P, FC, S], F32R, e)
        assert e_top <= 229344
        T0, e = at("T0", [P, 8, S], F32, a0)
        xin, _ = at("xin", [P, QT, D], F32, e)
        Q0, e = at("Q0", [P, 4, S], F32, e)
        K0, e = at("K0", [P, 2, S], F32, e)
        V0, e = at("V0", [P, 2, QT, P], F32, e)
        Uc, e = at("Uc", [P, 4, PAD + S + 2], F32, e)
        CA, e = at("CA", [P, 4, S], F32, e)
        tm, e = at("tm", [P, 3, S], F32, e)
        onehot, _ = at("onehot", [BUCKETS + 1, 2, FROW], F32, e)
        pst, _ = at("pst", [P, 4, P], F32, _)
        brow, _ = at("brow", [12, 2, FROW], F32, _)
        assert _ <= e_top
        phw, e = at("phw", [P, 2, NPAIR, 2 * P], F32, e)
        assert e <= e_top
        T1, e = at("T1", [P, 12, S], F32, a0)
        Q1, e = at("Q1", [P, 8, S], F32, e)
        K1, e = at("K1", [P, 8, S], F32, e)
        Vc, e = at("Vc", [P, QT, S], F32, e)
        Vd, e = at("Vd", [P, QT, S], F32, e)
        tn, e = at("tn", [P, 3, S], F32, e)
        assert e <= e_top
        xout, _ = at("xout", [P, KC, QT, P], F32, a0)

        bank = ctx.enter_context(nc.psum_tensor("bank", [P, 8, S], F32))

        raw_loaded = [sem(f"raw_loaded{n}") for n in range(RAW)]
        weights_hi = sem("weights_hi")
        weights_lo = sem("weights_lo")
        unit_done = sem("unit_done")
        tile_read = [sem(f"tile_read{n}") for n in range(NACC)]
        x_loaded = sem("x_loaded")
        consts_loaded = sem("consts_loaded")
        params_loaded = sem("params_loaded")
        small_loaded = sem("small_loaded")
        phi_loaded = sem("phi_loaded")
        rows_stored = sem("rows_stored")
        strips_loaded = sem("strips_loaded")
        memsets = sem("memsets")
        turned = sem("turned")
        param_copied = sem("param_copied")
        row_made = sem("row_made")
        row_copied = sem("row_copied")
        xt_ready = sem("xt_ready")
        sq_ready = sem("sq_ready")
        sq_used = sem("sq_used")
        rms_ready = sem("rms_ready")
        hf_ready = sem("hf_ready")
        hh_ready = sem("hh_ready")
        h_ready = sem("h_ready")
        dstep = sem("dstep")
        ft_ready = sem("ft_ready")
        hid_made = sem("hid_made")
        hid_ready = sem("hid_ready")
        cmp_made = sem("cmp_made")
        cmp_ready = sem("cmp_ready")
        conv_done = sem("conv_done")
        ln_mean = sem("ln_mean")
        ln_centered = sem("ln_centered")
        ln_sq = sem("ln_sq")
        ln_var = sem("ln_var")
        ln_std = sem("ln_std")
        ln_scaled = sem("ln_scaled")
        u_ready = sem("u_ready")
        cc_hi = sem("cc_hi")
        cc_ready = sem("cc_ready")
        qk_done = sem("qk_done")
        scores_read = sem("scores_read")
        probs_ready = sem("probs_ready")
        probs_turned = sem("probs_turned")
        pt_copied = [sem("pt_copied_dve"), sem("pt_copied_act")]
        pv_done = sem("pv_done")
        combined = sem("combined")
        ct_turned = sem("ct_turned")
        ct_hi = sem("ct_hi")
        sc_made = sem("sc_made")
        sc_shifted = sem("sc_shifted")
        pc_ready = sem("pc_ready")
        pc_turned = sem("pc_turned")
        pc_copied = sem("pc_copied")
        oc_made = sem("oc_made")
        o_squared = sem("o_squared")
        o_rms = sem("o_rms")
        lam_dots = sem("lam_dots")
        lam_exps = sem("lam_exps")
        y_base = sem("y_base")
        y_gelu = sem("y_gelu")
        ah_ready = sem("ah_ready")
        a_ready = sem("a_ready")
        fin_ready = sem("fin_ready")
        fin_turned = sem("fin_turned")
        fin_copied = sem("fin_copied")
        out_stored = sem("out_stored")

        w_in0 = ev_w_in[0].rearrange("(k p) n -> p k n", p=P)
        w_out = [ev_w_out[0].rearrange("(k p) n -> p k n", p=P), od_w_out[0].rearrange("(k p) n -> p k n", p=P)]
        w_in1 = od_w_in[0].rearrange("(k p) n -> p k n", p=P)
        w_gate = [ffn_w_gate[n].rearrange("(k p) n -> p k n", p=P) for n in range(2)]
        w_up = [ffn_w_up[n].rearrange("(k p) n -> p k n", p=P) for n in range(2)]
        w_down = [ffn_w_down[n].rearrange("(k p) n -> p k n", p=P) for n in range(2)]
        UN0, UN1 = in0_units(), in1_units()

        def spread(ap, *dims):
            return bass.AP(ap.tensor, ap.offset, [ap.ap[0], *[list(d) for d in dims]])

        def strip(t, head, i):
            v = t[:, head, :]
            return bass.AP(v.tensor, v.offset + P - 1 + P * i, [v.ap[0], [-1, P * (i + 1)]])

        def job(layer, j):
            i, r = divmod(j, PER)
            ks = slice(0, P * (i + 1))
            qs = slice(P * i, P * (i + 1))
            if layer == 0:
                c, g, br = r // 4, (r // 2) % 2, r % 2
                h = 4 * g + c
                half = slice(HD * g, HD * g + HD)
                return (Q0[half, c, qs], K0[half, br, ks], strip(T0, h, i),
                        [V0[:, br, t, half] for t in range(i + 1)], bank[:, br, HD * h:HD * h + HD],
                        Ls[:, i % 2, 8 + 8 * br + h:9 + 8 * br + h])
            if r < 8:
                h, m = divmod(r, 2)
                half = slice(HD * m, HD * m + HD)
                return (Q1[half, h, qs], K1[half, h, ks], strip(T1, h, i),
                        [Vc[:, t, P * h:P * h + P] for t in range(i + 1)], bank[:, m, P * h:P * h + P],
                        Ls[:, i % 2, 4 * m + h:4 * m + h + 1])
            h = r - 8
            half = slice(HD * (h % 2), HD * (h % 2) + HD)
            return (Q1[half, 4 + h // 2, qs], K1[half, 4 + h // 2, ks], strip(T1, 4 + h, i),
                    [Vd[:, t, HD * h:HD * h + HD] for t in range(i + 1)], bank[:, 2, HD * h:HD * h + HD],
                    Ls[:, i % 2, 8 + h:9 + h])

        CT = [{PER * i + 21: [(i, 0)] for i in range(QT)},
              {**{PER * i + 21: [(i, 0)] for i in range(QT)}, **{PER * i + 22: [(i, 1)] for i in range(QT)}}]
        STEPS = PER * (QT - 1) + 23
        use = {}
        for layer in range(2):
            for s in range(STEPS):
                if s < JOBS:
                    use[layer, s] = len(use)
                for key in CT[layer].get(s, []):
                    use[layer, "ct", key] = len(use)
        CTN = {key: n for n, key in enumerate(k for k in use if k[1] == "ct")}
        STEP_CMP = {"scores": 0, "shift": 0, "exp": 1, "sum": 2, "turn": 3, "copy": 4, "values": 6}
        STEP_COMBINE = PER + 3

        block = ctx.enter_context(nc.Block())

        def wait_read(eng, o, it=0):
            for n, o0 in enumerate((O_OUT0, O_DN[0], O_OUT1, O_DN[1])):
                if o0 <= o < o0 + KC:
                    eng.wait_ge(xt_ready, KC * (n + 1) + o - o0 + 1)
                    return
            eng.wait_ge(tile_read[o % NACC], reads(o) + it)

        def reads(o):
            kept = [range(o0, o0 + KC) for o0 in (O_OUT0, O_DN[0], O_OUT1, O_DN[1])]
            return sum(not any(t in r for r in kept) for t in range(o % NACC, o + 1, NACC))

        def raw_count(u):
            n = 0
            for v in range(u % RAW, u + 1, RAW):
                n += 32 if v < N_IN0 and UN0[v][0] == "q" else 16
            return n

        def sq2(c):
            return tm[:, c % 2, :]

        def prm_ff(layer, it, q):
            return [prm[:, bass.ds(it * 2 + (PR_FF[layer] + FC * t + q), 1)] for t in range(4)]

        def one(t, it, q):
            return t[:, bass.ds(it * 2 + q, 1), :].rearrange("p a n -> p (a n)")

        @block.sync
        def _(sp):
            def load(u, src, nk=8, w=P, it=0, stride=0):
                if u >= RAW:
                    sp.wait_ge(weights_lo, u - RAW + 1 + it * stride)
                sp.dma_start(raw[:, u % RAW, 0:nk, 0:w], src).then_inc(raw_loaded[u % RAW], 16)

            def load_in0(u):
                kind, n, col, w = UN0[u - U_IN0]
                if kind != "q":
                    load(u, w_in0[:, :, col:col + w], w=w)
                    return
                if u >= RAW:
                    sp.wait_ge(weights_lo, u - RAW + 1)
                for g in range(2):
                    sp.dma_start(raw[:, u % RAW, :, HD * g:HD * g + HD],
                                 w_in0[:, :, col + 4 * HD * g:col + 4 * HD * g + HD]).then_inc(
                        raw_loaded[u % RAW], 16)

            sp.dma_start(ident[:], c_ident).then_inc(consts_loaded, 16)
            for t in range(QT):
                sp.dma_start(xin[:, t, :], x[0, t * P:(t + 1) * P, :]).then_inc(x_loaded, 16)
            rows = [(0, PR_MIX, mix_norm_g.rearrange("l (k p) -> (l k) p", p=P)),
                    (0, PR_FFN, ffn_norm_g.rearrange("l (k p) -> (l k) p", p=P)),
                    (0, PR_FIN, final_norm_g.rearrange("(k p) -> k p", p=P)),
                    (0, PR_DWB, conv_dw_b[0].rearrange("(k p) -> k p", p=P)),
                    (0, PR_LNG, conv_ln_g[0].rearrange("(k p) -> k p", p=P)),
                    (0, PR_LNB, conv_ln_b[0].rearrange("(k p) -> k p", p=P)),
                    (0, PR_POS, nsa_phi_pos[0].rearrange("v (k l) d -> (v k) (l d)", l=2)),
                    (1, 0, conv_dw_w[0].rearrange("t (k p) -> (t k) p", p=P)),
                    (2, 0, ffn_conv_w[0].rearrange("t (k p) -> (t k) p", p=P)),
                    (2, 3 * FC, ffn_conv_b[0].rearrange("(k p) -> k p", p=P)),
                    (3, 0, ffn_conv_w[1].rearrange("t (k p) -> (t k) p", p=P)),
                    (3, 3 * FC, ffn_conv_b[1].rearrange("(k p) -> k p", p=P))]
            for b, r, src in rows:
                sp.dma_start(pst[r:r + src.shape[0], b, :], src).then_inc(params_loaded, 16)
            for u in range(2):
                load_in0(u)
            sp.dma_start(tab[0:BUCKETS, :], rel_bias_table).then_inc(consts_loaded, 16)
            sp.dma_start(onehot[:], c_onehot).then_inc(consts_loaded, 16)
            for u in range(2, RAW):
                load_in0(u)
            sp.dma_start(cmask[:], c_cmpmask).then_inc(small_loaded, 16)
            sp.dma_start(w2s[:], nsa_phi_w2[0].rearrange("v (h p) d -> p v h d", p=P)).then_inc(small_loaded, 16)
            sp.dma_start(lamp[:], bass.AP(diff_lambda.tensor, 0, [[0, P], [HD, 4], [1, HD]])).then_inc(small_loaded, 16)
            sp.dma_start(dng[:], bass.AP(diff_norm_g.tensor, 0, [[0, P], [1, 2 * HD]])).then_inc(small_loaded, 16)
            sp.wait_ge(row_copied, 2)
            sp.dma_start(bias_rows[0:12, :], brow[0:12, 0, :]).then_inc(rows_stored, 16)
            sp.dma_start(bias_rows[12:20, :], brow[0:8, 1, :]).then_inc(rows_stored, 16)
            sp.wait_ge(rows_stored, 32)

            def strips(dst, head, n):
                src = bass.AP(bias_rows.tensor, head * FROW, [[1, P], [FROW, n], [1, S]])
                sp.dma_start(dst[:, 0:n, :], src).then_inc(strips_loaded, 16)

            strips(T0, 0, 8)
            sp.wait_ge(param_copied, 4)
            for kv in range(2):
                sp.dma_start(phw[:, kv], nsa_phi_w1[0, kv].rearrange("(k p) h -> p k h", p=P)).then_inc(phi_loaded, 16)
            for u in range(RAW, N_IN0):
                load_in0(u)
            for n in range(KC):
                load(U_OUT0 + n, w_out[0][:, :, n * P:(n + 1) * P])

            def load_ffn(layer):
                with sp.Fori(0, FC // 2) as it:
                    for j in range(4):
                        w = (w_gate, w_up)[j % 2][layer]
                        load(U_GU[layer] + j, w[:, :, bass.ds(it * (2 * P) + (j // 2) * P, P)], it=it, stride=4)
                for n in range(KC):
                    k = 0
                    for r in range(3):
                        load(U_DN[layer] + 3 * n + r, w_down[layer][:, k:k + DOWN[r], n * P:(n + 1) * P], nk=DOWN[r])
                        k += DOWN[r]

            load_ffn(0)
            for u, (kind, n, col, w) in enumerate(UN1):
                if u == 6:
                    sp.wait_ge(unit_done, U_IN1)
                    strips(T1, 8, 12)
                load(U_IN1 + u, w_in1[:, :, col:col + w])
            for n in range(KC):
                load(U_OUT1 + n, w_out[1][:, :, n * P:(n + 1) * P])
            load_ffn(1)
            for k in range(KC):
                sp.wait_ge(fin_copied, k + 1)
                sp.dma_start(out[0, :, k * P:(k + 1) * P].rearrange("(t p) c -> p t c", p=P), xout[:, k]).then_inc(out_stored, 16)
            sp.wait_ge(out_stored, 16 * KC)

        @block.gpsimd
        def _(pool):
            fills = [(ones[:], 1.0), (tab[BUCKETS:BUCKETS + 1, :], 1.0), (kcT[:], 0.0), (vbd[:], 0.0),
                     (Uc[:, :, 0:PAD], 0.0), (eps[:], EPS)]
            assert len(fills) == N_MEMSETS
            for n, (dst, value) in enumerate(fills):
                if n:
                    pool.wait_ge(memsets, n)
                nc.gpsimd.memset(dst, value).then_inc(memsets, 1)
            pool.wait_ge(memsets, N_MEMSETS)

            def rest(u, nk=8, w=P, it=0, stride=0):
                pool.wait_ge(weights_hi, u + 1 + it * stride)
                hi = Wh[:, u % SPL, 0:nk, 0:w]
                nc.gpsimd.tensor_tensor(Wl[:, u % SPL, 0:nk, 0:w], raw[:, u % RAW, 0:nk, 0:w], hi.bitcast(F32),
                                        ALU.subtract).then_inc(weights_lo, 1)

            def rest_ffn(layer):
                with pool.Fori(0, FC // 2) as it:
                    for j in range(4):
                        rest(U_GU[layer] + j, it=it, stride=4)
                for n in range(3 * KC):
                    rest(U_DN[layer] + n, nk=DOWN[n % 3])

            for u in range(N_IN0):
                rest(u, w=UN0[u][3])
            for n in range(KC):
                rest(U_OUT0 + n)
            rest_ffn(0)
            for n in range(N_IN1 + KC):
                rest(U_IN1 + n)
            rest_ffn(1)

        @block.tensor
        def _(pe):
            pe.wait_ge(consts_loaded, 16)
            pe.wait_ge(x_loaded, 64)
            for k in range(KC):
                if k >= 4:
                    pe.wait_ge(xt_ready, k - 3)
                for t in range(QT):
                    mm = nc.tensor.transpose(bank[:, 4 + k % 4, t * P:(t + 1) * P], xin[:, t, k * P:(k + 1) * P], ident[:])
                mm.then_inc(turned, 1)
            pe.wait_ge(params_loaded, 16 * 12)
            for b, n in enumerate((PR_A, 4 * CONV_W, 4 * FC, 4 * FC)):
                nc.tensor.transpose(bank[:, b, 0:n], pst[0:n, b, :], ident[0:n, 0:n]).then_inc(turned, 1)

            def stats(norm, k):
                pe.wait_ge(sq_ready, norm * KC + k + 1)
                nc.tensor.matmul(bank[:, 7, :], ones[:], sq[:, k % 2, :], start=k == 0, stop=k == KC - 1).then_inc(sq_used, 1)

            pe.wait_ge(memsets, N_MEMSETS)
            pe.wait_ge(xt_ready, KC)
            for k in range(KC):
                stats(0, k)
            pe.wait_ge(consts_loaded, 48)
            for v, (c0, c1) in enumerate(((0, 12), (12, 20))):
                if v == 1:
                    pe.wait_ge(row_copied, 1)
                nc.tensor.matmul(bank[0:c1 - c0, 4, :], tab[:, c0:c1], onehot[:, v, 0:S], start=True, stop=True)
                nc.tensor.matmul(bank[0:c1 - c0, 5, 0:FROW - S], tab[:, c0:c1], onehot[:, v, S:FROW], start=True,
                                 stop=True).then_inc(row_made, 1)

            def begin(o, it=0):
                if o >= NACC:
                    wait_read(pe, o - NACC, it)
                return bank[:, o % NACC, :]

            def product(dst, u, nk, oh, ol, k0=0, first=True, last=True, hwait=None, it=0, stride=0):
                pe.wait_ge(weights_lo, u + 1 + it * stride)
                s = u % SPL
                for k in range(nk):
                    if hwait is not None:
                        pe.wait_ge(h_ready, hwait + k + 1)
                    a = first and k == 0
                    z = last and k == nk - 1
                    nc.tensor.matmul(dst, Wh[:, s, k, :], oh[:, k0 + k, :], start=a, stop=False)
                    nc.tensor.matmul(dst, Wh[:, s, k, :], ol[:, k0 + k, :], start=False, stop=False)
                    mm = nc.tensor.matmul(dst, Wl[:, s, k, :], oh[:, k0 + k, :], start=False, stop=z)
                mm.then_inc(unit_done, 1)

            def product_by_token(dst, u, w):
                pe.wait_ge(weights_lo, u + 1)
                s = u % SPL
                for t in range(QT):
                    for k in range(KC):
                        d = dst[:, t * w:(t + 1) * w]
                        ts = slice(t * P, (t + 1) * P)
                        nc.tensor.matmul(d, Hh[:, k, ts], Wh[:, s, k, 0:w], start=k == 0, stop=False)
                        nc.tensor.matmul(d, Hl[:, k, ts], Wh[:, s, k, 0:w], start=False, stop=False)
                        mm = nc.tensor.matmul(d, Hh[:, k, ts], Wl[:, s, k, 0:w], start=False, stop=k == KC - 1)
                mm.then_inc(unit_done, 1)

            pe.wait_ge(param_copied, 4)
            for n, (kind, idx, col, w) in enumerate(UN0):
                dst = begin(O_IN0 + n)
                if kind in ("v", "gate"):
                    product_by_token(dst, U_IN0 + n, w)
                else:
                    product(dst, U_IN0 + n, KC, Hh, Hl, hwait=0 if n == 0 else None)

            pe.wait_ge(phi_loaded, 32)
            for kv in range(2):
                pe.wait_ge(ft_ready, kv + 1)
                for hh in range(2):
                    for l in range(NPAIR):
                        mm = nc.tensor.matmul(bank[:, 5 + kv, hh * P:hh * P + 2 * NCMP],
                                              phw[:, kv, l, hh * P:(hh + 1) * P], FT[:, kv, l, :],
                                              start=l == 0, stop=l == NPAIR - 1)
                mm.then_inc(hid_made, 1)
            for c in range(4):
                pe.wait_ge(conv_done, c + 1)
                mm = nc.tensor.matmul(bank[:, 7, :], ones[:], CA[:, c, :], start=c == 0, stop=c == 3)
            mm.then_inc(ln_mean, 1)
            pe.wait_ge(hid_ready, 2)
            for g in range(2):
                for hh in range(2):
                    nc.tensor.matmul(bank[HD * g:HD * g + HD, 5, 0:NCMP], w2s[:, 0, hh, :],
                                     hid[:, 0, hh, NCMP * g:NCMP * g + NCMP], start=hh == 0, stop=hh == 1)
            for g in range(2):
                for q in range(4):
                    for hh in range(2):
                        mm = nc.tensor.matmul(bank[32 * q:32 * q + NCMP, 6, 256 * g + HD * q:256 * g + HD * q + HD],
                                              hid[:, 1, hh, NCMP * g:NCMP * g + NCMP], w2s[:, 1, hh, :],
                                              start=hh == 0, stop=hh == 1)
            mm.then_inc(cmp_made, 1)
            for c in range(4):
                pe.wait_ge(ln_sq, c + 1)
                nc.tensor.matmul(bank[:, 4, :], ones[:], sq2(c), start=c == 0, stop=c == 3).then_inc(ln_var, 1)

            def attention(layer):
                J = JOBS * layer
                base = QT * layer
                Tm = (tm, tn)[layer]
                for s in range(STEPS):
                    i, r = divmod(s, PER)
                    if layer == 0 and r == STEP_CMP["scores"] and i < QT:
                        for g in range(2):
                            for c in range(4):
                                mm = nc.tensor.matmul(bank[:, 2 + g, 32 * c:32 * c + 32],
                                                      Q0[HD * g:HD * g + HD, c, P * i:P * (i + 1)],
                                                      kcT[HD * g:HD * g + HD, :], start=True, stop=True)
                        mm.then_inc(sc_made, 1)
                    if s < JOBS:
                        q, k, _, _, _, _ = job(layer, s)
                        n = use[layer, s]
                        if n >= 2:
                            pe.wait_ge(scores_read, n - 1)
                        nc.tensor.matmul(bank[:, 4 + n % 2, 0:k.shape[1]], q, k, start=True, stop=True).then_inc(qk_done, 1)
                    for key in CT[layer].get(s, []):
                        n = use[layer, "ct", key]
                        pe.wait_ge(combined, 1 + base + key[0])
                        pe.wait_ge(scores_read, n - 1)
                        for c in range(4):
                            mm = nc.tensor.transpose(bank[:, 4 + n % 2, c * P:(c + 1) * P],
                                                     Tm[:, ct_tile[key[1]], c * P:(c + 1) * P], ident[:])
                        mm.then_inc(ct_turned, 1)
                    j = s - 2
                    if 0 <= j < JOBS:
                        pe.wait_ge(probs_ready, J + j + 1)
                        if J + j >= 2:
                            pe.wait_ge(pt_copied[j % 2], (J + j) // 2)
                        for t in range(j // PER + 1):
                            mm = nc.tensor.transpose(bank[:, 6 + j % 2, t * P:(t + 1) * P], Pb[:, j % 3, t * P:(t + 1) * P],
                                                     ident[:])
                        mm.then_inc(probs_turned, 1)
                    j = s - 3
                    if 0 <= j < JOBS:
                        if j % PER == 0 and j > 0:
                            pe.wait_ge(combined, base + j // PER)
                        pe.wait_ge(pt_copied[j % 2], (J + j) // 2 + 1)
                        _, _, _, v, o, _ = job(layer, j)
                        for t, vt in enumerate(v):
                            mm = nc.tensor.matmul(o, PTs[:, j % 2, t * P:(t + 1) * P], vt, start=t == 0, stop=t == len(v) - 1)
                        mm.then_inc(pv_done, 1)
                    if layer == 0 and r == STEP_CMP["turn"] and i < QT:
                        pe.wait_ge(pc_ready, i + 1)
                        for g in range(2):
                            mm = nc.tensor.transpose(bank[:, 2 + g, P:2 * P], Pc[:, 4 * g:4 * g + 4, :].rearrange("p h n -> p (h n)"),
                                                     ident[:])
                        mm.then_inc(pc_turned, 1)
                    if layer == 0 and r == STEP_CMP["values"] and i < QT:
                        pe.wait_ge(pc_copied, i + 1)
                        if i > 0:
                            pe.wait_ge(combined, i)
                        for g in range(2):
                            mm = nc.tensor.matmul(bank[:, 2 + g, 2 * P:4 * P], PcT[:, g, :], vbd[:, g, :], start=True, stop=True)
                        mm.then_inc(oc_made, 1)

            ct_tile = [0, 2]

            def project_out(layer, u0, o0, norm):
                for n in range(KC):
                    dst = begin(o0 + n)
                    product(dst, u0 + n, KC, Hh, Hl)
                    if n > 0:
                        stats(norm, n - 1)
                stats(norm, KC - 1)

            def ffn(layer):
                norm = 2 * layer + 1
                pe.wait_ge(h_ready, KC * (norm + 1))
                with pe.Fori(0, FC // 2) as it:
                    for j in range(4):
                        dst = bank[:, (O_GU[layer] + j) % NACC, :]
                        pe.wait_ge(tile_read[(O_GU[layer] + j) % NACC], reads(O_GU[layer] + j) - 1 + it)
                        product(dst, U_GU[layer] + j, KC, Hh, Hl, it=it, stride=4)
                pe.wait_ge(a_ready, FC * (layer + 1))
                for n in range(KC):
                    dst = begin(O_DN[layer] + n)
                    k = 0
                    for r in range(3):
                        product(dst, U_DN[layer] + 3 * n + r, DOWN[r], Ah, Al, k0=k, first=r == 0, last=r == 2)
                        k += DOWN[r]
                    if n > 0:
                        stats(norm + 1, n - 1)
                stats(norm + 1, KC - 1)

            pe.wait_ge(cmp_ready, 1)
            pe.wait_ge(ln_std, 1)
            for o in range(O_IN0 + N_IN0 - NACC, O_IN0 + N_IN0):
                wait_read(pe, o)
            attention(0)
            pe.wait_ge(cc_ready, 4)
            pe.wait_ge(scores_read, use[0, "ct", (QT - 1, 0)] + 1)
            project_out(0, U_OUT0, O_OUT0, 1)
            ffn(0)
            for n, (kind, idx, col, w) in enumerate(UN1):
                dst = begin(O_IN1 + n)
                if kind in ("cv", "dv"):
                    product_by_token(dst, U_IN1 + n, w)
                else:
                    product(dst, U_IN1 + n, KC, Hh, Hl, hwait=2 * KC if n == 0 else None)
            for o in range(O_IN1 + N_IN1 - NACC, O_IN1 + N_IN1):
                wait_read(pe, o)
            attention(1)
            pe.wait_ge(scores_read, use[1, "ct", (QT - 1, 1)] + 1)
            project_out(1, U_OUT1, O_OUT1, 3)
            ffn(1)
            for k in range(KC):
                pe.wait_ge(fin_ready, k + 1)
                if k >= 2:
                    pe.wait_ge(fin_copied, k - 1)
                for t in range(QT):
                    mm = nc.tensor.transpose(bank[:, 4 + k % 2, t * P:(t + 1) * P], hf[:, k % 2, t * P:(t + 1) * P], ident[:])
                mm.then_inc(fin_turned, 1)

        @block.scalar
        def _(act):
            def round_unit(u, it=0, stride=0):
                if u >= U_END:
                    return
                nk, w = 8, P
                for d in U_DN:
                    if d <= u < d + 3 * KC:
                        nk = DOWN[(u - d) % 3]
                if u < N_IN0:
                    w = UN0[u][3]
                if u >= SPL:
                    act.wait_ge(unit_done, u - SPL + 1 + it * stride)
                act.wait_ge(raw_loaded[u % RAW], raw_count(u) + it * (stride // RAW * 16))
                nc.scalar.copy(Wh[:, u % SPL, 0:nk, 0:w], raw[:, u % RAW, 0:nk, 0:w]).then_inc(weights_hi, 1)

            def square(norm, k):
                n = norm * KC + k
                act.wait_ge(xt_ready, n + 1)
                if n >= 2:
                    act.wait_ge(sq_used, n - 1)
                nc.scalar.activation(sq[:, k % 2, :], XT[:, k, :], ACT.Square).then_inc(sq_ready, 1)

            def norm_root(norm):
                act.wait_ge(sq_used, KC * (norm + 1))
                nc.scalar.activation(rs[:], bank[:, 7, :], ACT.Sqrt, bias=eps[:, 0:1], scale=1.0 / D).then_inc(rms_ready, 1)

            def norm_round(norm):
                for k in range(KC):
                    act.wait_ge(hf_ready, norm * KC + k + 1)
                    nc.scalar.copy(Hh[:, k, :], hf[:, k % 2, :]).then_inc(hh_ready, 1)

            round_unit(0)
            round_unit(1)
            for k in range(KC):
                square(0, k)
            act.wait_ge(memsets, N_MEMSETS)
            norm_root(0)
            for v in range(2):
                act.wait_ge(row_made, v + 1)
                n = (12, 8)[v]
                nc.scalar.copy(brow[0:n, v, 0:S], bank[0:n, 4, :])
                nc.scalar.copy(brow[0:n, v, S:FROW], bank[0:n, 5, 0:FROW - S]).then_inc(row_copied, 1)
            norm_round(0)
            for n, (kind, idx, col, w) in enumerate(UN0):
                o = O_IN0 + n
                src = bank[:, o % NACC, :]
                free = tile_read[o % NACC]
                round_unit(U_IN0 + n + SPL)
                if kind == "g":
                    if idx >= 2:
                        wait_read(act, o - 3)
                    nc.scalar.activation(yb[:, idx % 2, :], src, ACT.Sigmoid).then_inc(free, 1)
                elif kind == "kc":
                    if idx == 0:
                        act.wait_ge(h_ready, KC)
                    for g in range(2):
                        half = slice(HD * g, HD * g + HD)
                        nc.scalar.copy(KK[0:HD, idx, g, :], bank[half, o % NACC, :])
                        last = nc.scalar.copy(KK[HD:P, idx, g, 0:S - 1], bank[half, o % NACC, 1:S])
                    last.then_inc(free, 1)
                elif kind == "q":
                    nc.scalar.mul(Q0[:, idx, :], src, HD ** -0.5).then_inc(free, 1)
                elif kind == "k":
                    nc.scalar.copy(K0[:, idx, :], src).then_inc(free, 1)
                elif kind == "v":
                    nc.scalar.copy(V0[:, idx].rearrange("p t c -> p (t c)"), src).then_inc(free, 1)
                elif kind == "gate":
                    nc.scalar.activation(gate[:].rearrange("p t c -> p (t c)"), bank[:, o % NACC, 0:QT * 24],
                                         ACT.Sigmoid).then_inc(free, 1)
            for kv in range(2):
                act.wait_ge(hid_made, kv + 1)
                nc.scalar.activation(hid[:, kv], bank[:, 5 + kv, 0:2 * P].rearrange("p (a n) -> p a n", a=2)[:, :, 0:2 * NCMP],
                                     ACT.Silu).then_inc(hid_ready, 1)
            act.wait_ge(cmp_made, 1)
            nc.scalar.copy(kcT[:, 0:NCMP], bank[:, 5, 0:NCMP])
            for g in range(2):
                for q in range(4):
                    last = nc.scalar.copy(vbd[32 * q:32 * q + NCMP, g, HD * q:HD * q + HD],
                                          bank[32 * q:32 * q + NCMP, 6, 256 * g + HD * q:256 * g + HD * q + HD])
            last.then_inc(cmp_ready, 1)
            for c in range(4):
                act.wait_ge(ln_centered, c + 1)
                if c >= 2:
                    act.wait_ge(ln_var, c - 1)
                nc.scalar.activation(sq2(c), CA[:, c, :], ACT.Square).then_inc(ln_sq, 1)
            act.wait_ge(ln_var, 4)
            nc.scalar.activation(tm[:, 2, :], bank[:, 4, :], ACT.Sqrt, bias=eps[:, 0:1], scale=1.0 / 512).then_inc(ln_std, 1)
            for c in range(4):
                act.wait_ge(ln_scaled, c + 1)
                nc.scalar.activation(CA[:, c, :], CA[:, c, :], ACT.Silu, bias=prm[:, PR_LNB + c:PR_LNB + c + 1]).then_inc(u_ready, 1)
            for c in range(4):
                act.wait_ge(u_ready, c + 1)
                nc.scalar.copy(Hh[:, 4 + c, :], CA[:, c, :]).then_inc(cc_hi, 1)

            def attention(layer):
                J = JOBS * layer
                if layer == 1:
                    act.wait_ge(lam_dots, 1)
                    nc.scalar.activation(lamb[:, 2:4], lamb[:, 0:2], ACT.Exp).then_inc(lam_exps, 1)
                for s in range(STEPS):
                    i, r = divmod(s, PER)
                    if s < JOBS:
                        L = job(layer, s)[5]
                        w = P * (s // PER + 1)
                        act.wait_ge(scores_read, use[layer, s] + 1)
                        if J + s >= 3:
                            act.wait_ge(probs_turned, J + s - 2)
                        nc.scalar.activation(Pb[:, s % 3, 0:w], S2[:, s % 2, 0:w], ACT.Exp, bias=nmx[:, s % 2:s % 2 + 1],
                                             scale=-1.0, accum_out=L).then_inc(probs_ready, 1)
                    for key in CT[layer].get(s, []):
                        n = use[layer, "ct", key]
                        act.wait_ge(ct_turned, CTN[layer, "ct", key] + 1)
                        c0 = 4 * key[1]
                        nc.scalar.copy(Hh[:, c0:c0 + 4, P * key[0]:P * (key[0] + 1)],
                                       bank[:, 4 + n % 2, :].rearrange("p (c t) -> p c t", c=4)).then_inc(ct_hi, 1)
                    j = s - 2
                    if 0 <= j < JOBS and j % 2 == 1:
                        w = P * (j // PER + 1)
                        act.wait_ge(probs_turned, J + j + 1)
                        if J + j >= 2:
                            act.wait_ge(pv_done, J + j - 1)
                        nc.scalar.copy(PTs[:, 1, 0:w], bank[:, 7, 0:w]).then_inc(pt_copied[1], 1)
                    if layer == 0 and r == STEP_CMP["exp"] and i < QT:
                        act.wait_ge(sc_shifted, i + 1)
                        nc.scalar.activation(Pc[:].rearrange("p h n -> p (h n)"), Sm[:].rearrange("p h n -> p (h n)"),
                                             ACT.Exp).then_inc(pc_ready, 1)
                    if layer == 1 and s >= STEP_COMBINE and (s - STEP_COMBINE) % PER == 0:
                        n = (s - STEP_COMBINE) // PER
                        act.wait_ge(o_squared, n + 1)
                        nc.scalar.activation(Rs[:, 20:24], Rs[:, 16:20], ACT.Sqrt, bias=eps[:, 0:1],
                                             scale=1.0 / (2 * HD)).then_inc(o_rms, 1)

            def project_out(u0, norm):
                for n in range(KC):
                    round_unit(u0 + n + SPL)
                    square(norm, n)
                norm_root(norm)
                norm_round(norm)

            def ffn(layer):
                u0, o0 = U_GU[layer], O_GU[layer]
                with act.Fori(0, FC // 2) as it:
                    for q in range(2):
                        u, o, m = u0 + 2 * q, o0 + 2 * q, FC * layer + q
                        cols = prm_ff(layer, it, q)
                        round_unit(u + SPL, it, 4)
                        nc.scalar.activation(yb[:, q, :], bank[:, o % NACC, :], ACT.Identity, bias=cols[3],
                                             scale=cols[2]).then_inc(y_base, 1)
                        act.wait_ge(tile_read[o % NACC], reads(o) + it)
                        nc.scalar.activation(yb[:, q, :], yb[:, q, :], ACT.Gelu).then_inc(y_gelu, 1)
                        round_unit(u + 1 + SPL, it, 4)
                        act.wait_ge(tile_read[(o + 1) % NACC], reads(o + 1) + it)
                        nc.scalar.copy(one(Ah, it, q), ab[:, q, :]).then_inc(ah_ready, 1)
                norm = 2 * layer + 2
                for n in range(KC):
                    for r in range(3):
                        round_unit(U_DN[layer] + 3 * n + r + SPL)
                    square(norm, n)
                norm_root(norm)
                if layer == 0:
                    norm_round(norm)

            attention(0)
            project_out(U_OUT0, 1)
            ffn(0)
            for n, (kind, idx, col, w) in enumerate(UN1):
                o = O_IN1 + n
                src = bank[:, o % NACC, :]
                free = tile_read[o % NACC]
                round_unit(U_IN1 + n + SPL)
                if kind == "q":
                    nc.scalar.mul(Q1[:, idx, :], src, HD ** -0.5).then_inc(free, 1)
                elif kind == "k":
                    nc.scalar.copy(K1[:, idx, :], src).then_inc(free, 1)
                else:
                    V = Vc if kind == "cv" else Vd
                    nc.scalar.copy(V[:, :, P * idx:P * (idx + 1)], src.rearrange("p (t c) -> p t c", t=QT)).then_inc(free, 1)
            attention(1)
            project_out(U_OUT1, 3)
            ffn(1)

        @block.vector
        def _(dve):
            count = [0]

            def step(ins):
                count[0] += 1
                ins.then_inc(dstep, 1)
                dve.wait_ge(dstep, count[0])

            def norm_apply(norm, col):
                dve.wait_ge(rms_ready, norm + 1)
                step(nc.vector.reciprocal(rs[:], rs[:]))

                def rest(k):
                    dve.wait_ge(hh_ready, norm * KC + k + 1)
                    nc.vector.tensor_tensor(Hl[:, k, :], hf[:, k % 2, :], Hh[:, k, :].bitcast(F32),
                                            ALU.subtract).then_inc(h_ready, 1)

                for k in range(KC):
                    if k >= 2:
                        dve.wait_ge(h_ready, norm * KC + k - 1)
                    nc.vector.scalar_tensor_tensor(out=hf[:, k % 2, :], in0=XT[:, k, :], scalar=prm[:, col + k:col + k + 1],
                                                   in1=rs[:], op0=ALU.mult, op1=ALU.mult).then_inc(hf_ready, 1)
                    if k >= 1:
                        rest(k - 1)
                rest(KC - 1)

            for k in range(KC):
                dve.wait_ge(turned, k + 1)
                nc.vector.tensor_copy(XT[:, k, :], bank[:, 4 + k % 4, :]).then_inc(xt_ready, 1)
            c0 = 0
            for b, n in enumerate((PR_A, 4 * CONV_W, 4 * FC, 4 * FC)):
                dve.wait_ge(turned, KC + b + 1)
                nc.vector.tensor_copy(prm[:, c0:c0 + n], bank[:, b, 0:n]).then_inc(param_copied, 1)
                c0 += n
            dve.wait_ge(param_copied, 4)
            norm_apply(0, PR_MIX)

            def glu(c):
                wait_read(dve, O_IN0 + 2 * c)
                o = O_IN0 + 2 * c + 1
                dve.wait_ge(unit_done, U_IN0 + 2 * c + 2)
                nc.vector.tensor_tensor(Uc[:, c, PAD:PAD + S], yb[:, c % 2, :], bank[:, o % NACC, :],
                                        ALU.mult).then_inc(tile_read[o % NACC], 1)

            def taps(c, t0, t1):
                w = PR_DWW + c
                if t0 == 0:
                    wait_read(dve, O_IN0 + 2 * c + 1)
                for t in range(t0, t1):
                    if t == 0:
                        step(nc.vector.tensor_scalar(CA[:, c, :], Uc[:, c, 0:S], prm[:, w:w + 1],
                                                     prm[:, PR_DWB + c:PR_DWB + c + 1], ALU.mult, ALU.add))
                        continue
                    ins = nc.vector.scalar_tensor_tensor(out=CA[:, c, :], in0=Uc[:, c, t:t + S],
                                                         scalar=prm[:, w + 4 * t:w + 4 * t + 1], in1=CA[:, c, :],
                                                         op0=ALU.mult, op1=ALU.add)
                    if t < CONV_W - 1:
                        step(ins)
                    else:
                        ins.then_inc(conv_done, 1)

            def flat(kv):
                wait_read(dve, O_IN0 + 8 + kv)
                for g in range(2):
                    src = spread(KK[:, kv, g, 0:1], (2, NPAIR), (16, NCMP))
                    pos = spread(prm[:, PR_POS + NPAIR * kv:PR_POS + NPAIR * kv + 1], (1, NPAIR), (0, NCMP))
                    ins = nc.vector.tensor_tensor(FT[:, kv, :, NCMP * g:NCMP * (g + 1)], src, pos, ALU.add)
                ins.then_inc(ft_ready, 1)

            dve.wait_ge(memsets, N_MEMSETS)
            glu(0)
            taps(0, 0, 14)
            glu(1)
            taps(0, 14, CONV_W)
            glu(2)
            taps(1, 0, 16)
            glu(3)
            taps(1, 16, CONV_W)
            flat(0)
            flat(1)
            taps(2, 0, CONV_W)
            taps(3, 0, CONV_W)
            dve.wait_ge(ln_mean, 1)
            for c in range(4):
                nc.vector.scalar_tensor_tensor(out=CA[:, c, :], in0=bank[:, 7, :], scalar=-1.0 / 512, in1=CA[:, c, :],
                                               op0=ALU.mult, op1=ALU.add).then_inc(ln_centered, 1)
            dve.wait_ge(ln_std, 1)
            step(nc.vector.reciprocal(tm[:, 2, :], tm[:, 2, :]))
            dve.wait_ge(ln_sq, 4)
            for c in range(4):
                nc.vector.scalar_tensor_tensor(out=CA[:, c, :], in0=CA[:, c, :], scalar=prm[:, PR_LNG + c:PR_LNG + c + 1],
                                               in1=tm[:, 2, :], op0=ALU.mult, op1=ALU.mult).then_inc(ln_scaled, 1)
            for c in range(4):
                dve.wait_ge(cc_hi, c + 1)
                nc.vector.tensor_tensor(Hl[:, 4 + c, :], CA[:, c, :], Hh[:, 4 + c, :].bitcast(F32),
                                        ALU.subtract).then_inc(cc_ready, 1)

            def combine0(i):
                dve.wait_ge(pv_done, PER * (i + 1))
                dve.wait_ge(oc_made, i + 1)
                step(nc.vector.reciprocal(Rs[:], Ls[:, i % 2, :]))
                step(nc.vector.tensor_tensor(Cs[:].rearrange("p (b h) -> p b h", b=3), Rs[:].rearrange("p (b h) -> p b h", b=3),
                                             spread(gate[:, i, 0:1], (1, 3), (3, 8)), ALU.mult))
                step(nc.vector.tensor_scalar(Cs[:, 0:8], Cs[:, 0:8], cmask[:, i, 32:33], None, ALU.mult))
                oc = spread(bank[:, 2, 2 * P:2 * P + 1], (S, 2), (HD, 4), (1, HD))
                nc.vector.tensor_tensor(tm[:, 0, :].rearrange("p (g h d) -> p g h d", g=2, h=4), oc,
                                        spread(Cs[:, 0:1], (4, 2), (1, 4), (0, HD)), ALU.mult)
                for b in range(2):
                    ins = nc.vector.tensor_tensor(tm[:, 1 + b, :].rearrange("p (h d) -> p h d", h=8),
                                                  bank[:, b, :].rearrange("p (h d) -> p h d", h=8),
                                                  spread(Cs[:, 8 + 8 * b:9 + 8 * b], (1, 8), (0, HD)), ALU.mult)
                step(ins)
                step(nc.vector.tensor_tensor(tm[:, 0, :], tm[:, 0, :], tm[:, 1, :], ALU.add))
                nc.vector.tensor_tensor(tm[:, 0, :], tm[:, 0, :], tm[:, 2, :], ALU.add).then_inc(combined, 1)

            def combine1(i):
                dve.wait_ge(pv_done, JOBS + PER * (i + 1))
                step(nc.vector.reciprocal(Rs[:, 0:16], Ls[:, i % 2, 0:16]))
                step(nc.vector.tensor_scalar(Rs[:, 4:8], Rs[:, 4:8], lamb[:, 4:5], None, ALU.mult))
                for m in range(2):
                    nc.vector.tensor_tensor(tn[:, m, :].rearrange("p (h d) -> p h d", h=4),
                                            bank[:, m, :].rearrange("p (h d) -> p h d", h=4),
                                            spread(Rs[:, 4 * m:4 * m + 1], (1, 4), (0, P)), ALU.mult)
                step(nc.vector.tensor_tensor(tn[:, 2, :].rearrange("p (h d) -> p h d", h=8),
                                             bank[:, 2, :].rearrange("p (h d) -> p h d", h=8),
                                             spread(Rs[:, 8:9], (1, 8), (0, HD)), ALU.mult))
                step(nc.vector.tensor_tensor(tn[:, 0, :], tn[:, 0, :], tn[:, 1, :], ALU.subtract))
                step(nc.vector.tensor_tensor(tn[:, 1, :], tn[:, 0, :], tn[:, 0, :], ALU.mult))
                nc.vector.tensor_reduce(Rs[:, 16:20], tn[:, 1, :].rearrange("p (h d) -> p h d", h=4), AXX,
                                        ALU.add).then_inc(o_squared, 1)
                dve.wait_ge(o_rms, i + 1)
                step(nc.vector.reciprocal(Rs[:, 20:24], Rs[:, 20:24]))
                step(nc.vector.tensor_tensor(tn[:, 0, :].rearrange("p (h d) -> p h d", h=4),
                                             tn[:, 0, :].rearrange("p (h d) -> p h d", h=4),
                                             spread(Rs[:, 20:21], (1, 4), (0, P)), ALU.mult))
                nc.vector.tensor_tensor(tn[:, 0, :].rearrange("p (h d) -> p h d", h=4),
                                        tn[:, 0, :].rearrange("p (h d) -> p h d", h=4),
                                        spread(dng[:, 0:1], (0, 4), (1, P)), ALU.mult).then_inc(combined, 1)

            def attention(layer):
                J = JOBS * layer
                dve.wait_ge(strips_loaded, 16 * (layer + 1))
                if layer == 1:
                    step(nc.vector.tensor_tensor(lamp[:, 0, :], lamp[:, 0, :], lamp[:, 1, :], ALU.mult))
                    step(nc.vector.tensor_tensor(lamp[:, 2, :], lamp[:, 2, :], lamp[:, 3, :], ALU.mult))
                    nc.vector.tensor_reduce(lamb[:, 0:2], spread(lamp[:, 0, 0:1], (2 * HD, 2), (1, HD)), AXX,
                                            ALU.add).then_inc(lam_dots, 1)
                    dve.wait_ge(lam_exps, 1)
                    step(nc.vector.tensor_tensor(lamb[:, 4:5], lamb[:, 2:3], lamb[:, 3:4], ALU.subtract))
                    step(nc.vector.tensor_scalar(lamb[:, 4:5], lamb[:, 4:5], LAM_INIT, None, ALU.add))
                    step(nc.vector.tensor_scalar(dng[:], dng[:], 1.0 - LAM_INIT, None, ALU.mult))
                for s in range(STEPS):
                    i, r = divmod(s, PER)
                    if s < JOBS:
                        T = job(layer, s)[2]
                        w = P * (i + 1)
                        n = use[layer, s]
                        dve.wait_ge(qk_done, J + s + 1)
                        if J + s >= 2:
                            dve.wait_ge(probs_ready, J + s - 1)
                        nc.vector.tensor_tensor_reduce(out=S2[:, s % 2, 0:w], in0=bank[:, 4 + n % 2, 0:w], in1=T, scale=-1.0,
                                                       scalar=3.0e38, op0=ALU.add, op1=ALU.min,
                                                       accum_out=nmx[:, s % 2:s % 2 + 1]).then_inc(scores_read, 1)
                    for key in CT[layer].get(s, []):
                        n = use[layer, "ct", key]
                        c0 = 4 * key[1]
                        dve.wait_ge(ct_hi, CTN[layer, "ct", key] + 1)
                        ts = slice(P * key[0], P * (key[0] + 1))
                        nc.vector.tensor_tensor(Hl[:, c0:c0 + 4, ts], bank[:, 4 + n % 2, :].rearrange("p (c t) -> p c t", c=4),
                                                Hh[:, c0:c0 + 4, ts].bitcast(F32), ALU.subtract).then_inc(scores_read, 1)
                    j = s - 2
                    if 0 <= j < JOBS and j % 2 == 0:
                        w = P * (j // PER + 1)
                        dve.wait_ge(probs_turned, J + j + 1)
                        if J + j >= 2:
                            dve.wait_ge(pv_done, J + j - 1)
                        nc.vector.tensor_copy(PTs[:, 0, 0:w], bank[:, 6, 0:w]).then_inc(pt_copied[0], 1)
                    if layer == 0 and i < QT:
                        if r == STEP_CMP["shift"]:
                            dve.wait_ge(sc_made, i + 1)
                            step(nc.vector.tensor_tensor(Sm[:].rearrange("p (g h) n -> p g h n", g=2),
                                                         spread(bank[:, 2, 0:1], (S, 2), (32, 4), (1, 32)),
                                                         spread(cmask[:, i, 0:1], (0, 2), (0, 4), (1, 32)), ALU.add))
                            step(nc.vector.tensor_reduce(cmx[:], Sm[:], AXX, ALU.max))
                            nc.vector.tensor_tensor(Sm[:], Sm[:], spread(cmx[:, 0:1], (1, 8), (0, 32)),
                                                    ALU.subtract).then_inc(sc_shifted, 1)
                        if r == STEP_CMP["sum"]:
                            dve.wait_ge(pc_ready, i + 1)
                            nc.vector.tensor_reduce(Ls[:, i % 2, 0:8], Pc[:], AXX, ALU.add)
                        if r == STEP_CMP["copy"]:
                            dve.wait_ge(pc_turned, i + 1)
                            nc.vector.tensor_copy(PcT[:], spread(bank[:, 2, P:P + 1], (S, 2), (1, P))).then_inc(pc_copied, 1)
                    if s >= STEP_COMBINE and (s - STEP_COMBINE) % PER == 0:
                        (combine0, combine1)[layer]((s - STEP_COMBINE) // PER)

            def project_out(layer, u0, o0, norm):
                for n in range(KC):
                    dve.wait_ge(unit_done, u0 + n + 1)
                    nc.vector.tensor_tensor(XT[:, n, :], XT[:, n, :], bank[:, (o0 + n) % NACC, :], ALU.add).then_inc(xt_ready, 1)
                norm_apply(norm, PR_FFN + KC * layer)

            def ffn(layer):
                u0, o0 = U_GU[layer], O_GU[layer]
                base = count[0]
                with dve.Fori(0, FC // 2) as it:
                    for q in range(2):
                        u, o, m = u0 + 2 * q, o0 + 2 * q, FC * layer + q
                        cols = prm_ff(layer, it, q)
                        y, a = yb[:, q, :], ab[:, q, :]
                        gt, up = bank[:, o % NACC, :], bank[:, (o + 1) % NACC, :]
                        dve.wait_ge(y_base, m + 1 + it * 2)
                        nc.vector.scalar_tensor_tensor(out=y[:, 1:S], in0=gt[:, 0:S - 1], scalar=cols[1], in1=y[:, 1:S],
                                                       op0=ALU.mult, op1=ALU.add).then_inc(dstep, 1)
                        dve.wait_ge(dstep, base + q + 1 + it * 2)
                        nc.vector.scalar_tensor_tensor(out=y[:, 2:S], in0=gt[:, 0:S - 2], scalar=cols[0], in1=y[:, 2:S],
                                                       op0=ALU.mult, op1=ALU.add).then_inc(tile_read[o % NACC], 1)
                        dve.wait_ge(y_gelu, m + 1 + it * 2)
                        dve.wait_ge(unit_done, u + 2 + it * 4)
                        nc.vector.tensor_tensor(a, y, up, ALU.mult).then_inc(tile_read[(o + 1) % NACC], 1)
                        dve.wait_ge(ah_ready, m + 1 + it * 2)
                        nc.vector.tensor_tensor(one(Al, it, q), a, one(Ah, it, q).bitcast(F32), ALU.subtract).then_inc(a_ready, 1)
                count[0] = base + FC
                for n in range(KC):
                    dve.wait_ge(unit_done, U_DN[layer] + 3 * n + 3)
                    nc.vector.tensor_tensor(XT[:, n, :], XT[:, n, :], bank[:, (O_DN[layer] + n) % NACC, :],
                                            ALU.add).then_inc(xt_ready, 1)

            attention(0)
            project_out(0, U_OUT0, O_OUT0, 1)
            ffn(0)
            norm_apply(2, PR_MIX + KC)
            attention(1)
            project_out(1, U_OUT1, O_OUT1, 3)
            ffn(1)
            dve.wait_ge(rms_ready, 5)
            step(nc.vector.reciprocal(rs[:], rs[:]))

            def leave(k):
                dve.wait_ge(fin_turned, k + 1)
                nc.vector.tensor_copy(xout[:, k].rearrange("p t c -> p (t c)"), bank[:, 4 + k % 2, :]).then_inc(fin_copied, 1)

            for k in range(KC):
                nc.vector.scalar_tensor_tensor(out=hf[:, k % 2, :], in0=XT[:, k, :], scalar=prm[:, PR_FIN + k:PR_FIN + k + 1],
                                               in1=rs[:], op0=ALU.mult, op1=ALU.mult).then_inc(fin_ready, 1)
                if k >= 1:
                    leave(k - 1)
            leave(KC - 1)


INPUTS = ["x", "rel_bias_table", "mix_norm_g", "ffn_norm_g", "ffn_w_gate", "ffn_w_up", "ffn_conv_w", "ffn_conv_b",
          "ffn_w_down", "ev_w_in", "ev_w_out", "nsa_phi_pos", "nsa_phi_w1", "nsa_phi_w2", "conv_dw_w", "conv_dw_b",
          "conv_ln_g", "conv_ln_b", "od_w_in", "od_w_out", "diff_lambda", "diff_norm_g", "final_norm_g"]


def shape_constants():
    import numpy as np

    onehot = np.zeros((BUCKETS + 1, 2, FROW), np.float32)
    exact = BUCKETS // 2
    for j in range(FROW):
        d = j - (P - 1)
        if d < 0 or d >= S:
            onehot[BUCKETS, :, j] = NEG
            continue
        b = d if d < exact else min(BUCKETS - 1, exact + int(math.log(d / exact) / math.log(2048 / exact) * (BUCKETS - exact)))
        onehot[b, :, j] = 1.0
        m = (d <= 128) + (d % 4 == 0) + (d % 16 == 0)
        onehot[BUCKETS, 1, j] = math.log(m) if m else NEG
    cmask = np.zeros((P, QT, 33), np.float32)
    for i in range(QT):
        for p in range(P):
            for n in range(32):
                if n >= NCMP or 16 * n + 31 > P * i + p:
                    cmask[p, i, n] = NEG
            cmask[p, i, 32] = float(P * i + p >= 31)
    return {"onehot": onehot, "ident": np.eye(P, dtype=np.float32), "cmpmask": cmask}


def kernel(**inputs):
    import numpy as np
    import concourse.bacc as bacc
    from concourse.bass_utils import run_bass_kernel_spmd

    nc = bacc.Bacc("TRN2", target_bir_lowering=False, num_devices=1)
    arrays, args = {}, []
    given = {name: np.ascontiguousarray(inputs[name]) for name in INPUTS}
    given.update(shape_constants())
    for name, a in given.items():
        arrays[f"in_{name}"] = a
        args.append(nc.dram_tensor(f"in_{name}", a.shape, mybir.dt.from_np(a.dtype), kind="ExternalInput").ap())
    args.append(nc.dram_tensor("bias_rows", (20, FROW), F32, kind="Internal").ap())
    args.append(nc.dram_tensor("out_0", (1, S, D), F32, kind="ExternalOutput").ap())
    build(nc, *args)
    r = run_bass_kernel_spmd(nc, [arrays], core_ids=[0])
    return r.results[0]["out_0"]
```

```python
import math
from contextlib import ExitStack

import concourse.bass as bass
from concourse import mybir

F32 = mybir.dt.float32
F32R = mybir.dt.float32r
ALU = mybir.AluOpType
ACT = mybir.ActivationFunctionType
AXX = mybir.AxisListType.X

P = 128
D = 1024
S = 512
KC = D // P
QT = S // P
HD = 64
F = 2816
FC = F // P
EPS = 1e-6
NEG = -1e30
EV_IN = 2328
CONV_W = 31
PAD = CONV_W - 1
NCMP = 31
NPAIR = 16
BUCKETS = 32
FROW = 640
LAM_INIT = 0.8 - 0.6 * math.exp(-0.3)
DOWN = (8, 8, 6)

U_IN0 = 0
N_IN0 = 19
U_OUT0 = U_IN0 + N_IN0
U_GU = [U_OUT0 + KC, 0]
U_DN = [U_GU[0] + 2 * FC, 0]
U_IN1 = U_DN[0] + 3 * KC
N_IN1 = 24
U_OUT1 = U_IN1 + N_IN1
U_GU[1] = U_OUT1 + KC
U_DN[1] = U_GU[1] + 2 * FC
U_END = U_DN[1] + 3 * KC
O_IN0 = 0
O_OUT0 = O_IN0 + N_IN0
O_GU = [O_OUT0 + KC, 0]
O_DN = [O_GU[0] + 2 * FC, 0]
O_IN1 = O_DN[0] + KC
O_OUT1 = O_IN1 + N_IN1
O_GU[1] = O_OUT1 + KC
O_DN[1] = O_GU[1] + 2 * FC
RAW = 4
SPL = 2
NACC = 4

PR_MIX, PR_FFN, PR_FIN = 0, 16, 32
PR_DWB, PR_LNG, PR_LNB, PR_POS = 40, 44, 48, 52
PR_A = 84
PR_DWW = PR_A
PR_FF = [PR_DWW + CONV_W * 4, PR_DWW + CONV_W * 4 + 4 * FC]
PR_N = PR_FF[1] + 4 * FC

N_MEMSETS = 6
JOBS = 64
PER = JOBS // QT


def in0_units():
    kv = 512
    glu = 512 + 768 + 24
    units = []
    for c in range(4):
        units += [("g", c, glu + 512 + c * P, P), ("a", c, glu + c * P, P)]
    units += [("kc", 0, kv, P), ("kc", 1, kv + P, P)]
    units += [("v", 0, kv + 384, P), ("v", 1, kv + 640, P), ("gate", 0, kv + 768, P)]
    units += [("k", 0, kv + 256, P), ("k", 1, kv + 512, P)]
    units += [("q", c, c * HD, P) for c in range(4)]
    return units


def in1_units():
    kinds = ["q"] * 4 + ["k"] * 4 + ["cv"] * 4 + ["q"] * 4 + ["k"] * 4 + ["dv"] * 4
    index = list(range(4)) * 3 + list(range(4, 8)) * 2 + list(range(4))
    units = [(k, n, u * P, P) for u, (k, n) in enumerate(zip(kinds, index))]
    return units[8:12] + units[20:24] + units[0:8] + units[12:20]


def build(nc, x, rel_bias_table, mix_norm_g, ffn_norm_g, ffn_w_gate, ffn_w_up, ffn_conv_w, ffn_conv_b,
          ffn_w_down, ev_w_in, ev_w_out, nsa_phi_pos, nsa_phi_w1, nsa_phi_w2, conv_dw_w, conv_dw_b,
          conv_ln_g, conv_ln_b, od_w_in, od_w_out, diff_lambda, diff_norm_g, final_norm_g,
          c_onehot, c_ident, c_cmpmask, bias_rows, out):
    ctx = ExitStack()
    with ctx:
        top = [16896]

        def at(name, shape, dt=F32, offset=None):
            size = 4
            for n in shape[1:]:
                size *= n
            size = -(-size // 32) * 32
            where = top[0] if offset is None else offset
            if offset is None:
                top[0] += size
            t = nc.alloc_sbuf_tensor_at(name, shape, dt, offset=where)
            return t, where + size

        def sb(name, shape, dt=F32):
            return at(name, shape, dt)[0]

        def sem(name):
            return ctx.enter_context(nc.semaphore(name))

        XT = sb("XT", [P, KC, S])
        Hh = sb("Hh", [P, KC, S], F32R)
        Hl = sb("Hl", [P, KC, S], F32R)
        raw = sb("raw", [P, RAW, 8, P])
        Wh = sb("Wh", [P, SPL, 8, P], F32R)
        Wl = sb("Wl", [P, SPL, 8, P], F32R)
        ident = sb("ident", [P, P])
        ones = sb("ones", [P, P])
        prm = sb("prm", [P, PR_N])
        kcT = sb("kcT", [P, 2, 32])
        vbd = sb("vbd", [P, 2, 4 * HD])
        cmask = sb("cmask", [P, QT, 33])
        gate = sb("gate", [P, QT, 24])
        Ls = sb("Ls", [P, 2, 24])
        Rs = sb("Rs", [P, 24])
        Cs = sb("Cs", [P, 24])
        nmx = sb("nmx", [P, 4])
        cmx = sb("cmx", [P, 8])
        Sm = sb("Sm", [P, 8, 32])
        Pc = sb("Pc", [P, 8, 32])
        PcT = sb("PcT", [P, 2, P])
        lamb = sb("lamb", [P, 8])
        eps = sb("eps", [P, 8])
        xs = sb("xs", [P, 2, QT])
        lamp = sb("lamp", [P, 4, HD])
        dng = sb("dng", [P, 2])
        tab = sb("tab", [BUCKETS + 1, 20])
        w2s = sb("w2s", [P, 2, 2, HD])
        hid = sb("hid", [P, 2, 2, 2 * NCMP])

        g0 = top[0]
        sq, e = at("sq", [P, 2, S], F32, g0)
        hf, e = at("hf", [P, 2, S], F32, e)
        rs, e = at("rs", [P, S], F32, e)
        yb, e = at("yb", [P, 2, S], F32, e)
        ab, e_work = at("ab", [P, 2, S], F32, e)
        S2, e = at("S2", [P, 2, S], F32, g0)
        Pb, e = at("Pb", [P, 4, S], F32, e)
        PTs, e = at("PTs", [P, 2, S], F32, e)
        acc = ab[:, 1, :]
        KK, e = at("KK", [P, 2, 2, S], F32, g0)
        FT, e = at("FT", [P, 2, NPAIR, 2 * NCMP], F32, e)
        assert e <= e_work
        a0 = e_work
        Ah, e = at("Ah", [P, FC, S], F32R, a0)
        Al, e_top = at("Al", [P, FC, S], F32R, e)
        assert e_top <= 229344
        T0, e = at("T0", [P, 8, S], F32, a0)
        xin, _ = at("xin", [P, QT, D], F32, e)
        Q0, e = at("Q0", [P, 4, S], F32, e)
        K0, e = at("K0", [P, 2, S], F32, e)
        V0, e = at("V0", [P, 2, QT, P], F32, e)
        Uc, e = at("Uc", [P, 4, PAD + S + 2], F32, e)
        CA, e = at("CA", [P, 4, S], F32, e)
        tm, e = at("tm", [P, 3, S], F32, e)
        onehot, _ = at("onehot", [BUCKETS + 1, 2, FROW], F32, e)
        pst, _ = at("pst", [P, 4, P], F32, _)
        brow, _ = at("brow", [12, 2, FROW], F32, _)
        xn, _ = at("xn", [P, QT, D], F32, _)
        assert _ <= e_top
        phw, e = at("phw", [P, 2, NPAIR, 2 * P], F32, e)
        assert e <= e_top
        T1, e = at("T1", [P, 12, S], F32, a0)
        Q1, e = at("Q1", [P, 8, S], F32, e)
        K1, e = at("K1", [P, 8, S], F32, e)
        Vc, e = at("Vc", [P, QT, S], F32, e)
        Vd, e = at("Vd", [P, QT, S], F32, e)
        tn, e = at("tn", [P, 3, S], F32, e)
        assert e <= e_top
        xout, _ = at("xout", [P, KC, QT, P], F32, a0)

        bank = ctx.enter_context(nc.psum_tensor("bank", [P, 8, S], F32))

        raw_loaded = [sem(f"raw_loaded{n}") for n in range(RAW)]
        weights_hi = sem("weights_hi")
        weights_lo = sem("weights_lo")
        unit_done = sem("unit_done")
        tile_read = [sem(f"tile_read{n}") for n in range(NACC)]
        x_loaded = [sem(f"x_loaded{t}") for t in range(QT)]
        ident_loaded = sem("ident_loaded")
        consts_loaded = sem("consts_loaded")
        params_loaded = [sem(f"params_loaded{b}") for b in range(4)]
        small_loaded = sem("small_loaded")
        phi_loaded = sem("phi_loaded")
        rows_stored = sem("rows_stored")
        strips_loaded = sem("strips_loaded")
        memsets = sem("memsets")
        turned = sem("turned")
        param_copied = sem("param_copied")
        row_made = sem("row_made")
        row_copied = sem("row_copied")
        xt_ready = sem("xt_ready")
        sq_ready = sem("sq_ready")
        sq_added = sem("sq_added")
        sq_summed = sem("sq_summed")
        rms_ready = sem("rms_ready")
        hh_ready = sem("hh_ready")
        h_ready = sem("h_ready")
        dstep = sem("dstep")
        ft_ready = sem("ft_ready")
        hid_made = sem("hid_made")
        hid_ready = sem("hid_ready")
        cmp_made = sem("cmp_made")
        cmp_ready = sem("cmp_ready")
        conv_done = sem("conv_done")
        ln_mean = sem("ln_mean")
        ln_centered = sem("ln_centered")
        ln_sq = sem("ln_sq")
        ln_var = sem("ln_var")
        ln_std = sem("ln_std")
        ln_scaled = sem("ln_scaled")
        u_ready = sem("u_ready")
        cc_hi = sem("cc_hi")
        cc_ready = sem("cc_ready")
        qk_done = sem("qk_done")
        scores_read = sem("scores_read")
        probs_ready = sem("probs_ready")
        probs_turned = sem("probs_turned")
        pt_copied = [sem("pt_copied_dve"), sem("pt_copied_act")]
        mixed = sem("mixed")
        pv_done = sem("pv_done")
        read_a = sem("read_a")
        read_b = sem("read_b")
        combined_a = sem("combined_a")
        combined_b = sem("combined_b")
        ct_turned = sem("ct_turned")
        ct_hi = sem("ct_hi")
        sc_made = sem("sc_made")
        sc_shifted = sem("sc_shifted")
        pc_ready = sem("pc_ready")
        pc_turned = sem("pc_turned")
        pc_copied = sem("pc_copied")
        oc_made = sem("oc_made")
        o_squared = sem("o_squared")
        o_rms = sem("o_rms")
        lam_dots = sem("lam_dots")
        lam_exps = sem("lam_exps")
        gain_ready = sem("gain_ready")
        y_base = sem("y_base")
        y_gelu = sem("y_gelu")
        ah_ready = sem("ah_ready")
        a_ready = sem("a_ready")
        fin_ready = sem("fin_ready")
        x_squared = sem("x_squared")
        x_std = sem("x_std")
        x_inverse = sem("x_inverse")
        x_scaled = sem("x_scaled")
        x_scaled_act = sem("x_scaled_act")
        xn_turned = sem("xn_turned")
        v_turned = sem("v_turned")
        v_placed = sem("v_placed")
        y_conv = sem("y_conv")
        prod = sem("prod")
        fin_turned = sem("fin_turned")
        fin_copied = sem("fin_copied")
        out_stored = sem("out_stored")

        w_in0 = ev_w_in[0].rearrange("(k p) n -> p k n", p=P)
        w_out = [ev_w_out[0].rearrange("(k p) n -> p k n", p=P), od_w_out[0].rearrange("(k p) n -> p k n", p=P)]
        w_in1 = od_w_in[0].rearrange("(k p) n -> p k n", p=P)
        w_gate = [ffn_w_gate[n].rearrange("(k p) n -> p k n", p=P) for n in range(2)]
        w_up = [ffn_w_up[n].rearrange("(k p) n -> p k n", p=P) for n in range(2)]
        w_down = [ffn_w_down[n].rearrange("(k p) n -> p k n", p=P) for n in range(2)]
        UN0, UN1 = in0_units(), in1_units()

        def spread(ap, *dims):
            return bass.AP(ap.tensor, ap.offset, [ap.ap[0], *[list(d) for d in dims]])

        def strip(t, head, i):
            v = t[:, head, :]
            return bass.AP(v.tensor, v.offset + P - 1 + P * i, [v.ap[0], [-1, P * (i + 1)]])

        def job(layer, j):
            i, r = divmod(j, PER)
            ks = slice(0, P * (i + 1))
            qs = slice(P * i, P * (i + 1))
            if layer == 0:
                br, c, g = r // 8, (r % 8) // 2, r % 2
                h = 4 * g + c
                half = slice(HD * g, HD * g + HD)
                return (Q0[half, c, qs], K0[half, br, ks], strip(T0, h, i),
                        [V0[:, br, t, half] for t in range(i + 1)], bank[:, br, HD * h:HD * h + HD],
                        Ls[:, i % 2, 8 + 8 * br + h:9 + 8 * br + h])
            if r < 8:
                h, m = divmod(r, 2)
                half = slice(HD * m, HD * m + HD)
                return (Q1[half, h, qs], K1[half, h, ks], strip(T1, h, i),
                        [Vc[:, t, P * h:P * h + P] for t in range(i + 1)], bank[:, 0, P * h:P * h + P],
                        Ls[:, i % 2, 4 * m + h:4 * m + h + 1])
            h = r - 8
            half = slice(HD * (h % 2), HD * (h % 2) + HD)
            return (Q1[half, 4 + h // 2, qs], K1[half, 4 + h // 2, ks], strip(T1, 4 + h, i),
                    [Vd[:, t, HD * h:HD * h + HD] for t in range(i + 1)], bank[:, 2, HD * h:HD * h + HD],
                    Ls[:, i % 2, 8 + h:9 + h])

        CT = [{PER * i + 23: [(i, 0)] for i in range(QT)},
              {**{PER * i + 19: [(i, 0)] for i in range(QT)}, **{PER * i + 22: [(i, 1)] for i in range(QT)}}]
        LAST_CT = [PER * (QT - 1) + 23, PER * (QT - 1) + 22]
        STEPS = PER * (QT - 1) + 24
        LAG_T, LAG_V = 3, 4
        use = {}
        for layer in range(2):
            for s in range(STEPS):
                if s < JOBS:
                    use[layer, s] = len(use)
                for key in CT[layer].get(s, []):
                    use[layer, "ct", key] = len(use)
        CTN = {key: n for n, key in enumerate(k for k in use if k[1] == "ct")}

        def map_of(layer, j):
            return j % 2 if layer == 1 and j % PER < 8 else None

        def pairs(j):
            return 4 * (j // PER) + j % PER // 2 + 1

        turns = {}
        for layer in range(2):
            for j in range(JOBS):
                if map_of(layer, j) != 0:
                    turns[layer, j] = len(turns)
        STEP_CMP = {"scores": 1, "shift": 1, "exp": 4, "sum": 5, "turn": 6, "copy": 7, "values": 9}
        HIDDEN_AFTER, LN_AFTER = (14, 15), 16
        TURN0 = [n for n, un in enumerate(UN0) if un[0] in ("v", "gate")]
        TURN1 = [n for n, un in enumerate(UN1) if un[0] in ("cv", "dv")]
        STEP_ROOT = 15
        STEP_U = {2 * PER + 2: 0, 2 * PER + 4: 1, 2 * PER + 6: 2, 2 * PER + 8: 3}

        block = ctx.enter_context(nc.Block())

        def wait_read(eng, o, it=0):
            for n, o0 in enumerate((O_OUT0, O_DN[0], O_OUT1, O_DN[1])):
                if o0 <= o < o0 + KC:
                    eng.wait_ge(xt_ready, KC * (n + 1) + o - o0 + 1)
                    return
            eng.wait_ge(tile_read[o % NACC], reads(o) + it)

        def reads(o):
            kept = [range(o0, o0 + KC) for o0 in (O_OUT0, O_DN[0], O_OUT1, O_DN[1])]
            return sum(not any(t in r for r in kept) for t in range(o % NACC, o + 1, NACC))

        def raw_count(u):
            n = 0
            for v in range(u % RAW, u + 1, RAW):
                n += 32 if v < N_IN0 and UN0[v][0] == "q" else 16
            return n

        def staged_at(v):
            o = O_IN0 + TURN0[v] if v < len(TURN0) else O_IN1 + TURN1[v - len(TURN0)]
            return tile_read[o % NACC], reads(o)

        def gain(norm, k):
            col = {1: PR_FFN, 2: PR_MIX + KC, 3: PR_FFN + KC}[norm] + k
            return prm[:, col:col + 1]

        def sq2(c):
            return tm[:, c % 2, :]

        def prm_ff(layer, it, q):
            return [prm[:, bass.ds(it * 2 + (PR_FF[layer] + FC * t + q), 1)] for t in range(4)]

        def one(t, it, q):
            return t[:, bass.ds(it * 2 + q, 1), :].rearrange("p a n -> p (a n)")

        @block.sync
        def _(sp):
            def load(u, src, nk=8, w=P, it=0, stride=0):
                if u >= RAW:
                    sp.wait_ge(weights_lo, u - RAW + 1 + it * stride)
                sp.dma_start(raw[:, u % RAW, 0:nk, 0:w], src).then_inc(raw_loaded[u % RAW], 16)

            def load_in0(u):
                kind, n, col, w = UN0[u - U_IN0]
                if kind != "q":
                    load(u, w_in0[:, :, col:col + w], w=w)
                    return
                if u >= RAW:
                    sp.wait_ge(weights_lo, u - RAW + 1)
                for g in range(2):
                    sp.dma_start(raw[:, u % RAW, :, HD * g:HD * g + HD],
                                 w_in0[:, :, col + 4 * HD * g:col + 4 * HD * g + HD]).then_inc(
                        raw_loaded[u % RAW], 16)

            for t in range(QT):
                sp.dma_start(xin[:, t, :], x[0, t * P:(t + 1) * P, :]).then_inc(x_loaded[t], 16)
            rows = [(0, PR_MIX, mix_norm_g.rearrange("l (k p) -> (l k) p", p=P)),
                    (0, PR_FFN, ffn_norm_g.rearrange("l (k p) -> (l k) p", p=P)),
                    (0, PR_FIN, final_norm_g.rearrange("(k p) -> k p", p=P)),
                    (0, PR_DWB, conv_dw_b[0].rearrange("(k p) -> k p", p=P)),
                    (0, PR_LNG, conv_ln_g[0].rearrange("(k p) -> k p", p=P)),
                    (0, PR_LNB, conv_ln_b[0].rearrange("(k p) -> k p", p=P)),
                    (0, PR_POS, nsa_phi_pos[0].rearrange("v (k l) d -> (v k) (l d)", l=2)),
                    (1, 0, conv_dw_w[0].rearrange("t (k p) -> (t k) p", p=P)),
                    (2, 0, ffn_conv_w[0].rearrange("t (k p) -> (t k) p", p=P)),
                    (2, 3 * FC, ffn_conv_b[0].rearrange("(k p) -> k p", p=P)),
                    (3, 0, ffn_conv_w[1].rearrange("t (k p) -> (t k) p", p=P)),
                    (3, 3 * FC, ffn_conv_b[1].rearrange("(k p) -> k p", p=P))]
            for b, r, src in rows:
                sp.dma_start(pst[r:r + src.shape[0], b, :], src).then_inc(params_loaded[b], 16)
            for u in range(2, RAW):
                load_in0(u)
            sp.dma_start(tab[0:BUCKETS, :], rel_bias_table).then_inc(consts_loaded, 16)
            sp.dma_start(onehot[:], c_onehot).then_inc(consts_loaded, 16)
            sp.dma_start(cmask[:], c_cmpmask).then_inc(small_loaded, 16)
            sp.dma_start(w2s[:], nsa_phi_w2[0].rearrange("v (h p) d -> p v h d", p=P)).then_inc(small_loaded, 16)
            sp.dma_start(lamp[:], bass.AP(diff_lambda.tensor, 0, [[0, P], [HD, 4], [1, HD]])).then_inc(small_loaded, 16)
            sp.dma_start(dng[:, 0:1], diff_norm_g.rearrange("l p -> p l")).then_inc(small_loaded, 16)
            for u in range(RAW, RAW + 4):
                load_in0(u)
            sp.wait_ge(row_copied, 2)
            sp.dma_start(bias_rows[0:12, :], brow[0:12, 0, :]).then_inc(rows_stored, 16)
            sp.dma_start(bias_rows[12:20, :], brow[0:8, 1, :]).then_inc(rows_stored, 16)
            sp.wait_ge(rows_stored, 32)

            def strips(dst, head, n):
                src = bass.AP(bias_rows.tensor, head * FROW, [[1, P], [FROW, n], [1, S]])
                sp.dma_start(dst[:, 0:n, :], src).then_inc(strips_loaded, 16)

            strips(T0, 0, 8)
            sp.wait_ge(param_copied, 4)
            sp.wait_ge(xn_turned, KC)
            for n, u in enumerate(range(RAW + 4, N_IN0)):
                load_in0(u)
                if n < 8:
                    kv, l0 = n // 4, 4 * (n % 4)
                    sp.dma_start(phw[:, kv, l0:l0 + 4], nsa_phi_w1[0, kv, P * l0:P * (l0 + 4)].rearrange(
                        "(k p) h -> p k h", p=P)).then_inc(phi_loaded, 16)
            for n in range(KC):
                load(U_OUT0 + n, w_out[0][:, :, n * P:(n + 1) * P])

            def load_ffn(layer):
                with sp.Fori(0, FC // 2) as it:
                    for j in range(4):
                        w = (w_gate, w_up)[j % 2][layer]
                        load(U_GU[layer] + j, w[:, :, bass.ds(it * (2 * P) + (j // 2) * P, P)], it=it, stride=4)
                for n in range(KC):
                    k = 0
                    for r in range(3):
                        load(U_DN[layer] + 3 * n + r, w_down[layer][:, k:k + DOWN[r], n * P:(n + 1) * P], nk=DOWN[r])
                        k += DOWN[r]

            load_ffn(0)
            for u, (kind, n, col, w) in enumerate(UN1):
                if u == 6:
                    sp.wait_ge(unit_done, U_IN1)
                    strips(T1, 8, 12)
                load(U_IN1 + u, w_in1[:, :, col:col + w])
            for n in range(KC):
                load(U_OUT1 + n, w_out[1][:, :, n * P:(n + 1) * P])
            load_ffn(1)
            for k in range(KC):
                sp.wait_ge(fin_copied, k + 1)
                sp.dma_start(out[0, :, k * P:(k + 1) * P].rearrange("(t p) c -> p t c", p=P), xout[:, k]).then_inc(out_stored, 16)
            sp.wait_ge(out_stored, 16 * KC)

        @block.gpsimd
        def _(pool):
            fills = [(eps[:], EPS), (ones[:], 1.0), (tab[BUCKETS:BUCKETS + 1, :], 1.0), (kcT[:], 0.0), (vbd[:], 0.0),
                     (Uc[:, :, 0:PAD], 0.0)]
            assert len(fills) == N_MEMSETS
            for n, (dst, value) in enumerate(fills):
                if n:
                    pool.wait_ge(memsets, n)
                nc.gpsimd.memset(dst, value).then_inc(memsets, 1)
            pool.wait_ge(memsets, N_MEMSETS)

            def rest(u, nk=8, w=P, it=0, stride=0):
                pool.wait_ge(weights_hi, u + 1 + it * stride)
                hi = Wh[:, u % SPL, 0:nk, 0:w]
                nc.gpsimd.tensor_tensor(Wl[:, u % SPL, 0:nk, 0:w], raw[:, u % RAW, 0:nk, 0:w], hi.bitcast(F32),
                                        ALU.subtract).then_inc(weights_lo, 1)

            def add_square(norm, k):
                if not 1 <= k < KC - 1:
                    return
                n = (norm - 1) * (KC - 2) + k
                pool.wait_ge(sq_ready, (norm - 1) * KC + k + 1)
                if n > 1:
                    pool.wait_ge(sq_added, n - 1)
                if k == 1 and norm > 1:
                    pool.wait_ge(sq_summed, norm - 1)
                nc.gpsimd.tensor_tensor(acc, sq[:, 0, :] if k == 1 else acc, sq[:, k % 2, :], ALU.add).then_inc(sq_added, 1)

            def rest_ffn(layer):
                with pool.Fori(0, FC // 2) as it:
                    for j in range(4):
                        rest(U_GU[layer] + j, it=it, stride=4)
                for n in range(3 * KC):
                    rest(U_DN[layer] + n, nk=DOWN[n % 3])
                    m, r = divmod(n - 4, 3)
                    if r == 0:
                        add_square(2 * layer + 2, m)

            for u in range(N_IN0):
                rest(u, w=UN0[u][3])
            for n in range(KC):
                rest(U_OUT0 + n)
                add_square(1, n - 2)
            add_square(1, KC - 2)
            rest_ffn(0)
            for n in range(N_IN1 + KC):
                rest(U_IN1 + n)
                if n >= N_IN1:
                    add_square(3, n - N_IN1 - 2)
            add_square(3, KC - 2)
            rest_ffn(1)

        @block.tensor
        def _(pe):
            pe.wait_ge(ident_loaded, 16)
            for b, n in enumerate((PR_A, 4 * CONV_W, 4 * FC, 4 * FC)):
                pe.wait_ge(params_loaded[b], 16 * (7, 1, 2, 2)[b])
                nc.tensor.transpose(bank[:, b, 0:n], pst[0:n, b, :], ident[0:n, 0:n]).then_inc(turned, 1)
            for k in range(KC):
                pe.wait_ge(x_scaled, QT // 2)
                pe.wait_ge(x_scaled_act, QT // 2)
                if k >= 4:
                    pe.wait_ge(h_ready, k - 3)
                for t in range(QT):
                    mm = nc.tensor.transpose(bank[:, 4 + k % 4, t * P:(t + 1) * P], xn[:, t, k * P:(k + 1) * P], ident[:])
                mm.then_inc(xn_turned, 1)

            def turn_input(k):
                pe.wait_ge(h_ready, min(KC, k + 5))
                if k >= 4:
                    pe.wait_ge(xt_ready, k - 3)
                for t in range(QT):
                    mm = nc.tensor.transpose(bank[:, 4 + k % 4, t * P:(t + 1) * P], xin[:, t, k * P:(k + 1) * P], ident[:])
                mm.then_inc(turned, 1)

            def stats(norm):
                pe.wait_ge(sq_added, norm * (KC - 2))
                nc.tensor.matmul(bank[:, 7, :], ones[:], acc, start=True, stop=False)
                pe.wait_ge(sq_ready, norm * KC)
                nc.tensor.matmul(bank[:, 7, :], ones[:], sq[:, (KC - 1) % 2, :], start=False, stop=True).then_inc(sq_summed, 1)

            pe.wait_ge(memsets, N_MEMSETS)

            def bias_row(v):
                c0, c1 = ((0, 12), (12, 20))[v]
                pe.wait_ge(consts_loaded, 32)
                pe.wait_ge(xt_ready, KC)
                if v == 1:
                    pe.wait_ge(row_copied, 1)
                nc.tensor.matmul(bank[0:c1 - c0, 4, :], tab[:, c0:c1], onehot[:, v, 0:S], start=True, stop=True)
                nc.tensor.matmul(bank[0:c1 - c0, 5, 0:FROW - S], tab[:, c0:c1], onehot[:, v, S:FROW], start=True,
                                 stop=True).then_inc(row_made, 1)

            def begin(o, it=0):
                if o >= NACC:
                    wait_read(pe, o - NACC, it)
                return bank[:, o % NACC, :]

            def product(dst, u, nk, oh, ol, k0=0, first=True, last=True, ready=h_ready, hwait=None, it=0, stride=0,
                        kw=0, done=True):
                pe.wait_ge(weights_lo, u + 1 + it * stride)
                s = u % SPL
                for k in range(nk):
                    if hwait is not None:
                        pe.wait_ge(ready, hwait + k0 + k + 1)
                    a = first and k == 0
                    z = last and k == nk - 1
                    nc.tensor.matmul(dst, Wh[:, s, kw + k, :], oh[:, k0 + k, :], start=a, stop=False)
                    nc.tensor.matmul(dst, Wh[:, s, kw + k, :], ol[:, k0 + k, :], start=False, stop=False)
                    mm = nc.tensor.matmul(dst, Wl[:, s, kw + k, :], oh[:, k0 + k, :], start=False, stop=z)
                if done:
                    mm.then_inc(unit_done, 1)

            def turn_values(v, stage):
                pe.wait_ge(staged_at(v)[0], staged_at(v)[1])
                if v >= 2:
                    pe.wait_ge(v_placed, v - 1)
                for t in range(QT):
                    mm = nc.tensor.transpose(bank[:, 4 + v % 2, t * P:(t + 1) * P], stage[:, v % 2, t * P:(t + 1) * P], ident[:])
                mm.then_inc(v_turned, 1)

            def hidden(kv):
                pe.wait_ge(v_placed, len(TURN0))
                pe.wait_ge(phi_loaded, 64 * (kv + 1))
                pe.wait_ge(ft_ready, kv + 1)
                for hh in range(2):
                    for l in range(NPAIR):
                        mm = nc.tensor.matmul(bank[:, 5 + kv, hh * P:hh * P + 2 * NCMP],
                                              phw[:, kv, l, hh * P:(hh + 1) * P], FT[:, kv, l, :],
                                              start=l == 0, stop=l == NPAIR - 1)
                mm.then_inc(hid_made, 1)

            def conv_mean():
                for c in range(4):
                    pe.wait_ge(conv_done, c + 1)
                    mm = nc.tensor.matmul(bank[:, 4, :], ones[:], CA[:, c, :], start=c == 0, stop=c == 3)
                mm.then_inc(ln_mean, 1)

            def compressed():
                pe.wait_ge(small_loaded, 64)
                pe.wait_ge(hid_ready, 2)
                for g in range(2):
                    for hh in range(2):
                        nc.tensor.matmul(bank[HD * g:HD * g + HD, 5, 0:NCMP], w2s[:, 0, hh, :],
                                         hid[:, 0, hh, NCMP * g:NCMP * g + NCMP], start=hh == 0, stop=hh == 1)
                for g in range(2):
                    for q in range(4):
                        for hh in range(2):
                            mm = nc.tensor.matmul(bank[32 * q:32 * q + NCMP, 6, 256 * g + HD * q:256 * g + HD * q + HD],
                                                  hid[:, 1, hh, NCMP * g:NCMP * g + NCMP], w2s[:, 1, hh, :],
                                                  start=hh == 0, stop=hh == 1)
                mm.then_inc(cmp_made, 1)

            def conv_variance():
                for c in range(4):
                    pe.wait_ge(ln_sq, c + 1)
                    nc.tensor.matmul(bank[:, 7, :], ones[:], sq2(c), start=c == 0, stop=c == 3).then_inc(ln_var, 1)

            pe.wait_ge(param_copied, 4)
            for n, (kind, idx, col, w) in enumerate(UN0):
                dst = begin(O_IN0 + n)
                product(dst, U_IN0 + n, KC, Hh, Hl, hwait=0 if n == 0 else None)
                if n < 2:
                    for k in range(4 * n, 4 * n + 4):
                        turn_input(k)
                if 2 <= n < 4:
                    bias_row(n - 2)
                if n - 1 in TURN0:
                    turn_values(TURN0.index(n - 1), tm)
                if n in HIDDEN_AFTER:
                    hidden(HIDDEN_AFTER.index(n))
                if n == LN_AFTER:
                    conv_mean()
                    compressed()
                    conv_variance()

            def first_half(layer, n):
                if layer == 0:
                    pe.wait_ge(cc_ready, 4)
                    k0 = 4
                else:
                    pe.wait_ge(scores_read, use[1, "ct", (QT - 1, 0)] + 1)
                    k0 = 0
                product(begin((O_OUT0, O_OUT1)[layer] + n), (U_OUT0, U_OUT1)[layer] + n, 4, Hh, Hl, k0=k0, kw=k0, last=False,
                        done=False)

            def attention(layer):
                J = JOBS * layer
                base = QT * layer
                Tm = (tm, tn)[layer]
                for s in range(STEPS):
                    i, r = divmod(s, PER)
                    j = s - LAG_T
                    if (layer, j) in turns:
                        v = turns[layer, j]
                        if map_of(layer, j) == 1:
                            pe.wait_ge(mixed, pairs(j))
                        else:
                            pe.wait_ge(probs_ready, J + j + 1)
                        if v == 1:
                            pe.wait_ge(ln_std, 1)
                        if v >= 2:
                            pe.wait_ge(pt_copied[v % 2], v // 2)
                        for t in range(j // PER + 1):
                            mm = nc.tensor.transpose(bank[:, 6 + v % 2, t * P:(t + 1) * P], Pb[:, j % 4, t * P:(t + 1) * P],
                                                     ident[:])
                        mm.then_inc(probs_turned, 1)
                    if s < JOBS:
                        q, k, _, _, _, _ = job(layer, s)
                        n = use[layer, s]
                        if n >= 2:
                            pe.wait_ge(scores_read, n - 1)
                        nc.tensor.matmul(bank[:, 4 + n % 2, 0:k.shape[1]], q, k, start=True, stop=True).then_inc(qk_done, 1)
                    if layer == 0 and r == STEP_CMP["scores"] and i < QT:
                        if i == 0:
                            for o in range(O_IN0 + N_IN0 - 2, O_IN0 + N_IN0):
                                wait_read(pe, o)
                        for c in range(4):
                            mm = nc.tensor.matmul(bank[:, 2, 64 * c:64 * c + 64], Q0[:, c, P * i:P * (i + 1)],
                                                  kcT[:].rearrange("p g n -> p (g n)"), start=True, stop=True)
                        mm.then_inc(sc_made, 1)
                    if s == LAST_CT[layer]:
                        pe.wait_ge(read_a, base + QT)
                        first_half(layer, 0)
                    for key in CT[layer].get(s, []):
                        n = use[layer, "ct", key]
                        if layer == 0:
                            pe.wait_ge(combined_b, 1 + key[0])
                        elif key[1] == 0:
                            pe.wait_ge(combined_a, QT + 1 + key[0])
                        else:
                            pe.wait_ge(read_b, QT + 1 + key[0])
                        pe.wait_ge(scores_read, n - 1)
                        for c in range(4):
                            mm = nc.tensor.transpose(bank[:, 4 + n % 2, c * P:(c + 1) * P],
                                                     Tm[:, ct_tile[key[1]], c * P:(c + 1) * P], ident[:])
                        mm.then_inc(ct_turned, 1)
                    j = s - LAG_V
                    if (layer, j) in turns:
                        p = turns[layer, j]
                        if j >= PER and j % PER in (layer, PER // 2):
                            pe.wait_ge((read_a, read_b)[j % PER // 8], base + j // PER)
                        pe.wait_ge(pt_copied[p % 2], p // 2 + 1)
                        _, _, _, values, o, _ = job(layer, j)
                        for t, vt in enumerate(values):
                            mm = nc.tensor.matmul(o, PTs[:, p % 2, t * P:(t + 1) * P], vt, start=t == 0,
                                                  stop=t == len(values) - 1)
                        mm.then_inc(pv_done, 1)
                    if layer == 0 and r == STEP_CMP["turn"] and i < QT:
                        pe.wait_ge(pc_ready, i + 1)
                        for g in range(2):
                            mm = nc.tensor.transpose(bank[:, 3, g * P:(g + 1) * P], Pc[:, 4 * g:4 * g + 4, :].rearrange("p h n -> p (h n)"),
                                                     ident[:])
                        mm.then_inc(pc_turned, 1)
                    if layer == 0 and r == STEP_CMP["values"] and i < QT:
                        pe.wait_ge(pc_copied, i + 1)
                        if i > 0:
                            pe.wait_ge(read_a, i)
                        for g in range(2):
                            mm = nc.tensor.matmul(bank[:, 2 + g, 2 * P:4 * P], PcT[:, g, :], vbd[:, g, :], start=True, stop=True)
                        mm.then_inc(oc_made, 1)

            ct_tile = [0, 2]

            def project_out(layer, u0, o0, norm):
                first_half(layer, 1)
                pe.wait_ge(scores_read, use[layer, "ct", (QT - 1, layer)] + 1)
                k0 = 4 * layer
                for n in range(KC):
                    if n < 2:
                        product(bank[:, (o0 + n) % NACC, :], u0 + n, 4, Hh, Hl, k0=k0, kw=k0, first=False)
                    else:
                        product(begin(o0 + n), u0 + n, KC, Hh, Hl)
                stats(norm)

            def ffn(layer):
                norm = 2 * layer + 1
                with pe.Fori(0, FC // 2) as it:
                    for j in range(4):
                        dst = bank[:, (O_GU[layer] + j) % NACC, :]
                        pe.wait_ge(tile_read[(O_GU[layer] + j) % NACC], reads(O_GU[layer] + j) - 1 + it)
                        product(dst, U_GU[layer] + j, KC, Hh, Hl, hwait=KC * norm if j == 0 else None, it=it, stride=4)
                for n in range(KC):
                    dst = begin(O_DN[layer] + n)
                    k = 0
                    for r in range(3):
                        product(dst, U_DN[layer] + 3 * n + r, DOWN[r], Ah, Al, k0=k, first=r == 0, last=r == 2,
                                ready=a_ready, hwait=FC * layer if n == 0 else None)
                        k += DOWN[r]
                if layer == 1:
                    stats(norm + 1)

            pe.wait_ge(cmp_ready, 1)
            pe.wait_ge(ln_centered, 4)
            for o in range(O_IN0 + N_IN0 - 6, O_IN0 + N_IN0 - 2):
                wait_read(pe, o)
            attention(0)
            project_out(0, U_OUT0, O_OUT0, 1)
            ffn(0)
            for n, (kind, idx, col, w) in enumerate(UN1):
                dst = begin(O_IN1 + n)
                product(dst, U_IN1 + n, KC, Hh, Hl, hwait=2 * KC if n == 0 else None)
                if n == 0:
                    stats(2)
                if n - 1 in TURN1:
                    turn_values(len(TURN0) + TURN1.index(n - 1), tn)
            pe.wait_ge(v_placed, len(TURN0) + len(TURN1))
            for o in range(O_IN1 + N_IN1 - NACC, O_IN1 + N_IN1):
                wait_read(pe, o)
            attention(1)
            project_out(1, U_OUT1, O_OUT1, 3)
            ffn(1)
            for k in range(KC):
                pe.wait_ge(fin_ready, k + 1)
                if k >= 2:
                    pe.wait_ge(fin_copied, k - 1)
                for t in range(QT):
                    mm = nc.tensor.transpose(bank[:, 4 + k % 2, t * P:(t + 1) * P], hf[:, k % 2, t * P:(t + 1) * P], ident[:])
                mm.then_inc(fin_turned, 1)

        @block.scalar
        def _(act):
            def round_unit(u, it=0, stride=0):
                if u >= U_END:
                    return
                nk, w = 8, P
                for d in U_DN:
                    if d <= u < d + 3 * KC:
                        nk = DOWN[(u - d) % 3]
                if u < N_IN0:
                    w = UN0[u][3]
                if u >= SPL:
                    act.wait_ge(unit_done, u - SPL + 1 + it * stride)
                act.wait_ge(raw_loaded[u % RAW], raw_count(u) + it * (stride // RAW * 16))
                nc.scalar.copy(Wh[:, u % SPL, 0:nk, 0:w], raw[:, u % RAW, 0:nk, 0:w]).then_inc(weights_hi, 1)

            def square(norm, k):
                act.wait_ge(xt_ready, norm * KC + k + 1)
                if k >= 2:
                    act.wait_ge(sq_added, (norm - 1) * (KC - 2) + max(1, k - 2))
                elif norm > 1:
                    act.wait_ge(sq_summed, norm - 1)
                nc.scalar.activation(sq[:, k % 2, :], XT[:, k, :], ACT.Square).then_inc(sq_ready, 1)

            def norm_root(norm):
                act.wait_ge(sq_summed, norm)
                nc.scalar.activation(rs[:], bank[:, 7, :], ACT.Sqrt, bias=eps[:, 0:1], scale=1.0 / D).then_inc(rms_ready, 1)

            def gain_round(norm, k):
                act.wait_ge(xt_ready, KC * norm + k + 1)
                nc.scalar.activation(Hh[:, k, :], XT[:, k, :], ACT.Identity, scale=gain(norm, k)).then_inc(hh_ready, 1)

            act.dma_start(ident[:], c_ident).then_inc(ident_loaded, 16)
            for u in range(2):
                _, _, col, w = UN0[u]
                act.dma_start(raw[:, u, :, 0:w], w_in0[:, :, col:col + w]).then_inc(raw_loaded[u], 16)
            act.wait_ge(memsets, 1)
            nc.scalar.activation(lamb[:, 7:8], eps[:, 0:1], ACT.Sqrt)
            for t in range(QT):
                act.wait_ge(x_loaded[t], 16)
                nc.scalar.activation(xn[:, t, :], xin[:, t, :], ACT.Square, accum_out=xs[:, 0, t:t + 1]).then_inc(x_squared, 1)
            act.wait_ge(memsets, N_MEMSETS)
            act.wait_ge(x_squared, QT)
            nc.scalar.activation(xs[:, 1, :], xs[:, 0, :], ACT.Sqrt, bias=eps[:, 0:1], scale=1.0 / D).then_inc(x_std, 1)
            act.wait_ge(x_inverse, 1)
            for t in range(QT // 2, QT):
                nc.scalar.mul(xn[:, t, :], xin[:, t, :], xs[:, 1, t:t + 1]).then_inc(x_scaled_act, 1)
            round_unit(0)
            round_unit(1)
            act.wait_ge(param_copied, 1)
            for k in range(KC):
                act.wait_ge(xn_turned, k + 1)
                nc.scalar.activation(Hh[:, k, :], bank[:, 4 + k % 4, :], ACT.Identity,
                                     scale=prm[:, PR_MIX + k:PR_MIX + k + 1]).then_inc(hh_ready, 1)
            def bias_row(v):
                act.wait_ge(row_made, v + 1)
                n = (12, 8)[v]
                nc.scalar.copy(brow[0:n, v, 0:S], bank[0:n, 4, :])
                nc.scalar.copy(brow[0:n, v, S:FROW], bank[0:n, 5, 0:FROW - S]).then_inc(row_copied, 1)

            def place0(v):
                act.wait_ge(v_turned, v + 1)
                src = bank[:, 4 + v % 2, :]
                if v < 2:
                    nc.scalar.copy(V0[:, v].rearrange("p t c -> p (t c)"), src).then_inc(v_placed, 1)
                else:
                    nc.scalar.activation(gate[:], src.rearrange("p (t c) -> p t c", t=QT)[:, :, 0:24],
                                         ACT.Sigmoid).then_inc(v_placed, 1)

            def conv_squares():
                for c in range(4):
                    act.wait_ge(ln_centered, c + 1)
                    if c >= 2:
                        act.wait_ge(ln_var, c - 1)
                    nc.scalar.activation(sq2(c), CA[:, c, :], ACT.Square).then_inc(ln_sq, 1)

            def hidden(kv):
                act.wait_ge(hid_made, kv + 1)
                nc.scalar.activation(hid[:, kv], bank[:, 5 + kv, 0:2 * P].rearrange("p (a n) -> p a n", a=2)[:, :, 0:2 * NCMP],
                                     ACT.Silu).then_inc(hid_ready, 1)

            def compressed():
                act.wait_ge(cmp_made, 1)
                for g in range(2):
                    half = slice(HD * g, HD * g + HD)
                    nc.scalar.copy(kcT[half, g, 0:NCMP], bank[half, 5, 0:NCMP])
                for g in range(2):
                    for q in range(4):
                        last = nc.scalar.copy(vbd[32 * q:32 * q + NCMP, g, HD * q:HD * q + HD],
                                              bank[32 * q:32 * q + NCMP, 6, 256 * g + HD * q:256 * g + HD * q + HD])
                last.then_inc(cmp_ready, 1)

            for n, (kind, idx, col, w) in enumerate(UN0):
                o = O_IN0 + n
                src = bank[:, o % NACC, :]
                free = tile_read[o % NACC]
                if n < N_IN0 - 1:
                    round_unit(U_IN0 + n + SPL)
                else:
                    act.wait_ge(unit_done, U_IN0 + N_IN0)
                if kind == "g":
                    if idx >= 2:
                        wait_read(act, o - 3)
                    nc.scalar.activation(yb[:, idx % 2, :], src, ACT.Sigmoid).then_inc(free, 1)
                elif kind == "kc":
                    for g in range(2):
                        half = slice(HD * g, HD * g + HD)
                        nc.scalar.copy(KK[0:HD, idx, g, :], bank[half, o % NACC, :])
                        last = nc.scalar.copy(KK[HD:P, idx, g, 0:S - 1], bank[half, o % NACC, 1:S])
                    last.then_inc(free, 1)
                elif kind == "q":
                    nc.scalar.mul(Q0[:, idx, :], src, HD ** -0.5).then_inc(free, 1)
                elif kind == "k":
                    nc.scalar.copy(K0[:, idx, :], src).then_inc(free, 1)
                elif kind in ("v", "gate"):
                    v = TURN0.index(n)
                    if v >= 2:
                        act.wait_ge(v_turned, v - 1)
                    nc.scalar.copy(tm[:, v % 2, :], src).then_inc(free, 1)
                    if v >= 1:
                        place0(v - 1)
                if 2 <= n < 4:
                    bias_row(n - 2)
                if n == TURN0[-1] + 1:
                    place0(len(TURN0) - 1)
                if n in HIDDEN_AFTER:
                    hidden(HIDDEN_AFTER.index(n))
                if n == LN_AFTER:
                    conv_squares()
                    compressed()
                    act.wait_ge(ln_var, 4)
                    nc.scalar.activation(tm[:, 2, :], bank[:, 7, :], ACT.Sqrt, bias=eps[:, 0:1], scale=1.0 / 512).then_inc(ln_std, 1)
                if n == LN_AFTER + 1:
                    for c in range(4):
                        act.wait_ge(ln_scaled, c + 1)
                        nc.scalar.activation(CA[:, c, :], CA[:, c, :], ACT.Silu, bias=prm[:, PR_LNB + c:PR_LNB + c + 1]).then_inc(u_ready, 1)
                    nc.scalar.activation(lamb[:, 7:8], eps[:, 0:1], ACT.Exp)
            round_unit(U_IN0 + N_IN0 + 1)

            def conv_round(c):
                act.wait_ge(u_ready, c + 1)
                act.wait_ge(unit_done, U_IN0 + N_IN0)
                nc.scalar.copy(Hh[:, 4 + c, :], CA[:, c, :]).then_inc(cc_hi, 1)

            def attention(layer):
                J = JOBS * layer
                for s in range(STEPS):
                    i, r = divmod(s, PER)
                    v = turns.get((layer, s - LAG_T), 0)
                    if v % 2 == 1:
                        w = P * ((s - LAG_T) // PER + 1)
                        act.wait_ge(probs_turned, v + 1)
                        if v >= 2:
                            act.wait_ge(pv_done, v - 1)
                        nc.scalar.copy(PTs[:, 1, 0:w], bank[:, 7, 0:w]).then_inc(pt_copied[1], 1)
                    if s < JOBS:
                        L = job(layer, s)[5]
                        w = P * (s // PER + 1)
                        act.wait_ge(scores_read, use[layer, s] + 1)
                        if s >= 4 and map_of(layer, s - 4) == 0:
                            act.wait_ge(mixed, pairs(s - 4))
                        elif J + s >= 4:
                            act.wait_ge(probs_turned, turns[(layer, s - 4) if s >= 4 else (0, JOBS - 4 + s)] + 1)
                        nc.scalar.activation(Pb[:, s % 4, 0:w], S2[:, s % 2, 0:w], ACT.Exp, bias=nmx[:, s % 2:s % 2 + 1],
                                             scale=-1.0, accum_out=L).then_inc(probs_ready, 1)
                    for key in CT[layer].get(s, []):
                        n = use[layer, "ct", key]
                        if (layer, key[1]) == (1, 0):
                            act.wait_ge(gain_ready, 1)
                        act.wait_ge(ct_turned, CTN[layer, "ct", key] + 1)
                        c0 = 4 * key[1]
                        nc.scalar.activation(Hh[:, c0:c0 + 4, P * key[0]:P * (key[0] + 1)],
                                             bank[:, 4 + n % 2, :].rearrange("p (c t) -> p c t", c=4), ACT.Identity,
                                             scale=dng[:, 1:2] if (layer, key[1]) == (1, 0) else 1.0).then_inc(ct_hi, 1)
                    if layer == 0 and r == STEP_CMP["exp"] and i < QT:
                        act.wait_ge(sc_shifted, i + 1)
                        nc.scalar.activation(Pc[:].rearrange("p h n -> p (h n)"), Sm[:].rearrange("p h n -> p (h n)"),
                                             ACT.Exp).then_inc(pc_ready, 1)
                    if layer == 0 and s in STEP_U:
                        conv_round(STEP_U[s])
                    if layer == 1 and s >= STEP_ROOT and (s - STEP_ROOT) % PER == 0:
                        n = (s - STEP_ROOT) // PER
                        act.wait_ge(o_squared, n + 1)
                        nc.scalar.activation(Rs[:, 20:24], Rs[:, 16:20], ACT.Sqrt, bias=eps[:, 0:1],
                                             scale=1.0 / (2 * HD)).then_inc(o_rms, 1)

            def project_out(u0, norm):
                for n in range(KC):
                    round_unit(u0 + n + SPL)
                    square(norm, n)
                for k in range(KC):
                    gain_round(norm, k)
                norm_root(norm)

            def ffn(layer):
                u0, o0 = U_GU[layer], O_GU[layer]
                with act.Fori(0, FC // 2) as it:
                    for q in range(2):
                        u, o, m = u0 + 2 * q, o0 + 2 * q, FC * layer + q
                        cols = prm_ff(layer, it, q)
                        round_unit(u + SPL, it, 4)
                        act.wait_ge(tile_read[o % NACC], reads(o) + it)
                        nc.scalar.activation(yb[:, q, :], hf[:, q, :], ACT.Identity, bias=cols[3],
                                             scale=cols[2]).then_inc(y_base, 1)
                        act.wait_ge(y_conv, m + 1 + it * 2)
                        nc.scalar.activation(yb[:, q, :], yb[:, q, :], ACT.Gelu).then_inc(y_gelu, 1)
                        round_unit(u + 1 + SPL, it, 4)
                        act.wait_ge(prod, m + 1 + it * 2)
                        nc.scalar.copy(one(Ah, it, q), ab[:, q, :]).then_inc(ah_ready, 1)
                norm = 2 * layer + 2
                for n in range(KC):
                    for r in range(3):
                        round_unit(U_DN[layer] + 3 * n + r + SPL)
                    square(norm, n)
                    if layer == 0:
                        gain_round(norm, n)
                norm_root(norm)

            attention(0)
            project_out(U_OUT0, 1)
            ffn(0)
            def place1(v):
                v += len(TURN0)
                act.wait_ge(v_turned, v + 1)
                w = v - len(TURN0)
                dst = (Vc, Vd)[w // 4][:, :, P * (w % 4):P * (w % 4 + 1)]
                nc.scalar.copy(dst, bank[:, 4 + v % 2, :].rearrange("p (t c) -> p t c", t=QT)).then_inc(v_placed, 1)

            act.wait_ge(lam_dots, 1)
            nc.scalar.activation(lamb[:, 2:4], lamb[:, 0:2], ACT.Exp).then_inc(lam_exps, 1)
            for n in range(N_IN1):
                round_unit(U_IN1 + n + SPL)
                if n - 1 in TURN1:
                    place1(TURN1.index(n - 1))
            attention(1)
            project_out(U_OUT1, 3)
            ffn(1)

        @block.vector
        def _(dve):
            count = [0]

            def step(ins):
                count[0] += 1
                ins.then_inc(dstep, 1)
                dve.wait_ge(dstep, count[0])

            def rest_of_gain(norm, k):
                dve.wait_ge(hh_ready, norm * KC + k + 1)
                nc.vector.scalar_tensor_tensor(out=Hl[:, k, :], in0=XT[:, k, :], scalar=gain(norm, k),
                                               in1=Hh[:, k, :].bitcast(F32), op0=ALU.mult,
                                               op1=ALU.subtract).then_inc(h_ready, 1)

            def inverse_rms(norm):
                dve.wait_ge(rms_ready, norm)
                step(nc.vector.reciprocal(rs[:], rs[:]))

            c0 = 0
            for b, n in enumerate((PR_A, 4 * CONV_W, 4 * FC, 4 * FC)):
                dve.wait_ge(turned, b + 1)
                nc.vector.tensor_copy(prm[:, c0:c0 + n], bank[:, b, 0:n]).then_inc(param_copied, 1)
                c0 += n
            dve.wait_ge(x_std, 1)
            nc.vector.reciprocal(xs[:, 1, :], xs[:, 1, :]).then_inc(x_inverse, 1)
            dve.wait_ge(x_inverse, 1)
            for t in range(QT // 2):
                nc.vector.tensor_scalar(xn[:, t, :], xin[:, t, :], xs[:, 1, t:t + 1], None, ALU.mult).then_inc(x_scaled, 1)
            dve.wait_ge(param_copied, 4)
            for k in range(KC):
                dve.wait_ge(hh_ready, k + 1)
                nc.vector.scalar_tensor_tensor(out=Hl[:, k, :], in0=bank[:, 4 + k % 4, :], scalar=prm[:, PR_MIX + k:PR_MIX + k + 1],
                                               in1=Hh[:, k, :].bitcast(F32), op0=ALU.mult,
                                               op1=ALU.subtract).then_inc(h_ready, 1)
            for k in range(KC):
                dve.wait_ge(turned, 4 + k + 1)
                nc.vector.tensor_copy(XT[:, k, :], bank[:, 4 + k % 4, :]).then_inc(xt_ready, 1)

            def glu(c):
                wait_read(dve, O_IN0 + 2 * c)
                o = O_IN0 + 2 * c + 1
                dve.wait_ge(unit_done, U_IN0 + 2 * c + 2)
                nc.vector.tensor_tensor(Uc[:, c, PAD:PAD + S], yb[:, c % 2, :], bank[:, o % NACC, :],
                                        ALU.mult).then_inc(tile_read[o % NACC], 1)

            last_tap = {}

            def tap(c):
                t, n = last_tap.get(c, (-1, 0))
                t += 1
                w = PR_DWW + c
                if t == 0:
                    wait_read(dve, O_IN0 + 2 * c + 1)
                    ins = nc.vector.tensor_scalar(CA[:, c, :], Uc[:, c, 0:S], prm[:, w:w + 1],
                                                  prm[:, PR_DWB + c:PR_DWB + c + 1], ALU.mult, ALU.add)
                else:
                    dve.wait_ge(dstep, n)
                    ins = nc.vector.scalar_tensor_tensor(out=CA[:, c, :], in0=Uc[:, c, t:t + S],
                                                         scalar=prm[:, w + 4 * t:w + 4 * t + 1], in1=CA[:, c, :],
                                                         op0=ALU.mult, op1=ALU.add)
                if t == CONV_W - 1:
                    ins.then_inc(conv_done, 1)
                    n = 0
                else:
                    count[0] += 1
                    n = count[0]
                    ins.then_inc(dstep, 1)
                last_tap[c] = (t, n)

            def flat(kv):
                wait_read(dve, O_IN0 + 8 + kv)
                for g in range(2):
                    src = spread(KK[:, kv, g, 0:1], (2, NPAIR), (16, NCMP))
                    pos = spread(prm[:, PR_POS + NPAIR * kv:PR_POS + NPAIR * kv + 1], (1, NPAIR), (0, NCMP))
                    ins = nc.vector.tensor_tensor(FT[:, kv, :, NCMP * g:NCMP * (g + 1)], src, pos, ALU.add)
                ins.then_inc(ft_ready, 1)

            dve.wait_ge(memsets, N_MEMSETS)
            glu(0)
            for t in range(14):
                tap(0)
            glu(1)
            for t in range(8):
                tap(0)
                tap(1)
            glu(2)
            for t in range(9):
                tap(0)
                tap(1)
            glu(3)
            for t in range(14):
                tap(1)
                tap(2)
            flat(0)
            flat(1)
            for t in range(17):
                tap(2)
                tap(3)
            for t in range(14):
                tap(3)
            dve.wait_ge(ln_mean, 1)
            for c in range(4):
                nc.vector.scalar_tensor_tensor(out=CA[:, c, :], in0=bank[:, 4, :], scalar=-1.0 / 512, in1=CA[:, c, :],
                                               op0=ALU.mult, op1=ALU.add).then_inc(ln_centered, 1)
            dve.wait_ge(ln_std, 1)
            dve.wait_ge(ln_sq, 4)
            step(nc.vector.reciprocal(tm[:, 2, :], tm[:, 2, :]))
            for c in range(4):
                nc.vector.scalar_tensor_tensor(out=CA[:, c, :], in0=CA[:, c, :], scalar=prm[:, PR_LNG + c:PR_LNG + c + 1],
                                               in1=tm[:, 2, :], op0=ALU.mult, op1=ALU.mult).then_inc(ln_scaled, 1)

            def conv_rest(c):
                dve.wait_ge(cc_hi, c + 1)
                nc.vector.tensor_tensor(Hl[:, 4 + c, :], CA[:, c, :], Hh[:, 4 + c, :].bitcast(F32),
                                        ALU.subtract).then_inc(cc_ready, 1)

            def mark(ins):
                count[0] += 1
                ins.then_inc(dstep, 1)

            def settled():
                dve.wait_ge(dstep, count[0])

            def combine0(i, r):
                if r == 8:
                    dve.wait_ge(probs_ready, PER * i + 8)
                    mark(nc.vector.reciprocal(Rs[:, 0:16], Ls[:, i % 2, 0:16]))
                elif r == 9:
                    settled()
                    mark(nc.vector.tensor_tensor(Cs[:, 0:16].rearrange("p (b h) -> p b h", b=2),
                                                 Rs[:, 0:16].rearrange("p (b h) -> p b h", b=2),
                                                 spread(gate[:, i, 0:1], (1, 2), (3, 8)), ALU.mult))
                elif r == 10:
                    settled()
                    mark(nc.vector.tensor_scalar(Cs[:, 0:8], Cs[:, 0:8], cmask[:, i, 32:33], None, ALU.mult))
                elif r == 11:
                    dve.wait_ge(oc_made, i + 1)
                    settled()
                    oc = spread(bank[:, 2, 2 * P:2 * P + 1], (S, 2), (HD, 4), (1, HD))
                    nc.vector.tensor_tensor(tm[:, 0, :].rearrange("p (g h d) -> p g h d", g=2, h=4), oc,
                                            spread(Cs[:, 0:1], (4, 2), (1, 4), (0, HD)), ALU.mult)
                elif r in (12, 20):
                    half = (r - 12) // 8
                    settled()
                    dve.wait_ge(pv_done, PER * i + 8 * half + 8)
                    n = 8 + 8 * half
                    nc.vector.tensor_tensor(tm[:, 1, :].rearrange("p (h d) -> p h d", h=8),
                                            bank[:, half, :].rearrange("p (h d) -> p h d", h=8),
                                            spread(Cs[:, n:n + 1], (1, 8), (0, HD)), ALU.mult).then_inc((read_a, read_b)[half], 1)
                elif r in (13, 21):
                    half = (r - 13) // 8
                    dve.wait_ge((read_a, read_b)[half], i + 1)
                    nc.vector.tensor_tensor(tm[:, 0, :], tm[:, 0, :], tm[:, 1, :],
                                            ALU.add).then_inc((combined_a, combined_b)[half], 1)
                elif r == 17:
                    dve.wait_ge(probs_ready, PER * (i + 1))
                    mark(nc.vector.reciprocal(Rs[:, 16:24], Ls[:, i % 2, 16:24]))
                elif r == 18:
                    settled()
                    dve.wait_ge(combined_a, i + 1)
                    mark(nc.vector.tensor_tensor(Cs[:, 16:24], Rs[:, 16:24], spread(gate[:, i, 2:3], (3, 8)), ALU.mult))

            def mix(j):
                i, r = divmod(j, PER)
                h, w = r // 2, P * (i + 1)
                dve.wait_ge(probs_ready, JOBS + j + 1)
                step(nc.vector.reciprocal(Rs[:, 4 + h:5 + h], Ls[:, i % 2, 4 + h:5 + h]))
                step(nc.vector.scalar_tensor_tensor(out=Cs[:, h:h + 1], in0=Rs[:, 4 + h:5 + h], scalar=lamb[:, 4:5],
                                                    in1=Ls[:, i % 2, h:h + 1], op0=ALU.mult, op1=ALU.mult))
                nc.vector.scalar_tensor_tensor(out=Pb[:, j % 4, 0:w], in0=Pb[:, j % 4, 0:w], scalar=Cs[:, h:h + 1],
                                               in1=Pb[:, (j - 1) % 4, 0:w], op0=ALU.mult, op1=ALU.add).then_inc(mixed, 1)

            def combine1(i, r):
                heads = lambda t: t.rearrange("p (h d) -> p h d", h=4)
                if r == 9:
                    dve.wait_ge(probs_ready, JOBS + PER * i + 8)
                    mark(nc.vector.reciprocal(Rs[:, 0:4], Ls[:, i % 2, 0:4]))
                elif r == 12:
                    settled()
                    dve.wait_ge(pv_done, turns[1, PER * i + 7] + 1)
                    nc.vector.tensor_tensor(heads(tn[:, 0, :]), heads(bank[:, 0, :]),
                                            spread(Rs[:, 0:1], (1, 4), (0, P)), ALU.mult).then_inc(read_a, 1)
                elif r == 13:
                    dve.wait_ge(read_a, QT + i + 1)
                    mark(nc.vector.tensor_tensor(tn[:, 1, :], tn[:, 0, :], tn[:, 0, :], ALU.mult))
                elif r == 14:
                    settled()
                    nc.vector.tensor_reduce(Rs[:, 16:20], heads(tn[:, 1, :]), AXX, ALU.add).then_inc(o_squared, 1)
                elif r == 17:
                    dve.wait_ge(o_rms, i + 1)
                    mark(nc.vector.reciprocal(Rs[:, 20:24], Rs[:, 20:24]))
                elif r == 18:
                    settled()
                    nc.vector.tensor_tensor(heads(tn[:, 0, :]), heads(tn[:, 0, :]),
                                            spread(Rs[:, 20:21], (1, 4), (0, P)), ALU.mult).then_inc(combined_a, 1)
                elif r == 19:
                    dve.wait_ge(probs_ready, JOBS + PER * (i + 1))
                    mark(nc.vector.reciprocal(Rs[:, 8:16], Ls[:, i % 2, 8:16]))
                elif r == 20:
                    settled()
                    dve.wait_ge(pv_done, turns[1, PER * i + PER - 1] + 1)
                    nc.vector.tensor_tensor(tn[:, 2, :].rearrange("p (h d) -> p h d", h=8),
                                            bank[:, 2, :].rearrange("p (h d) -> p h d", h=8),
                                            spread(Rs[:, 8:9], (1, 8), (0, HD)), ALU.mult).then_inc(read_b, 1)

            def attention(layer):
                J = JOBS * layer
                dve.wait_ge(small_loaded, 64)
                dve.wait_ge(strips_loaded, 16 * (layer + 1))
                for s in range(STEPS):
                    i, r = divmod(s, PER)
                    v = turns.get((layer, s - LAG_T), 1)
                    if v % 2 == 0:
                        w = P * ((s - LAG_T) // PER + 1)
                        dve.wait_ge(probs_turned, v + 1)
                        if v >= 2:
                            dve.wait_ge(pv_done, v - 1)
                        nc.vector.tensor_copy(PTs[:, 0, 0:w], bank[:, 6, 0:w]).then_inc(pt_copied[0], 1)
                    if s < JOBS:
                        T = job(layer, s)[2]
                        w = P * (i + 1)
                        n = use[layer, s]
                        dve.wait_ge(qk_done, J + s + 1)
                        if J + s >= 2:
                            dve.wait_ge(probs_ready, J + s - 1)
                        nc.vector.tensor_tensor_reduce(out=S2[:, s % 2, 0:w], in0=bank[:, 4 + n % 2, 0:w], in1=T, scale=-1.0,
                                                       scalar=3.0e38, op0=ALU.add, op1=ALU.min,
                                                       accum_out=nmx[:, s % 2:s % 2 + 1]).then_inc(scores_read, 1)
                    if (layer, s - 1) in turns and map_of(layer, s - 1) == 1:
                        mix(s - 1)
                    for key in CT[layer].get(s, []):
                        n = use[layer, "ct", key]
                        c0 = 4 * key[1]
                        dve.wait_ge(ct_hi, CTN[layer, "ct", key] + 1)
                        ts = slice(P * key[0], P * (key[0] + 1))
                        src = bank[:, 4 + n % 2, :].rearrange("p (c t) -> p c t", c=4)
                        if (layer, key[1]) == (1, 0):
                            nc.vector.scalar_tensor_tensor(out=Hl[:, c0:c0 + 4, ts], in0=src, scalar=dng[:, 1:2],
                                                           in1=Hh[:, c0:c0 + 4, ts].bitcast(F32), op0=ALU.mult,
                                                           op1=ALU.subtract).then_inc(scores_read, 1)
                        else:
                            nc.vector.tensor_tensor(Hl[:, c0:c0 + 4, ts], src, Hh[:, c0:c0 + 4, ts].bitcast(F32),
                                                    ALU.subtract).then_inc(scores_read, 1)
                    if layer == 0 and i < QT:
                        if r == STEP_CMP["shift"]:
                            dve.wait_ge(sc_made, i + 1)
                            mark(nc.vector.tensor_tensor(Sm[:].rearrange("p (g h) n -> p g h n", g=2),
                                                         spread(bank[:, 2, 0:1], (32, 2), (64, 4), (1, 32)),
                                                         spread(cmask[:, i, 0:1], (0, 2), (0, 4), (1, 32)), ALU.add))
                        if r == STEP_CMP["shift"] + 1:
                            settled()
                            mark(nc.vector.tensor_reduce(cmx[:], Sm[:], AXX, ALU.max))
                        if r == STEP_CMP["shift"] + 2:
                            settled()
                            nc.vector.tensor_tensor(Sm[:], Sm[:], spread(cmx[:, 0:1], (1, 8), (0, 32)),
                                                    ALU.subtract).then_inc(sc_shifted, 1)
                        if r == STEP_CMP["sum"]:
                            dve.wait_ge(pc_ready, i + 1)
                            nc.vector.tensor_reduce(Ls[:, i % 2, 0:8], Pc[:], AXX, ALU.add)
                        if r == STEP_CMP["copy"]:
                            dve.wait_ge(pc_turned, i + 1)
                            nc.vector.tensor_copy(PcT[:], bank[:, 3, 0:2 * P].rearrange("p (g t) -> p g t", g=2)).then_inc(pc_copied, 1)
                    for t in (i, i - 1):
                        if 0 <= t < QT:
                            (combine0, combine1)[layer](t, s - PER * t)
                    if layer == 0 and s - 1 in STEP_U:
                        conv_rest(STEP_U[s - 1])

            def project_out(layer, u0, o0, norm):
                for n in range(KC):
                    dve.wait_ge(unit_done, u0 + n + 1)
                    nc.vector.tensor_tensor(XT[:, n, :], XT[:, n, :], bank[:, (o0 + n) % NACC, :], ALU.add).then_inc(xt_ready, 1)
                for k in range(KC):
                    rest_of_gain(norm, k)
                inverse_rms(norm)

            def ffn(layer):
                u0, o0 = U_GU[layer], O_GU[layer]
                base = count[0]
                with dve.Fori(0, FC // 2) as it:
                    for q in range(2):
                        u, o, m = u0 + 2 * q, o0 + 2 * q, FC * layer + q
                        cols = prm_ff(layer, it, q)
                        y, a, gs = yb[:, q, :], ab[:, q, :], hf[:, q, :]
                        gt, up = bank[:, o % NACC, :], bank[:, (o + 1) % NACC, :]
                        dve.wait_ge(unit_done, u + 1 + it * 4)
                        nc.vector.tensor_tensor(gs, gt, rs[:], ALU.mult).then_inc(tile_read[o % NACC], 1)
                        dve.wait_ge(y_base, m + 1 + it * 2)
                        nc.vector.scalar_tensor_tensor(out=y[:, 1:S], in0=gs[:, 0:S - 1], scalar=cols[1], in1=y[:, 1:S],
                                                       op0=ALU.mult, op1=ALU.add).then_inc(dstep, 1)
                        dve.wait_ge(dstep, base + q + 1 + it * 2)
                        nc.vector.scalar_tensor_tensor(out=y[:, 2:S], in0=gs[:, 0:S - 2], scalar=cols[0], in1=y[:, 2:S],
                                                       op0=ALU.mult, op1=ALU.add).then_inc(y_conv, 1)
                        dve.wait_ge(unit_done, u + 2 + it * 4)
                        nc.vector.tensor_tensor(a, up, rs[:], ALU.mult).then_inc(tile_read[(o + 1) % NACC], 1)
                        dve.wait_ge(tile_read[(o + 1) % NACC], reads(o + 1) + it)
                        dve.wait_ge(y_gelu, m + 1 + it * 2)
                        nc.vector.tensor_tensor(a, y, a, ALU.mult).then_inc(prod, 1)
                        dve.wait_ge(ah_ready, m + 1 + it * 2)
                        nc.vector.tensor_tensor(one(Al, it, q), a, one(Ah, it, q).bitcast(F32), ALU.subtract).then_inc(a_ready, 1)
                count[0] = base + FC
                for n in range(KC):
                    dve.wait_ge(unit_done, U_DN[layer] + 3 * n + 3)
                    nc.vector.tensor_tensor(XT[:, n, :], XT[:, n, :], bank[:, (O_DN[layer] + n) % NACC, :],
                                            ALU.add).then_inc(xt_ready, 1)
                    if layer == 0:
                        rest_of_gain(2, n)

            attention(0)
            project_out(0, U_OUT0, O_OUT0, 1)
            ffn(0)
            dve.wait_ge(small_loaded, 64)
            step(nc.vector.tensor_tensor(lamp[:, 0, :], lamp[:, 0, :], lamp[:, 1, :], ALU.mult))
            step(nc.vector.tensor_tensor(lamp[:, 2, :], lamp[:, 2, :], lamp[:, 3, :], ALU.mult))
            nc.vector.tensor_reduce(lamb[:, 0:2], spread(lamp[:, 0, 0:1], (2 * HD, 2), (1, HD)), AXX,
                                    ALU.add).then_inc(lam_dots, 1)
            inverse_rms(2)
            dve.wait_ge(lam_exps, 1)
            step(nc.vector.tensor_tensor(lamb[:, 4:5], lamb[:, 3:4], lamb[:, 2:3], ALU.subtract))
            step(nc.vector.tensor_scalar(lamb[:, 4:5], lamb[:, 4:5], -LAM_INIT, None, ALU.add))
            nc.vector.tensor_scalar(dng[:, 1:2], dng[:, 0:1], 1.0 - LAM_INIT, None, ALU.mult).then_inc(gain_ready, 1)
            for n, (kind, idx, col, w) in enumerate(UN1):
                o = O_IN1 + n
                src = bank[:, o % NACC, :]
                free = tile_read[o % NACC]
                dve.wait_ge(unit_done, U_IN1 + n + 1)
                if kind == "q":
                    nc.vector.scalar_tensor_tensor(out=Q1[:, idx, :], in0=src, scalar=HD ** -0.5, in1=rs[:], op0=ALU.mult,
                                                   op1=ALU.mult).then_inc(free, 1)
                elif kind == "k":
                    nc.vector.tensor_tensor(K1[:, idx, :], src, rs[:], ALU.mult).then_inc(free, 1)
                else:
                    v = len(TURN0) + TURN1.index(n)
                    dve.wait_ge(v_turned, v - 1)
                    nc.vector.tensor_tensor(tn[:, v % 2, :], src, rs[:], ALU.mult).then_inc(free, 1)
            attention(1)
            project_out(1, U_OUT1, O_OUT1, 3)
            ffn(1)
            inverse_rms(4)

            def leave(k):
                dve.wait_ge(fin_turned, k + 1)
                nc.vector.tensor_copy(xout[:, k].rearrange("p t c -> p (t c)"), bank[:, 4 + k % 2, :]).then_inc(fin_copied, 1)

            for k in range(KC):
                nc.vector.scalar_tensor_tensor(out=hf[:, k % 2, :], in0=XT[:, k, :], scalar=prm[:, PR_FIN + k:PR_FIN + k + 1],
                                               in1=rs[:], op0=ALU.mult, op1=ALU.mult).then_inc(fin_ready, 1)
                if k >= 1:
                    leave(k - 1)
            leave(KC - 1)


INPUTS = ["x", "rel_bias_table", "mix_norm_g", "ffn_norm_g", "ffn_w_gate", "ffn_w_up", "ffn_conv_w", "ffn_conv_b",
          "ffn_w_down", "ev_w_in", "ev_w_out", "nsa_phi_pos", "nsa_phi_w1", "nsa_phi_w2", "conv_dw_w", "conv_dw_b",
          "conv_ln_g", "conv_ln_b", "od_w_in", "od_w_out", "diff_lambda", "diff_norm_g", "final_norm_g"]


def shape_constants():
    import numpy as np

    onehot = np.zeros((BUCKETS + 1, 2, FROW), np.float32)
    exact = BUCKETS // 2
    for j in range(FROW):
        d = j - (P - 1)
        if d < 0 or d >= S:
            onehot[BUCKETS, :, j] = NEG
            continue
        b = d if d < exact else min(BUCKETS - 1, exact + int(math.log(d / exact) / math.log(2048 / exact) * (BUCKETS - exact)))
        onehot[b, :, j] = 1.0
        m = (d <= 128) + (d % 4 == 0) + (d % 16 == 0)
        onehot[BUCKETS, 1, j] = math.log(m) if m else NEG
    cmask = np.zeros((P, QT, 33), np.float32)
    for i in range(QT):
        for p in range(P):
            for n in range(32):
                if n >= NCMP or 16 * n + 31 > P * i + p:
                    cmask[p, i, n] = NEG
            cmask[p, i, 32] = float(P * i + p >= 31)
    return {"onehot": onehot, "ident": np.eye(P, dtype=np.float32), "cmpmask": cmask}


def kernel(**inputs):
    import numpy as np
    import concourse.bacc as bacc
    from concourse.bass_utils import run_bass_kernel_spmd

    nc = bacc.Bacc("TRN2", target_bir_lowering=False, num_devices=1)
    arrays, args = {}, []
    given = {name: np.ascontiguousarray(inputs[name]) for name in INPUTS}
    given.update(shape_constants())
    for name, a in given.items():
        arrays[f"in_{name}"] = a
        args.append(nc.dram_tensor(f"in_{name}", a.shape, mybir.dt.from_np(a.dtype), kind="ExternalInput").ap())
    args.append(nc.dram_tensor("bias_rows", (20, FROW), F32, kind="Internal").ap())
    args.append(nc.dram_tensor("out_0", (1, S, D), F32, kind="ExternalOutput").ap())
    build(nc, *args)
    r = run_bass_kernel_spmd(nc, [arrays], core_ids=[0])
    return r.results[0]["out_0"]
```

```python
import math
from contextlib import ExitStack

import concourse.bass as bass
from concourse import mybir

F32 = mybir.dt.float32
F32R = mybir.dt.float32r
ALU = mybir.AluOpType
ACT = mybir.ActivationFunctionType
AXX = mybir.AxisListType.X

P = 128
D = 1024
S = 512
KC = D // P
QT = S // P
HD = 64
F = 2816
FC = F // P
EPS = 1e-6
NEG = -1e30
EV_IN = 2328
CONV_W = 31
PAD = CONV_W - 1
NCMP = 31
NPAIR = 16
BUCKETS = 32
FROW = 640
LAM_INIT = 0.8 - 0.6 * math.exp(-0.3)
DOWN = (8, 8, 6)

U_IN0 = 0
N_IN0 = 19
U_OUT0 = U_IN0 + N_IN0
U_GU = [U_OUT0 + KC, 0]
U_DN = [U_GU[0] + 2 * FC, 0]
U_IN1 = U_DN[0] + 3 * KC
N_IN1 = 24
U_OUT1 = U_IN1 + N_IN1
U_GU[1] = U_OUT1 + KC
U_DN[1] = U_GU[1] + 2 * FC
U_END = U_DN[1] + 3 * KC
O_IN0 = 0
O_OUT0 = O_IN0 + N_IN0
O_GU = [O_OUT0 + KC, 0]
O_DN = [O_GU[0] + 2 * FC, 0]
O_IN1 = O_DN[0] + KC
O_OUT1 = O_IN1 + N_IN1
O_GU[1] = O_OUT1 + KC
O_DN[1] = O_GU[1] + 2 * FC
RAW = 4
SPL = 2
NACC = 4

PR_MIX, PR_FFN, PR_FIN = 0, 16, 32
PR_DWB, PR_LNG, PR_LNB, PR_POS = 40, 44, 48, 52
PR_A = 84
PR_DWW = PR_A
PR_FF = [PR_DWW + CONV_W * 4, PR_DWW + CONV_W * 4 + 4 * FC]
PR_N = PR_FF[1] + 4 * FC

N_MEMSETS = 6
JOBS = 64
PER = JOBS // QT


def in0_units():
    kv = 512
    glu = 512 + 768 + 24
    units = []
    for c in range(4):
        units += [("g", c, glu + 512 + c * P, P), ("a", c, glu + c * P, P)]
    units += [("kc", 0, kv, P), ("kc", 1, kv + P, P)]
    units += [("v", 0, kv + 384, P), ("v", 1, kv + 640, P), ("gate", 0, kv + 768, P)]
    units += [("k", 0, kv + 256, P), ("k", 1, kv + 512, P)]
    units += [("q", c, c * HD, P) for c in range(4)]
    return units


def in1_units():
    kinds = ["q"] * 4 + ["k"] * 4 + ["cv"] * 4 + ["q"] * 4 + ["k"] * 4 + ["dv"] * 4
    index = list(range(4)) * 3 + list(range(4, 8)) * 2 + list(range(4))
    units = [(k, n, u * P, P) for u, (k, n) in enumerate(zip(kinds, index))]
    return units[8:12] + units[20:24] + units[0:8] + units[12:20]


def build(nc, x, rel_bias_table, mix_norm_g, ffn_norm_g, ffn_w_gate, ffn_w_up, ffn_conv_w, ffn_conv_b,
          ffn_w_down, ev_w_in, ev_w_out, nsa_phi_pos, nsa_phi_w1, nsa_phi_w2, conv_dw_w, conv_dw_b,
          conv_ln_g, conv_ln_b, od_w_in, od_w_out, diff_lambda, diff_norm_g, final_norm_g,
          c_onehot, c_ident, c_cmpmask, bias_rows, out):
    ctx = ExitStack()
    with ctx:
        top = [16896]

        def at(name, shape, dt=F32, offset=None):
            size = 4
            for n in shape[1:]:
                size *= n
            size = -(-size // 32) * 32
            where = top[0] if offset is None else offset
            if offset is None:
                top[0] += size
            t = nc.alloc_sbuf_tensor_at(name, shape, dt, offset=where)
            return t, where + size

        def sb(name, shape, dt=F32):
            return at(name, shape, dt)[0]

        def sem(name):
            return ctx.enter_context(nc.semaphore(name))

        XT = sb("XT", [P, KC, S])
        xout = at("xout", [P, QT, D], F32, top[0])[0]
        Hh = sb("Hh", [P, KC, S], F32R)
        Hl = sb("Hl", [P, KC, S], F32R)
        raw = sb("raw", [P, RAW, 8, P])
        Wh = sb("Wh", [P, SPL, 8, P], F32R)
        Wl = sb("Wl", [P, SPL, 8, P], F32R)
        ident = sb("ident", [P, P])
        ones = sb("ones", [P, P])
        prm = sb("prm", [P, PR_N])
        kcT = sb("kcT", [P, 2, 32])
        vbd = sb("vbd", [P, 2, 4 * HD])
        cmask = sb("cmask", [P, QT, 33])
        gate = sb("gate", [P, QT, 24])
        Ls = sb("Ls", [P, 2, 24])
        Rs = sb("Rs", [P, 48])
        Cs = sb("Cs", [P, 24])
        nmx = sb("nmx", [P, 4])
        cmx = sb("cmx", [P, 8])
        Sm = sb("Sm", [P, 8, 32])
        Pc = sb("Pc", [P, 8, 32])
        PcT = sb("PcT", [P, 2, P])
        lamb = sb("lamb", [P, 8])
        eps = sb("eps", [P, 8])
        xs = sb("xs", [P, 2, QT])
        lamp = sb("lamp", [P, 4, HD])
        dng = sb("dng", [P, 2])
        tab = sb("tab", [BUCKETS + 1, 20])
        w2s = sb("w2s", [P, 2, 2, HD])
        hid = sb("hid", [P, 2, 2, 2 * NCMP])

        g0 = top[0]
        sq, e = at("sq", [P, 2, S], F32, g0)
        hf, e = at("hf", [P, 2, S], F32, e)
        rs, e = at("rs", [P, S], F32, e)
        yb, e = at("yb", [P, 2, S], F32, e)
        ab, e_work = at("ab", [P, 2, S], F32, e)
        S2, e = at("S2", [P, 3, S], F32, g0)
        Pb, e = at("Pb", [P, 4, S], F32, e)
        PTs, e = at("PTs", [P, 2, S], F32, e)
        acc = ab[:, 1, :]
        KK, e = at("KK", [P, 2, 2, S], F32, g0)
        FT, e = at("FT", [P, 2, NPAIR, 2 * NCMP], F32, e)
        assert e <= e_work
        a0 = e_work
        Ah, e = at("Ah", [P, FC, S], F32R, a0)
        Al, e_top = at("Al", [P, FC, S], F32R, e)
        assert e_top <= 229344
        T0, e = at("T0", [P, 8, S], F32, a0)
        xin, _ = at("xin", [P, QT, D], F32, e)
        Q0, e = at("Q0", [P, 4, S], F32, e)
        V0, e = at("V0", [P, 2, QT, P], F32, e)
        tm, e = at("tm", [P, 3, S], F32, e)
        Uc, e = at("Uc", [P, 4, PAD + S + 2], F32, e)
        CA, e0 = at("CA", [P, 4, S], F32, e)
        onehot, e = at("onehot", [BUCKETS + 1, 2, FROW], F32, e0)
        pst, e = at("pst", [P, 4, P], F32, e)
        brow, e = at("brow", [12, 2, FROW], F32, e)
        xn, e = at("xn", [P, QT, D], F32, e)
        phw, e1 = at("phw", [P, 2, NPAIR, 2 * P], F32, e0)
        assert e <= e1
        Qs, e = at("Qs", [P, 8, S], F32R, e0)
        Kd, e = at("Kd", [P, 4, 2, S], F32R, e)
        assert max(e, e1) <= e_top
        T1, e = at("T1", [P, 12, S], F32, a0)
        Q1, e = at("Q1", [P, 8, S], F32, e)
        K1, e = at("K1", [P, 8, S], F32, e)
        Vc, e = at("Vc", [P, QT, S], F32, e)
        Vd, e = at("Vd", [P, QT, S], F32, e)
        tn, e = at("tn", [P, 5, S], F32, e)
        rs1, e = at("rs1", [P, S], F32, e)
        assert e <= e_top

        bank = ctx.enter_context(nc.psum_tensor("bank", [P, 8, S], F32))

        raw_loaded = [sem(f"raw_loaded{n}") for n in range(RAW)]
        weights_hi = sem("weights_hi")
        weights_lo = sem("weights_lo")
        unit_done = sem("unit_done")
        tile_read = [sem(f"tile_read{n}") for n in range(NACC)]
        x_loaded = [sem(f"x_loaded{t}") for t in range(QT)]
        ident_loaded = sem("ident_loaded")
        consts_loaded = sem("consts_loaded")
        params_loaded = [sem(f"params_loaded{b}") for b in range(4)]
        small_loaded = sem("small_loaded")
        phi_loaded = sem("phi_loaded")
        rows_stored = sem("rows_stored")
        strips_loaded = sem("strips_loaded")
        memsets = sem("memsets")
        turned = sem("turned")
        param_copied = sem("param_copied")
        row_made = sem("row_made")
        row_copied = sem("row_copied")
        xt_ready = sem("xt_ready")
        sq_ready = sem("sq_ready")
        sq_added = sem("sq_added")
        sq_summed = sem("sq_summed")
        rms_ready = sem("rms_ready")
        hh_ready = sem("hh_ready")
        h_ready = sem("h_ready")
        dstep = sem("dstep")
        ft_ready = sem("ft_ready")
        hid_made = sem("hid_made")
        hid_ready = sem("hid_ready")
        cmp_made = sem("cmp_made")
        cmp_ready = sem("cmp_ready")
        conv_done = sem("conv_done")
        ln_mean = sem("ln_mean")
        ln_centered = sem("ln_centered")
        ln_sq = sem("ln_sq")
        ln_var = sem("ln_var")
        ln_std = sem("ln_std")
        ln_scaled = sem("ln_scaled")
        u_ready = sem("u_ready")
        cc_hi = sem("cc_hi")
        cc_ready = sem("cc_ready")
        k_hi = sem("k_hi")
        q_split = sem("q_split")
        qk_done = sem("qk_done")
        scores_read = sem("scores_read")
        probs_ready = sem("probs_ready")
        probs_turned = sem("probs_turned")
        pt_copied = [sem("pt_copied_dve"), sem("pt_copied_act")]
        mixed = sem("mixed")
        pv_done = sem("pv_done")
        read_a = sem("read_a")
        read_b = sem("read_b")
        combined_a = sem("combined_a")
        combined_b = sem("combined_b")
        ct_turned = sem("ct_turned")
        ct_hi = sem("ct_hi")
        sc_made = sem("sc_made")
        sc_shifted = sem("sc_shifted")
        pc_ready = sem("pc_ready")
        pc_turned = sem("pc_turned")
        pc_copied = sem("pc_copied")
        oc_made = sem("oc_made")
        o_product = sem("o_product")
        o_squared = sem("o_squared")
        o_rms = sem("o_rms")
        lam_dots = sem("lam_dots")
        lam_exps = sem("lam_exps")
        gain_ready = sem("gain_ready")
        y_base = sem("y_base")
        y_gelu = sem("y_gelu")
        ah_ready = sem("ah_ready")
        a_ready = sem("a_ready")
        fin_ready = sem("fin_ready")
        x_squared = sem("x_squared")
        x_std = sem("x_std")
        x_inverse = sem("x_inverse")
        x_scaled = sem("x_scaled")
        x_scaled_act = sem("x_scaled_act")
        xn_turned = sem("xn_turned")
        v_turned = sem("v_turned")
        v_placed = sem("v_placed")
        y_conv = sem("y_conv")
        prod = sem("prod")
        fin_turned = sem("fin_turned")
        fin_copied = sem("fin_copied")
        out_std = sem("out_std")
        out_inverse = sem("out_inverse")
        out_scaled_dve = sem("out_scaled_dve")
        out_scaled_act = sem("out_scaled_act")
        out_stored = sem("out_stored")

        w_in0 = ev_w_in[0].rearrange("(k p) n -> p k n", p=P)
        w_out = [ev_w_out[0].rearrange("(k p) n -> p k n", p=P), od_w_out[0].rearrange("(k p) n -> p k n", p=P)]
        w_in1 = od_w_in[0].rearrange("(k p) n -> p k n", p=P)
        w_gate = [ffn_w_gate[n].rearrange("(k p) n -> p k n", p=P) for n in range(2)]
        w_up = [ffn_w_up[n].rearrange("(k p) n -> p k n", p=P) for n in range(2)]
        w_down = [ffn_w_down[n].rearrange("(k p) n -> p k n", p=P) for n in range(2)]
        UN0, UN1 = in0_units(), in1_units()

        def spread(ap, *dims):
            return bass.AP(ap.tensor, ap.offset, [ap.ap[0], *[list(d) for d in dims]])

        def strip(t, head, i):
            v = t[:, head, :]
            return bass.AP(v.tensor, v.offset + P - 1 + P * i, [v.ap[0], [-1, P * (i + 1)]])

        def job(layer, j):
            i, r = divmod(j, PER)
            ks = slice(0, P * (i + 1))
            qs = slice(P * i, P * (i + 1))
            if layer == 0:
                br, c, g = r // 8, (r % 8) // 2, r % 2
                h = 4 * g + c
                half = slice(HD * g, HD * g + HD)
                return ([(Qs[:, h, qs], Kd[:, 2 * br + g, m, ks]) for m in range(2)], strip(T0, h, i),
                        [V0[:, br, t, half] for t in range(i + 1)], bank[:, br, HD * h:HD * h + HD],
                        Ls[:, i % 2, 8 + 8 * br + h:9 + 8 * br + h])
            if r < 8:
                h, m = divmod(r, 2)
                half = slice(HD * m, HD * m + HD)
                return ([(Q1[half, h, qs], K1[half, h, ks])], strip(T1, h, i),
                        [Vc[:, t, P * h:P * h + P] for t in range(i + 1)], bank[:, 0, P * h:P * h + P],
                        Ls[:, i % 2, 4 * m + h:4 * m + h + 1])
            h = r - 8
            half = slice(HD * (h % 2), HD * (h % 2) + HD)
            return ([(Q1[half, 4 + h // 2, qs], K1[half, 4 + h // 2, ks])], strip(T1, 4 + h, i),
                    [Vd[:, t, HD * h:HD * h + HD] for t in range(i + 1)], bank[:, 2, HD * h:HD * h + HD],
                    Ls[:, i % 2, 8 + h:9 + h])

        LAST = QT - 1
        LAST_CT = PER * LAST + 23
        CT = [{PER * i + (25 if i < LAST else 23): [(i, 0)] for i in range(QT)},
              {**{PER * 2 + 22 + 3 * i: [(i, 0)] for i in range(LAST)}, PER * LAST + 20: [(LAST, 0)],
               **{PER * i + (26 if i < LAST else 23): [(i, 1)] for i in range(QT)}}]
        STEPS = PER * (QT - 1) + 24
        LAG_T, LAG_V = (3, 4), (4, 5)
        LAG_M = 2
        use = {}
        for layer in range(2):
            for s in range(STEPS):
                if s < JOBS:
                    use[layer, s] = len(use)
                for key in CT[layer].get(s, []):
                    use[layer, "ct", key] = len(use)
        first1 = use[1, 0]

        def score_bank(n):
            return 4 + n % 2 if n < first1 + PER else (4, 5, 1)[(n - first1 - PER) % 3]

        def before(n):
            return n - 1 if n < first1 + PER + 2 else n - 2

        CTN = {key: n for n, key in enumerate(k for k in use if k[1] == "ct")}

        def map_of(layer, j):
            return j % 2 if layer == 1 and j % PER < 8 else None

        def pairs(j):
            return 4 * (j // PER) + j % PER // 2 + 1

        turns = {}
        for layer in range(2):
            for j in range(JOBS):
                if map_of(layer, j) != 0:
                    turns[layer, j] = len(turns)
        STEP_CMP = {"scores": 2, "shift": 2, "exp": 5, "sum": 6, "turn": 7, "copy": 8, "values": 10}
        HIDDEN_AFTER, LN_AFTER = (11, 12), 15
        LATE = (N_IN1 - 2, N_IN1 - 1)
        LATE_CHUNKS = (2, 1, 2, 1, 2, 1, 2, 1, 2, 1, 1)
        assert sum(LATE_CHUNKS) == 2 * KC
        STEP_LATE = {6: 0, 12: 1}
        TURN0 = [n for n, un in enumerate(UN0) if un[0] in ("v", "gate")]
        TILE_K = [n for n, un in enumerate(UN0) if un[0] == "k"]
        TILE_Q = [n for n, un in enumerate(UN0) if un[0] == "q"]
        TURN1 = [n for n, un in enumerate(UN1) if un[0] in ("cv", "dv")]
        STEP_ROOT = 17
        STEP_U = {2 * PER + 2: 0, 2 * PER + 4: 1, 2 * PER + 6: 2, 2 * PER + 8: 3}

        ROOTS = {2: (0, 1, 2), 3: (3,)}

        def kept(i):
            return (3, 4, 0, 0)[i]

        def sums_at(i):
            return slice(16 + 4 * (i % 3), 20 + 4 * (i % 3))

        block = ctx.enter_context(nc.Block())

        def wait_read(eng, o, it=0):
            for n, o0 in enumerate((O_OUT0, O_DN[0], O_OUT1, O_DN[1])):
                if o0 <= o < o0 + KC:
                    eng.wait_ge(xt_ready, KC * (n + 1) + o - o0 + 1)
                    return
            eng.wait_ge(tile_read[o % NACC], reads(o) + it)

        def reads(o):
            kept = [range(o0, o0 + KC) for o0 in (O_OUT0, O_DN[0], O_OUT1, O_DN[1])]
            return sum(not any(t in r for r in kept) for t in range(o % NACC, o + 1, NACC))

        def raw_count(u):
            n = 0
            for v in range(u % RAW, u + 1, RAW):
                n += 32 if v < N_IN0 and UN0[v][0] == "q" else 16
            return n

        def staged_at(v):
            o = O_IN0 + TURN0[v] if v < len(TURN0) else O_IN1 + TURN1[v - len(TURN0)]
            return tile_read[o % NACC], reads(o)

        def gain(norm, k):
            col = {1: PR_FFN, 2: PR_MIX + KC, 3: PR_FFN + KC}[norm] + k
            return prm[:, col:col + 1]

        def sq2(c):
            return tm[:, c % 2, :]

        def prm_ff(layer, it, q):
            return [prm[:, bass.ds(it * 2 + (PR_FF[layer] + FC * t + q), 1)] for t in range(4)]

        def one(t, it, q):
            return t[:, bass.ds(it * 2 + q, 1), :].rearrange("p a n -> p (a n)")

        @block.sync
        def _(sp):
            def load(u, src, nk=8, w=P, it=0, stride=0):
                if u >= RAW:
                    sp.wait_ge(weights_lo, u - RAW + 1 + it * stride)
                sp.dma_start(raw[:, u % RAW, 0:nk, 0:w], src).then_inc(raw_loaded[u % RAW], 16)

            def load_in0(u):
                kind, n, col, w = UN0[u - U_IN0]
                if kind != "q":
                    load(u, w_in0[:, :, col:col + w], w=w)
                    return
                if u >= RAW:
                    sp.wait_ge(weights_lo, u - RAW + 1)
                for g in range(2):
                    sp.dma_start(raw[:, u % RAW, :, HD * g:HD * g + HD],
                                 w_in0[:, :, col + 4 * HD * g:col + 4 * HD * g + HD]).then_inc(
                        raw_loaded[u % RAW], 16)

            for t in range(QT):
                sp.dma_start(xin[:, t, :], x[0, t * P:(t + 1) * P, :]).then_inc(x_loaded[t], 16)
            rows = [(0, PR_MIX, mix_norm_g.rearrange("l (k p) -> (l k) p", p=P)),
                    (0, PR_FFN, ffn_norm_g.rearrange("l (k p) -> (l k) p", p=P)),
                    (0, PR_FIN, final_norm_g.rearrange("(k p) -> k p", p=P)),
                    (0, PR_DWB, conv_dw_b[0].rearrange("(k p) -> k p", p=P)),
                    (0, PR_LNG, conv_ln_g[0].rearrange("(k p) -> k p", p=P)),
                    (0, PR_LNB, conv_ln_b[0].rearrange("(k p) -> k p", p=P)),
                    (0, PR_POS, nsa_phi_pos[0].rearrange("v (k l) d -> (v k) (l d)", l=2)),
                    (1, 0, conv_dw_w[0].rearrange("t (k p) -> (t k) p", p=P)),
                    (2, 0, ffn_conv_w[0].rearrange("t (k p) -> (t k) p", p=P)),
                    (2, 3 * FC, ffn_conv_b[0].rearrange("(k p) -> k p", p=P)),
                    (3, 0, ffn_conv_w[1].rearrange("t (k p) -> (t k) p", p=P)),
                    (3, 3 * FC, ffn_conv_b[1].rearrange("(k p) -> k p", p=P))]
            for b, r, src in rows:
                sp.dma_start(pst[r:r + src.shape[0], b, :], src).then_inc(params_loaded[b], 16)
            for u in range(2, RAW):
                load_in0(u)
            sp.dma_start(tab[0:BUCKETS, :], rel_bias_table).then_inc(consts_loaded, 16)
            sp.dma_start(onehot[:], c_onehot).then_inc(consts_loaded, 16)
            sp.dma_start(cmask[:], c_cmpmask).then_inc(small_loaded, 16)
            sp.dma_start(w2s[:], nsa_phi_w2[0].rearrange("v (h p) d -> p v h d", p=P)).then_inc(small_loaded, 16)
            sp.dma_start(lamp[:], bass.AP(diff_lambda.tensor, 0, [[0, P], [HD, 4], [1, HD]])).then_inc(small_loaded, 16)
            sp.dma_start(dng[:, 0:1], diff_norm_g.rearrange("l p -> p l")).then_inc(small_loaded, 16)
            for u in range(RAW, RAW + 4):
                load_in0(u)
            sp.wait_ge(row_copied, 2)
            sp.dma_start(bias_rows[0:12, :], brow[0:12, 0, :]).then_inc(rows_stored, 16)
            sp.dma_start(bias_rows[12:20, :], brow[0:8, 1, :]).then_inc(rows_stored, 16)
            sp.wait_ge(rows_stored, 32)

            def strips(dst, head, n):
                src = bass.AP(bias_rows.tensor, head * FROW, [[1, P], [FROW, n], [1, S]])
                sp.dma_start(dst[:, 0:n, :], src).then_inc(strips_loaded, 16)

            strips(T0, 0, 8)
            sp.wait_ge(param_copied, 4)
            sp.wait_ge(xn_turned, KC)
            for n, u in enumerate(range(RAW + 4, N_IN0)):
                load_in0(u)
                for piece in range(8)[2 * n:2 * n + 2]:
                    kv, l0 = piece // 4, 4 * (piece % 4)
                    sp.dma_start(phw[:, kv, l0:l0 + 4], nsa_phi_w1[0, kv, P * l0:P * (l0 + 4)].rearrange(
                        "(k p) h -> p k h", p=P)).then_inc(phi_loaded, 16)
            for n in range(KC):
                load(U_OUT0 + n, w_out[0][:, :, n * P:(n + 1) * P])

            def load_ffn(layer):
                with sp.Fori(0, FC // 2) as it:
                    for j in range(4):
                        w = (w_gate, w_up)[j % 2][layer]
                        load(U_GU[layer] + j, w[:, :, bass.ds(it * (2 * P) + (j // 2) * P, P)], it=it, stride=4)
                for n in range(KC):
                    k = 0
                    for r in range(3):
                        load(U_DN[layer] + 3 * n + r, w_down[layer][:, k:k + DOWN[r], n * P:(n + 1) * P], nk=DOWN[r])
                        k += DOWN[r]

            load_ffn(0)
            for u, (kind, n, col, w) in enumerate(UN1):
                if u == 6:
                    sp.wait_ge(unit_done, U_IN1)
                    strips(T1, 8, 12)
                load(U_IN1 + u, w_in1[:, :, col:col + w])
            for n in range(KC):
                load(U_OUT1 + n, w_out[1][:, :, n * P:(n + 1) * P])
            load_ffn(1)
            for n in range(QT):
                t = (0, 2, 1, 3)[n]
                sp.wait_ge((out_scaled_dve, out_scaled_act)[t // 2], t % 2 + 1)
                sp.dma_start(out[0, t * P:(t + 1) * P, :], xout[:, t, :]).then_inc(out_stored, 16)
            sp.wait_ge(out_stored, 16 * QT)

        @block.gpsimd
        def _(pool):
            fills = [(eps[:], EPS), (ones[:], 1.0), (tab[BUCKETS:BUCKETS + 1, :], 1.0), (kcT[:], 0.0), (vbd[:], 0.0),
                     (Uc[:, :, 0:PAD], 0.0)]
            assert len(fills) == N_MEMSETS
            for n, (dst, value) in enumerate(fills):
                if n:
                    pool.wait_ge(memsets, n)
                nc.gpsimd.memset(dst, value).then_inc(memsets, 1)
            pool.wait_ge(memsets, N_MEMSETS)

            def rest(u, nk=8, w=P, it=0, stride=0):
                pool.wait_ge(weights_hi, u + 1 + it * stride)
                hi = Wh[:, u % SPL, 0:nk, 0:w]
                nc.gpsimd.tensor_tensor(Wl[:, u % SPL, 0:nk, 0:w], raw[:, u % RAW, 0:nk, 0:w], hi.bitcast(F32),
                                        ALU.subtract).then_inc(weights_lo, 1)

            def add_square(norm, k):
                if not 1 <= k < KC - 1:
                    return
                n = (norm - 1) * (KC - 2) + k
                pool.wait_ge(sq_ready, (norm - 1) * KC + k + 1)
                if n > 1:
                    pool.wait_ge(sq_added, n - 1)
                if k == 1 and norm > 1:
                    pool.wait_ge(sq_summed, norm - 1)
                nc.gpsimd.tensor_tensor(acc, sq[:, 0, :] if k == 1 else acc, sq[:, k % 2, :], ALU.add).then_inc(sq_added, 1)

            def rest_ffn(layer):
                with pool.Fori(0, FC // 2) as it:
                    for j in range(4):
                        rest(U_GU[layer] + j, it=it, stride=4)
                for n in range(3 * KC):
                    rest(U_DN[layer] + n, nk=DOWN[n % 3])
                    m, r = divmod(n - 4, 3)
                    if r == 0:
                        add_square(2 * layer + 2, m)

            for u in range(N_IN0):
                rest(u, w=UN0[u][3])
            def gated_sums():
                for i in range(QT):
                    for read, done in ((read_a, combined_a), (read_b, combined_b)):
                        pool.wait_ge(read, i + 1)
                        if done is combined_b:
                            pool.wait_ge(combined_a, i + 1)
                        nc.gpsimd.tensor_tensor(tm[:, 0, :], tm[:, 0, :], tm[:, 1, :], ALU.add).then_inc(done, 1)

            def differential_squares():
                for i in range(QT):
                    pool.wait_ge(read_a, QT + i + 1)
                    if i > 0:
                        pool.wait_ge(o_squared, i)
                    nc.gpsimd.tensor_tensor(tn[:, 1, :], tn[:, kept(i), :], tn[:, kept(i), :], ALU.mult).then_inc(o_product, 1)

            for n in range(KC):
                rest(U_OUT0 + n)
                if n == SPL - 1:
                    gated_sums()
                add_square(1, n - 2)
            add_square(1, KC - 2)
            rest_ffn(0)
            for n in range(N_IN1 + KC):
                rest(U_IN1 + n)
                if n == N_IN1 + SPL - 1:
                    differential_squares()
                if n >= N_IN1:
                    add_square(3, n - N_IN1 - 2)
            add_square(3, KC - 2)
            rest_ffn(1)

        @block.tensor
        def _(pe):
            pe.wait_ge(ident_loaded, 16)
            for b, n in enumerate((PR_A, 4 * CONV_W, 4 * FC, 4 * FC)):
                pe.wait_ge(params_loaded[b], 16 * (7, 1, 2, 2)[b])
                nc.tensor.transpose(bank[:, b, 0:n], pst[0:n, b, :], ident[0:n, 0:n]).then_inc(turned, 1)
            for k in range(KC):
                pe.wait_ge(x_scaled, QT // 2)
                pe.wait_ge(x_scaled_act, QT // 2)
                if k >= 4:
                    pe.wait_ge(h_ready, k - 3)
                for t in range(QT):
                    mm = nc.tensor.transpose(bank[:, 4 + k % 4, t * P:(t + 1) * P], xn[:, t, k * P:(k + 1) * P], ident[:])
                mm.then_inc(xn_turned, 1)

            def turn_input(k):
                pe.wait_ge(h_ready, min(KC, k + 5))
                if k >= 4:
                    pe.wait_ge(xt_ready, k - 3)
                for t in range(QT):
                    mm = nc.tensor.transpose(bank[:, 4 + k % 4, t * P:(t + 1) * P], xin[:, t, k * P:(k + 1) * P], ident[:])
                mm.then_inc(turned, 1)

            def stats(norm):
                pe.wait_ge(sq_added, norm * (KC - 2))
                nc.tensor.matmul(bank[:, 7, :], ones[:], acc, start=True, stop=False)
                pe.wait_ge(sq_ready, norm * KC)
                nc.tensor.matmul(bank[:, 7, :], ones[:], sq[:, (KC - 1) % 2, :], start=False, stop=True).then_inc(sq_summed, 1)

            pe.wait_ge(memsets, N_MEMSETS)

            def bias_row(v):
                c0, c1 = ((0, 12), (12, 20))[v]
                pe.wait_ge(consts_loaded, 32)
                pe.wait_ge(xt_ready, KC)
                if v == 1:
                    pe.wait_ge(row_copied, 1)
                nc.tensor.matmul(bank[0:c1 - c0, 4, :], tab[:, c0:c1], onehot[:, v, 0:S], start=True, stop=True)
                nc.tensor.matmul(bank[0:c1 - c0, 5, 0:FROW - S], tab[:, c0:c1], onehot[:, v, S:FROW], start=True,
                                 stop=True).then_inc(row_made, 1)

            def begin(o, it=0):
                if o >= NACC:
                    wait_read(pe, o - NACC, it)
                return bank[:, o % NACC, :]

            def product(dst, u, nk, oh, ol, k0=0, first=True, last=True, ready=h_ready, hwait=None, it=0, stride=0,
                        kw=0, done=True):
                pe.wait_ge(weights_lo, u + 1 + it * stride)
                s = u % SPL
                for k in range(nk):
                    if hwait is not None:
                        pe.wait_ge(ready, hwait + k0 + k + 1)
                    a = first and k == 0
                    z = last and k == nk - 1
                    nc.tensor.matmul(dst, Wh[:, s, kw + k, :], oh[:, k0 + k, :], start=a, stop=False)
                    nc.tensor.matmul(dst, Wh[:, s, kw + k, :], ol[:, k0 + k, :], start=False, stop=False)
                    mm = nc.tensor.matmul(dst, Wl[:, s, kw + k, :], oh[:, k0 + k, :], start=False, stop=z)
                if done:
                    mm.then_inc(unit_done, 1)

            def turn_values(v, stage):
                pe.wait_ge(staged_at(v)[0], staged_at(v)[1])
                if v >= 2:
                    pe.wait_ge(v_placed, v - 1)
                for t in range(QT):
                    mm = nc.tensor.transpose(bank[:, 4 + v % 2, t * P:(t + 1) * P], stage[:, v % 2, t * P:(t + 1) * P], ident[:])
                mm.then_inc(v_turned, 1)

            def hidden(kv):
                pe.wait_ge(phi_loaded, 64 * (kv + 1))
                pe.wait_ge(ft_ready, kv + 1)
                for hh in range(2):
                    for l in range(NPAIR):
                        mm = nc.tensor.matmul(bank[:, 6 + kv, hh * P:hh * P + 2 * NCMP],
                                              phw[:, kv, l, hh * P:(hh + 1) * P], FT[:, kv, l, :],
                                              start=l == 0, stop=l == NPAIR - 1)
                mm.then_inc(hid_made, 1)

            def conv_mean():
                pe.wait_ge(v_placed, len(TURN0))
                for c in range(4):
                    pe.wait_ge(conv_done, c + 1)
                    mm = nc.tensor.matmul(bank[:, 4, :], ones[:], CA[:, c, :], start=c == 0, stop=c == 3)
                mm.then_inc(ln_mean, 1)

            def compressed():
                pe.wait_ge(small_loaded, 64)
                pe.wait_ge(hid_ready, 2)
                for g in range(2):
                    for hh in range(2):
                        nc.tensor.matmul(bank[HD * g:HD * g + HD, 5, 0:NCMP], w2s[:, 0, hh, :],
                                         hid[:, 0, hh, NCMP * g:NCMP * g + NCMP], start=hh == 0, stop=hh == 1)
                for g in range(2):
                    for q in range(4):
                        for hh in range(2):
                            mm = nc.tensor.matmul(bank[32 * q:32 * q + NCMP, 6, 256 * g + HD * q:256 * g + HD * q + HD],
                                                  hid[:, 1, hh, NCMP * g:NCMP * g + NCMP], w2s[:, 1, hh, :],
                                                  start=hh == 0, stop=hh == 1)
                mm.then_inc(cmp_made, 1)

            def conv_variance():
                for c in range(4):
                    pe.wait_ge(ln_sq, c + 1)
                    nc.tensor.matmul(bank[:, 7, :], ones[:], sq2(c), start=c == 0, stop=c == 3).then_inc(ln_var, 1)

            pe.wait_ge(param_copied, 4)
            for n, (kind, idx, col, w) in enumerate(UN0):
                dst = begin(O_IN0 + n)
                product(dst, U_IN0 + n, KC, Hh, Hl, hwait=0 if n == 0 else None)
                if n < 2:
                    for k in range(4 * n, 4 * n + 4):
                        turn_input(k)
                if 2 <= n < 4:
                    bias_row(n - 2)
                if n - 1 in TURN0:
                    turn_values(TURN0.index(n - 1), tm)
                if n in HIDDEN_AFTER:
                    hidden(HIDDEN_AFTER.index(n))
                if n == LN_AFTER:
                    conv_mean()
                    compressed()
                    conv_variance()

            def first_half(layer, n, chunks=range(4)):
                if layer == 0:
                    pe.wait_ge(cc_ready, 4)
                    k0 = 4
                else:
                    pe.wait_ge(scores_read, use[1, "ct", (QT - 1, 0)] + 1)
                    k0 = 0
                o = (O_OUT0, O_OUT1)[layer] + n
                dst = begin(o) if chunks[0] == 0 else bank[:, o % NACC, :]
                k = k0 + chunks[0]
                product(dst, (U_OUT0, U_OUT1)[layer] + n, len(chunks), Hh, Hl, k0=k, kw=k, first=chunks[0] == 0, last=False,
                        done=False)

            def attention(layer):
                J = JOBS * layer
                base = QT * layer
                Tm = (tm, tn)[layer]
                for s in range(STEPS):
                    i, r = divmod(s, PER)
                    j = s - LAG_T[layer]
                    if (layer, j) in turns:
                        v = turns[layer, j]
                        if map_of(layer, j) == 1:
                            pe.wait_ge(mixed, pairs(j))
                        else:
                            pe.wait_ge(probs_ready, J + j + 1)
                        if v == 1:
                            pe.wait_ge(ln_std, 1)
                        if v >= 2:
                            pe.wait_ge(pt_copied[v % 2], v // 2)
                        for t in range(j // PER + 1):
                            mm = nc.tensor.transpose(bank[:, 6 + v % 2, t * P:(t + 1) * P], Pb[:, j % 4, t * P:(t + 1) * P],
                                                     ident[:])
                        mm.then_inc(probs_turned, 1)
                    for j in (range(s, s + 1), range(s + (s > 0), s + 2))[layer]:
                        if j >= JOBS:
                            continue
                        tile, r1 = divmod(j, PER)
                        scores = job(layer, j)[0]
                        if layer == 0 and tile == 0 and r1 % 2 == 0:
                            wait_read(pe, O_IN0 + TILE_K[r1 // 8])
                            pe.wait_ge(q_split, r1 % 8 // 2 + 1)
                        if layer == 1 and j == 2:
                            wait_read(pe, O_IN1 + LATE[0] - 1)
                        if layer == 1 and j in (PER - 4, PER - 2):
                            wait_read(pe, O_IN1 + LATE[j % 4 // 2])
                        n = use[layer, j]
                        if n >= 2:
                            pe.wait_ge(scores_read, before(n))
                        for m, (q, k) in enumerate(scores):
                            mm = nc.tensor.matmul(bank[:, score_bank(n), 0:P * (tile + 1)], q, k, start=m == 0,
                                                  stop=m == len(scores) - 1)
                        mm.then_inc(qk_done, 1)
                    if layer == 1 and s < len(LATE_CHUNKS):
                        done = sum(LATE_CHUNKS[:s])
                        for c in range(done, done + LATE_CHUNKS[s]):
                            n, k = LATE[c // KC], c % KC
                            dst = begin(O_IN1 + n) if k == 0 else bank[:, (O_IN1 + n) % NACC, :]
                            product(dst, U_IN1 + n, 1, Hh, Hl, k0=k, kw=k, first=k == 0, last=k == KC - 1, done=k == KC - 1)
                    if layer == 0 and r == STEP_CMP["scores"] and i < QT:
                        if i == 0:
                            for o in range(O_IN0 + N_IN0 - 2, O_IN0 + N_IN0):
                                wait_read(pe, o)
                        for c in range(4):
                            mm = nc.tensor.matmul(bank[:, 2, 64 * c:64 * c + 64], Q0[:, c, P * i:P * (i + 1)],
                                                  kcT[:].rearrange("p g n -> p (g n)"), start=True, stop=True)
                        mm.then_inc(sc_made, 1)
                    if s == LAST_CT:
                        pe.wait_ge(read_a, base + QT)
                        first_half(layer, 0)
                    for key in CT[layer].get(s, []):
                        n = use[layer, "ct", key]
                        if layer == 0:
                            pe.wait_ge(combined_b, 1 + key[0])
                        elif key[1] == 0:
                            pe.wait_ge(combined_a, QT + 1 + key[0])
                        else:
                            pe.wait_ge(read_b, QT + 1 + key[0])
                        pe.wait_ge(scores_read, before(n))
                        for c in range(4):
                            mm = nc.tensor.transpose(bank[:, score_bank(n), c * P:(c + 1) * P],
                                                     Tm[:, ct_tile(layer, key), c * P:(c + 1) * P], ident[:])
                        mm.then_inc(ct_turned, 1)
                    j = s - LAG_V[layer]
                    if (layer, j) in turns:
                        p = turns[layer, j]
                        if j >= PER and j % PER in (layer, PER // 2):
                            pe.wait_ge((read_a, read_b)[j % PER // 8], base + j // PER)
                        pe.wait_ge(pt_copied[p % 2], p // 2 + 1)
                        _, _, values, o, _ = job(layer, j)
                        for t, vt in enumerate(values):
                            mm = nc.tensor.matmul(o, PTs[:, p % 2, t * P:(t + 1) * P], vt, start=t == 0,
                                                  stop=t == len(values) - 1)
                        mm.then_inc(pv_done, 1)
                    if layer == 0 and r == STEP_CMP["turn"] and i < QT:
                        pe.wait_ge(pc_ready, i + 1)
                        for g in range(2):
                            mm = nc.tensor.transpose(bank[:, 3, g * P:(g + 1) * P], Pc[:, 4 * g:4 * g + 4, :].rearrange("p h n -> p (h n)"),
                                                     ident[:])
                        mm.then_inc(pc_turned, 1)
                    if layer == 0 and r == STEP_CMP["values"] and i < QT:
                        pe.wait_ge(pc_copied, i + 1)
                        if i > 0:
                            pe.wait_ge(read_a, i)
                        for g in range(2):
                            mm = nc.tensor.matmul(bank[:, 2 + g, 2 * P:4 * P], PcT[:, g, :], vbd[:, g, :], start=True, stop=True)
                        mm.then_inc(oc_made, 1)

            def ct_tile(layer, key):
                return 2 if key[1] else kept(key[0]) if layer else 0

            def project_out(layer, u0, o0, norm):
                first_half(layer, 1, range(3))
                pe.wait_ge(scores_read, use[layer, "ct", (QT - 1, layer)] + 1)
                k0 = 4 * layer
                for n in range(KC):
                    if n == 1:
                        first_half(layer, 1, range(3, 4))
                    if n < 2:
                        product(bank[:, (o0 + n) % NACC, :], u0 + n, 4, Hh, Hl, k0=k0, kw=k0, first=False)
                    else:
                        product(begin(o0 + n), u0 + n, KC, Hh, Hl)
                stats(norm)

            def turn_output(k):
                pe.wait_ge(fin_ready, k + 1)
                if k >= 2:
                    pe.wait_ge(fin_copied, k - 1)
                for t in range(QT):
                    mm = nc.tensor.transpose(bank[:, 4 + k % 2, t * P:(t + 1) * P], hf[:, k % 2, t * P:(t + 1) * P], ident[:])
                mm.then_inc(fin_turned, 1)

            def ffn(layer):
                norm = 2 * layer + 1
                with pe.Fori(0, FC // 2) as it:
                    for j in range(4):
                        dst = bank[:, (O_GU[layer] + j) % NACC, :]
                        pe.wait_ge(tile_read[(O_GU[layer] + j) % NACC], reads(O_GU[layer] + j) - 1 + it)
                        product(dst, U_GU[layer] + j, KC, Hh, Hl, hwait=KC * norm if j == 0 else None, it=it, stride=4)
                for n in range(KC):
                    dst = begin(O_DN[layer] + n)
                    k = 0
                    for r in range(3):
                        product(dst, U_DN[layer] + 3 * n + r, DOWN[r], Ah, Al, k0=k, first=r == 0, last=r == 2,
                                ready=a_ready, hwait=FC * layer if n == 0 else None)
                        k += DOWN[r]
                    if layer == 1 and n > 0:
                        turn_output(n - 1)
                if layer == 1:
                    turn_output(KC - 1)

            pe.wait_ge(cmp_ready, 1)
            pe.wait_ge(ln_centered, 4)
            for o in range(O_IN0 + N_IN0 - 6, O_IN0 + N_IN0 - 2):
                wait_read(pe, o)
            attention(0)
            project_out(0, U_OUT0, O_OUT0, 1)
            ffn(0)
            for n, (kind, idx, col, w) in enumerate(UN1[:LATE[0]]):
                dst = begin(O_IN1 + n)
                product(dst, U_IN1 + n, KC, Hh, Hl, hwait=2 * KC if n == 0 else None)
                if n == 0:
                    stats(2)
                if n - 1 in TURN1:
                    turn_values(len(TURN0) + TURN1.index(n - 1), tn)
            pe.wait_ge(v_placed, len(TURN0) + len(TURN1))
            for o in range(O_IN1 + LATE[0] - NACC, O_IN1 + LATE[0] - 1):
                wait_read(pe, o)
            attention(1)
            project_out(1, U_OUT1, O_OUT1, 3)
            ffn(1)
            pe.wait_ge(sq_added, 4 * (KC - 2))
            pe.wait_ge(sq_ready, 4 * KC)
            for t in range(QT):
                nc.tensor.matmul(bank[:, 7, t:t + 1], acc[:, t * P:(t + 1) * P], ones[:, 0:1], start=True, stop=False)
                mm = nc.tensor.matmul(bank[:, 7, t:t + 1], sq[:, (KC - 1) % 2, t * P:(t + 1) * P], ones[:, 0:1],
                                      start=False, stop=True)
            mm.then_inc(sq_summed, 1)

        @block.scalar
        def _(act):
            def round_unit(u, it=0, stride=0):
                if u >= U_END:
                    return
                nk, w = 8, P
                for d in U_DN:
                    if d <= u < d + 3 * KC:
                        nk = DOWN[(u - d) % 3]
                if u < N_IN0:
                    w = UN0[u][3]
                if u >= SPL:
                    act.wait_ge(unit_done, u - SPL + 1 + it * stride)
                act.wait_ge(raw_loaded[u % RAW], raw_count(u) + it * (stride // RAW * 16))
                nc.scalar.copy(Wh[:, u % SPL, 0:nk, 0:w], raw[:, u % RAW, 0:nk, 0:w]).then_inc(weights_hi, 1)

            def square(norm, k):
                act.wait_ge(xt_ready, norm * KC + k + 1)
                if k >= 2:
                    act.wait_ge(sq_added, (norm - 1) * (KC - 2) + max(1, k - 2))
                elif norm > 1:
                    act.wait_ge(sq_summed, norm - 1)
                nc.scalar.activation(sq[:, k % 2, :], XT[:, k, :], ACT.Square).then_inc(sq_ready, 1)

            def norm_root(norm):
                act.wait_ge(sq_summed, norm)
                nc.scalar.activation(rs[:], bank[:, 7, :], ACT.Sqrt, bias=eps[:, 0:1], scale=1.0 / D).then_inc(rms_ready, 1)

            def gain_round(norm, k):
                act.wait_ge(xt_ready, KC * norm + k + 1)
                nc.scalar.activation(Hh[:, k, :], XT[:, k, :], ACT.Identity, scale=gain(norm, k)).then_inc(hh_ready, 1)

            act.dma_start(ident[:], c_ident).then_inc(ident_loaded, 16)
            for u in range(2):
                _, _, col, w = UN0[u]
                act.dma_start(raw[:, u, :, 0:w], w_in0[:, :, col:col + w]).then_inc(raw_loaded[u], 16)
            act.wait_ge(memsets, 1)
            nc.scalar.activation(lamb[:, 7:8], eps[:, 0:1], ACT.Sqrt)
            for t in range(QT):
                act.wait_ge(x_loaded[t], 16)
                nc.scalar.activation(xn[:, t, :], xin[:, t, :], ACT.Square, accum_out=xs[:, 0, t:t + 1]).then_inc(x_squared, 1)
            act.wait_ge(memsets, N_MEMSETS)
            act.wait_ge(x_squared, QT)
            nc.scalar.activation(xs[:, 1, :], xs[:, 0, :], ACT.Sqrt, bias=eps[:, 0:1], scale=1.0 / D).then_inc(x_std, 1)
            act.wait_ge(x_inverse, 1)
            for t in range(QT // 2, QT):
                nc.scalar.mul(xn[:, t, :], xin[:, t, :], xs[:, 1, t:t + 1]).then_inc(x_scaled_act, 1)
            round_unit(0)
            round_unit(1)
            act.wait_ge(param_copied, 1)
            for k in range(KC):
                act.wait_ge(xn_turned, k + 1)
                nc.scalar.activation(Hh[:, k, :], bank[:, 4 + k % 4, :], ACT.Identity,
                                     scale=prm[:, PR_MIX + k:PR_MIX + k + 1]).then_inc(hh_ready, 1)
            def bias_row(v):
                act.wait_ge(row_made, v + 1)
                n = (12, 8)[v]
                nc.scalar.copy(brow[0:n, v, 0:S], bank[0:n, 4, :])
                nc.scalar.copy(brow[0:n, v, S:FROW], bank[0:n, 5, 0:FROW - S]).then_inc(row_copied, 1)

            def place0(v):
                act.wait_ge(v_turned, v + 1)
                src = bank[:, 4 + v % 2, :]
                if v < 2:
                    nc.scalar.copy(V0[:, v].rearrange("p t c -> p (t c)"), src).then_inc(v_placed, 1)
                else:
                    nc.scalar.activation(gate[:], src.rearrange("p (t c) -> p t c", t=QT)[:, :, 0:24],
                                         ACT.Sigmoid).then_inc(v_placed, 1)

            def conv_squares():
                for c in range(4):
                    act.wait_ge(ln_centered, c + 1)
                    if c >= 2:
                        act.wait_ge(ln_var, c - 1)
                    nc.scalar.activation(sq2(c), CA[:, c, :], ACT.Square).then_inc(ln_sq, 1)

            def hidden(kv):
                act.wait_ge(hid_made, kv + 1)
                nc.scalar.activation(hid[:, kv], bank[:, 6 + kv, 0:2 * P].rearrange("p (a n) -> p a n", a=2)[:, :, 0:2 * NCMP],
                                     ACT.Silu).then_inc(hid_ready, 1)

            def compressed():
                act.wait_ge(cmp_made, 1)
                for g in range(2):
                    half = slice(HD * g, HD * g + HD)
                    nc.scalar.copy(kcT[half, g, 0:NCMP], bank[half, 5, 0:NCMP])
                for g in range(2):
                    for q in range(4):
                        last = nc.scalar.copy(vbd[32 * q:32 * q + NCMP, g, HD * q:HD * q + HD],
                                              bank[32 * q:32 * q + NCMP, 6, 256 * g + HD * q:256 * g + HD * q + HD])
                last.then_inc(cmp_ready, 1)

            for n, (kind, idx, col, w) in enumerate(UN0):
                o = O_IN0 + n
                src = bank[:, o % NACC, :]
                free = tile_read[o % NACC]
                if n < N_IN0 - 1:
                    round_unit(U_IN0 + n + SPL)
                else:
                    act.wait_ge(unit_done, U_IN0 + N_IN0)
                if kind == "g":
                    if idx >= 2:
                        wait_read(act, o - 3)
                    nc.scalar.activation(yb[:, idx % 2, :], src, ACT.Sigmoid).then_inc(free, 1)
                elif kind == "kc":
                    for g in range(2):
                        half = slice(HD * g, HD * g + HD)
                        nc.scalar.copy(KK[0:HD, idx, g, :], bank[half, o % NACC, :])
                        last = nc.scalar.copy(KK[HD:P, idx, g, 0:S - 1], bank[half, o % NACC, 1:S])
                    last.then_inc(free, 1)
                elif kind == "q":
                    for g in range(2):
                        half = slice(HD * g, HD * g + HD)
                        nc.scalar.mul(Qs[half, 4 * g + idx, :], bank[half, o % NACC, :], HD ** -0.5)
                    nc.scalar.mul(Q0[:, idx, :], src, HD ** -0.5).then_inc(free, 1)
                elif kind == "k":
                    for g in range(2):
                        for to in range(2):
                            ins = nc.scalar.copy(Kd[HD * to:HD * to + HD, 2 * idx + g, 0, :],
                                                 bank[HD * g:HD * g + HD, o % NACC, :])
                    ins.then_inc(k_hi, 1)
                elif kind in ("v", "gate"):
                    v = TURN0.index(n)
                    if v >= 2:
                        act.wait_ge(v_turned, v - 1)
                    nc.scalar.copy(tm[:, v % 2, :], src).then_inc(free, 1)
                    if v >= 1:
                        place0(v - 1)
                if 2 <= n < 4:
                    bias_row(n - 2)
                if n == TURN0[-1] + 1:
                    place0(len(TURN0) - 1)
                if n in HIDDEN_AFTER:
                    hidden(HIDDEN_AFTER.index(n))
                if n == LN_AFTER:
                    conv_squares()
                    compressed()
                    act.wait_ge(ln_var, 4)
                    nc.scalar.activation(tm[:, 2, :], bank[:, 7, :], ACT.Sqrt, bias=eps[:, 0:1], scale=1.0 / 512).then_inc(ln_std, 1)
                if n == LN_AFTER + 1:
                    for c in range(4):
                        act.wait_ge(ln_scaled, c + 1)
                        nc.scalar.activation(CA[:, c, :], CA[:, c, :], ACT.Silu, bias=prm[:, PR_LNB + c:PR_LNB + c + 1]).then_inc(u_ready, 1)
                    nc.scalar.activation(lamb[:, 7:8], eps[:, 0:1], ACT.Exp)
            def conv_round(c):
                act.wait_ge(u_ready, c + 1)
                act.wait_ge(unit_done, U_IN0 + N_IN0)
                nc.scalar.copy(Hh[:, 4 + c, :], CA[:, c, :]).then_inc(cc_hi, 1)

            def attention(layer):
                J = JOBS * layer
                for s in range(STEPS):
                    i, r = divmod(s, PER)
                    v = turns.get((layer, s - LAG_T[layer]), 0)
                    if v % 2 == 1:
                        w = P * ((s - LAG_T[layer]) // PER + 1)
                        act.wait_ge(probs_turned, v + 1)
                        if v >= 2:
                            act.wait_ge(pv_done, v - 1)
                        nc.scalar.copy(PTs[:, 1, 0:w], bank[:, 7, 0:w]).then_inc(pt_copied[1], 1)
                    if s < JOBS:
                        L = job(layer, s)[4]
                        w = P * (s // PER + 1)
                        act.wait_ge(scores_read, use[layer, s] + 1)
                        if s >= 4 and map_of(layer, s - 4) == 0:
                            act.wait_ge(mixed, pairs(s - 4))
                        elif J + s >= 4:
                            act.wait_ge(probs_turned, turns[(layer, s - 4) if s >= 4 else (0, JOBS - 4 + s)] + 1)
                        nc.scalar.activation(Pb[:, s % 4, 0:w], S2[:, s % 3, 0:w], ACT.Exp, bias=nmx[:, s % 3:s % 3 + 1],
                                             scale=-1.0, accum_out=L).then_inc(probs_ready, 1)
                    for key in CT[layer].get(s, []):
                        n = use[layer, "ct", key]
                        if (layer, key[1]) == (1, 0):
                            act.wait_ge(gain_ready, 1)
                        act.wait_ge(ct_turned, CTN[layer, "ct", key] + 1)
                        c0 = 4 * key[1]
                        nc.scalar.activation(Hh[:, c0:c0 + 4, P * key[0]:P * (key[0] + 1)],
                                             bank[:, score_bank(n), :].rearrange("p (c t) -> p c t", c=4), ACT.Identity,
                                             scale=dng[:, 1:2] if (layer, key[1]) == (1, 0) else 1.0).then_inc(ct_hi, 1)
                    if layer == 0 and r == STEP_CMP["exp"] and i < QT:
                        act.wait_ge(sc_shifted, i + 1)
                        nc.scalar.activation(Pc[:].rearrange("p h n -> p (h n)"), Sm[:].rearrange("p h n -> p (h n)"),
                                             ACT.Exp).then_inc(pc_ready, 1)
                    if layer == 0 and s in STEP_U:
                        conv_round(STEP_U[s])
                    if layer == 0 and s == 4:
                        round_unit(U_OUT0 + 1)
                    if layer == 1 and s in STEP_LATE:
                        round_unit(U_OUT1 + STEP_LATE[s])
                    if layer == 1 and r == STEP_ROOT % PER and i - 1 in ROOTS:
                        act.wait_ge(o_squared, i)
                        w = 4 * len(ROOTS[i - 1])
                        nc.scalar.activation(Rs[:, 32:32 + w], Rs[:, 16:16 + w], ACT.Sqrt, bias=eps[:, 0:1],
                                             scale=1.0 / (2 * HD)).then_inc(o_rms, 1)

            def project_out(u0, norm):
                nc.scalar.activation(lamb[:, 7:8], eps[:, 0:1], ACT.Sqrt)
                for n in range(KC):
                    round_unit(u0 + n + SPL)
                    square(norm, n)
                for k in range(KC):
                    gain_round(norm, k)
                norm_root(norm)

            def ffn(layer):
                u0, o0 = U_GU[layer], O_GU[layer]
                with act.Fori(0, FC // 2) as it:
                    for q in range(2):
                        u, o, m = u0 + 2 * q, o0 + 2 * q, FC * layer + q
                        cols = prm_ff(layer, it, q)
                        round_unit(u + SPL, it, 4)
                        act.wait_ge(tile_read[o % NACC], reads(o) + it)
                        nc.scalar.activation(yb[:, q, :], hf[:, q, :], ACT.Identity, bias=cols[3],
                                             scale=cols[2]).then_inc(y_base, 1)
                        act.wait_ge(y_conv, m + 1 + it * 2)
                        nc.scalar.activation(yb[:, q, :], yb[:, q, :], ACT.Gelu).then_inc(y_gelu, 1)
                        round_unit(u + 1 + SPL, it, 4)
                        act.wait_ge(prod, m + 1 + it * 2)
                        nc.scalar.copy(one(Ah, it, q), ab[:, q, :]).then_inc(ah_ready, 1)
                norm = 2 * layer + 2
                nc.scalar.activation(lamb[:, 7:8], eps[:, 0:1], ACT.Sqrt)
                for n in range(KC):
                    for r in range(3):
                        round_unit(U_DN[layer] + 3 * n + r + SPL)
                    square(norm, n)
                    if layer == 0:
                        gain_round(norm, n)
                if layer == 0:
                    norm_root(norm)

            attention(0)
            project_out(U_OUT0, 1)
            ffn(0)
            def place1(v):
                v += len(TURN0)
                act.wait_ge(v_turned, v + 1)
                w = v - len(TURN0)
                dst = (Vc, Vd)[w // 4][:, :, P * (w % 4):P * (w % 4 + 1)]
                nc.scalar.copy(dst, bank[:, 4 + v % 2, :].rearrange("p (t c) -> p t c", t=QT)).then_inc(v_placed, 1)

            act.wait_ge(lam_dots, 1)
            nc.scalar.activation(lamb[:, 2:4], lamb[:, 0:2], ACT.Exp).then_inc(lam_exps, 1)
            for n in range(LATE[0]):
                round_unit(U_IN1 + n + SPL)
                if n - 1 in TURN1:
                    place1(TURN1.index(n - 1))
            attention(1)
            project_out(U_OUT1, 3)
            ffn(1)
            act.wait_ge(sq_summed, 4)
            nc.scalar.activation(xs[:, 1, :], bank[:, 7, 0:QT], ACT.Sqrt, bias=eps[:, 0:1], scale=1.0 / D).then_inc(out_std, 1)
            act.wait_ge(out_inverse, 1)
            act.wait_ge(fin_copied, KC)
            for t in range(QT // 2, QT):
                nc.scalar.mul(xout[:, t, :], xout[:, t, :], xs[:, 0, t:t + 1]).then_inc(out_scaled_act, 1)

        @block.vector
        def _(dve):
            count = [0]

            def step(ins):
                count[0] += 1
                ins.then_inc(dstep, 1)
                dve.wait_ge(dstep, count[0])

            def rest_of_gain(norm, k):
                dve.wait_ge(hh_ready, norm * KC + k + 1)
                nc.vector.scalar_tensor_tensor(out=Hl[:, k, :], in0=XT[:, k, :], scalar=gain(norm, k),
                                               in1=Hh[:, k, :].bitcast(F32), op0=ALU.mult,
                                               op1=ALU.subtract).then_inc(h_ready, 1)

            def inverse_rms(norm):
                dve.wait_ge(rms_ready, norm)
                step(nc.vector.reciprocal(rs[:], rs[:]))

            c0 = 0
            for b, n in enumerate((PR_A, 4 * CONV_W, 4 * FC, 4 * FC)):
                dve.wait_ge(turned, b + 1)
                nc.vector.tensor_copy(prm[:, c0:c0 + n], bank[:, b, 0:n]).then_inc(param_copied, 1)
                c0 += n
            dve.wait_ge(x_std, 1)
            nc.vector.reciprocal(xs[:, 1, :], xs[:, 1, :]).then_inc(x_inverse, 1)
            dve.wait_ge(x_inverse, 1)
            for t in range(QT // 2):
                nc.vector.tensor_scalar(xn[:, t, :], xin[:, t, :], xs[:, 1, t:t + 1], None, ALU.mult).then_inc(x_scaled, 1)
            dve.wait_ge(param_copied, 4)
            for k in range(KC):
                dve.wait_ge(hh_ready, k + 1)
                nc.vector.scalar_tensor_tensor(out=Hl[:, k, :], in0=bank[:, 4 + k % 4, :], scalar=prm[:, PR_MIX + k:PR_MIX + k + 1],
                                               in1=Hh[:, k, :].bitcast(F32), op0=ALU.mult,
                                               op1=ALU.subtract).then_inc(h_ready, 1)
            for k in range(KC):
                dve.wait_ge(turned, 4 + k + 1)
                nc.vector.tensor_copy(XT[:, k, :], bank[:, 4 + k % 4, :]).then_inc(xt_ready, 1)

            def glu(c):
                wait_read(dve, O_IN0 + 2 * c)
                o = O_IN0 + 2 * c + 1
                dve.wait_ge(unit_done, U_IN0 + 2 * c + 2)
                nc.vector.tensor_tensor(Uc[:, c, PAD:PAD + S], yb[:, c % 2, :], bank[:, o % NACC, :],
                                        ALU.mult).then_inc(tile_read[o % NACC], 1)

            last_tap = {}

            def tap(c):
                t, n = last_tap.get(c, (-1, 0))
                t += 1
                w = PR_DWW + c
                if t == 0:
                    wait_read(dve, O_IN0 + 2 * c + 1)
                    ins = nc.vector.tensor_scalar(CA[:, c, :], Uc[:, c, 0:S], prm[:, w:w + 1],
                                                  prm[:, PR_DWB + c:PR_DWB + c + 1], ALU.mult, ALU.add)
                else:
                    dve.wait_ge(dstep, n)
                    ins = nc.vector.scalar_tensor_tensor(out=CA[:, c, :], in0=Uc[:, c, t:t + S],
                                                         scalar=prm[:, w + 4 * t:w + 4 * t + 1], in1=CA[:, c, :],
                                                         op0=ALU.mult, op1=ALU.add)
                if t == CONV_W - 1:
                    ins.then_inc(conv_done, 1)
                    n = 0
                else:
                    count[0] += 1
                    n = count[0]
                    ins.then_inc(dstep, 1)
                last_tap[c] = (t, n)

            def flat(kv):
                wait_read(dve, O_IN0 + 8 + kv)
                for g in range(2):
                    src = spread(KK[:, kv, g, 0:1], (2, NPAIR), (16, NCMP))
                    pos = spread(prm[:, PR_POS + NPAIR * kv:PR_POS + NPAIR * kv + 1], (1, NPAIR), (0, NCMP))
                    ins = nc.vector.tensor_tensor(FT[:, kv, :, NCMP * g:NCMP * (g + 1)], src, pos, ALU.add)
                ins.then_inc(ft_ready, 1)

            def split_keys(br):
                dve.wait_ge(k_hi, br + 1)
                o = O_IN0 + TILE_K[br]
                for g in range(2):
                    half = slice(HD * g, HD * g + HD)
                    for to in range(2):
                        ins = nc.vector.tensor_tensor(Kd[HD * to:HD * to + HD, 2 * br + g, 1, :], bank[half, o % NACC, :],
                                                      Kd[half, 2 * br + g, 0, :].bitcast(F32), ALU.subtract)
                ins.then_inc(tile_read[o % NACC], 1)

            def split_queries(c):
                wait_read(dve, O_IN0 + TILE_Q[c])
                for g in range(2):
                    half, other = slice(HD * g, HD * g + HD), slice(HD * (1 - g), HD * (1 - g) + HD)
                    ins = nc.vector.tensor_tensor(Qs[other, 4 * g + c, :], Q0[half, c, :],
                                                  Qs[half, 4 * g + c, :].bitcast(F32), ALU.subtract)
                ins.then_inc(q_split, 1)

            dve.wait_ge(memsets, N_MEMSETS)
            glu(0)
            for t in range(14):
                tap(0)
            glu(1)
            for t in range(8):
                tap(0)
                tap(1)
            glu(2)
            for t in range(9):
                tap(0)
                tap(1)
            glu(3)
            for t in range(14):
                tap(1)
                tap(2)
                if t == 9:
                    flat(0)
            flat(1)
            for t in range(17):
                tap(2)
                tap(3)
            for t in range(14):
                tap(3)
            split_keys(0)
            dve.wait_ge(ln_mean, 1)
            for c in range(4):
                nc.vector.scalar_tensor_tensor(out=CA[:, c, :], in0=bank[:, 4, :], scalar=-1.0 / 512, in1=CA[:, c, :],
                                               op0=ALU.mult, op1=ALU.add).then_inc(ln_centered, 1)
            split_keys(1)
            split_queries(0)
            dve.wait_ge(ln_std, 1)
            dve.wait_ge(ln_sq, 4)
            step(nc.vector.reciprocal(tm[:, 2, :], tm[:, 2, :]))
            for c in range(4):
                nc.vector.scalar_tensor_tensor(out=CA[:, c, :], in0=CA[:, c, :], scalar=prm[:, PR_LNG + c:PR_LNG + c + 1],
                                               in1=tm[:, 2, :], op0=ALU.mult, op1=ALU.mult).then_inc(ln_scaled, 1)
            split_queries(1)
            split_queries(2)

            def conv_rest(c):
                dve.wait_ge(cc_hi, c + 1)
                nc.vector.tensor_tensor(Hl[:, 4 + c, :], CA[:, c, :], Hh[:, 4 + c, :].bitcast(F32),
                                        ALU.subtract).then_inc(cc_ready, 1)

            def mark(ins):
                count[0] += 1
                ins.then_inc(dstep, 1)

            def settled():
                dve.wait_ge(dstep, count[0])

            def combine0(i, r):
                if r == 8:
                    dve.wait_ge(probs_ready, PER * i + 8)
                    mark(nc.vector.reciprocal(Rs[:, 0:16], Ls[:, i % 2, 0:16]))
                elif r == 9:
                    settled()
                    mark(nc.vector.tensor_tensor(Cs[:, 0:16].rearrange("p (b h) -> p b h", b=2),
                                                 Rs[:, 0:16].rearrange("p (b h) -> p b h", b=2),
                                                 spread(gate[:, i, 0:1], (1, 2), (3, 8)), ALU.mult))
                elif r == 10:
                    settled()
                    mark(nc.vector.tensor_scalar(Cs[:, 0:8], Cs[:, 0:8], cmask[:, i, 32:33], None, ALU.mult))
                elif r == 11:
                    dve.wait_ge(oc_made, i + 1)
                    settled()
                    oc = spread(bank[:, 2, 2 * P:2 * P + 1], (S, 2), (HD, 4), (1, HD))
                    nc.vector.tensor_tensor(tm[:, 0, :].rearrange("p (g h d) -> p g h d", g=2, h=4), oc,
                                            spread(Cs[:, 0:1], (4, 2), (1, 4), (0, HD)), ALU.mult)
                elif r in (12, 20):
                    half = (r - 12) // 8
                    settled()
                    dve.wait_ge(pv_done, PER * i + 8 * half + 8)
                    n = 8 + 8 * half
                    nc.vector.tensor_tensor(tm[:, 1, :].rearrange("p (h d) -> p h d", h=8),
                                            bank[:, half, :].rearrange("p (h d) -> p h d", h=8),
                                            spread(Cs[:, n:n + 1], (1, 8), (0, HD)), ALU.mult).then_inc((read_a, read_b)[half], 1)
                elif r == 17:
                    dve.wait_ge(probs_ready, PER * (i + 1))
                    mark(nc.vector.reciprocal(Rs[:, 16:24], Ls[:, i % 2, 16:24]))
                elif r == 18:
                    settled()
                    dve.wait_ge(combined_a, i + 1)
                    mark(nc.vector.tensor_tensor(Cs[:, 16:24], Rs[:, 16:24], spread(gate[:, i, 2:3], (3, 8)), ALU.mult))

            def mix(j):
                i, r = divmod(j, PER)
                h, w = r // 2, P * (i + 1)
                dve.wait_ge(probs_ready, JOBS + j + 1)
                step(nc.vector.reciprocal(Rs[:, 4 + h:5 + h], Ls[:, i % 2, 4 + h:5 + h]))
                step(nc.vector.scalar_tensor_tensor(out=Cs[:, h:h + 1], in0=Rs[:, 4 + h:5 + h], scalar=lamb[:, 4:5],
                                                    in1=Ls[:, i % 2, h:h + 1], op0=ALU.mult, op1=ALU.mult))
                nc.vector.scalar_tensor_tensor(out=Pb[:, j % 4, 0:w], in0=Pb[:, j % 4, 0:w], scalar=Cs[:, h:h + 1],
                                               in1=Pb[:, (j - 1) % 4, 0:w], op0=ALU.mult, op1=ALU.add).then_inc(mixed, 1)

            def combine1(i, r):
                heads = lambda t: t.rearrange("p (h d) -> p h d", h=4)
                if r == 9:
                    dve.wait_ge(probs_ready, JOBS + PER * i + 8)
                    mark(nc.vector.reciprocal(Rs[:, 0:4], Ls[:, i % 2, 0:4]))
                elif r == 13:
                    settled()
                    dve.wait_ge(pv_done, turns[1, PER * i + 7] + 1)
                    nc.vector.tensor_tensor(heads(tn[:, kept(i), :]), heads(bank[:, 0, :]),
                                            spread(Rs[:, 0:1], (1, 4), (0, P)), ALU.mult).then_inc(read_a, 1)
                elif r == 16:
                    dve.wait_ge(o_product, i + 1)
                    nc.vector.tensor_reduce(Rs[:, sums_at(i)], heads(tn[:, 1, :]), AXX, ALU.add).then_inc(o_squared, 1)
                elif r == 18 and i in ROOTS:
                    dve.wait_ge(o_rms, i - 1)
                    w = 4 * len(ROOTS[i])
                    mark(nc.vector.reciprocal(Rs[:, 32:32 + w], Rs[:, 32:32 + w]))
                elif i in ROOTS and r in (19, 22, 24)[0:len(ROOTS[i])]:
                    settled()
                    n = (19, 22, 24).index(r)
                    slot = tn[:, kept(ROOTS[i][n]), :]
                    nc.vector.tensor_tensor(heads(slot), heads(slot), spread(Rs[:, 32 + 4 * n:33 + 4 * n], (1, 4), (0, P)),
                                            ALU.mult).then_inc(combined_a, 1)
                elif r == 20:
                    dve.wait_ge(probs_ready, JOBS + PER * (i + 1))
                    mark(nc.vector.reciprocal(Rs[:, 8:16], Ls[:, i % 2, 8:16]))
                elif r == 21:
                    settled()
                    dve.wait_ge(pv_done, turns[1, PER * i + PER - 1] + 1)
                    nc.vector.tensor_tensor(tn[:, 2, :].rearrange("p (h d) -> p h d", h=8),
                                            bank[:, 2, :].rearrange("p (h d) -> p h d", h=8),
                                            spread(Rs[:, 8:9], (1, 8), (0, HD)), ALU.mult).then_inc(read_b, 1)

            def place1(n):
                kind, idx, _, _ = UN1[n]
                o = O_IN1 + n
                src = bank[:, o % NACC, :]
                free = tile_read[o % NACC]
                dve.wait_ge(unit_done, U_IN1 + n + 1)
                if kind == "q":
                    nc.vector.scalar_tensor_tensor(out=Q1[:, idx, :], in0=src, scalar=HD ** -0.5, in1=rs1[:], op0=ALU.mult,
                                                   op1=ALU.mult).then_inc(free, 1)
                elif kind == "k":
                    nc.vector.tensor_tensor(K1[:, idx, :], src, rs1[:], ALU.mult).then_inc(free, 1)
                else:
                    v = len(TURN0) + TURN1.index(n)
                    dve.wait_ge(v_turned, v - 1)
                    nc.vector.tensor_tensor(tn[:, v % 2, :], src, rs1[:], ALU.mult).then_inc(free, 1)

            def attention(layer):
                J = JOBS * layer
                dve.wait_ge(small_loaded, 64)
                dve.wait_ge(strips_loaded, 16 * (layer + 1))
                for s in range(STEPS):
                    i, r = divmod(s, PER)
                    v = turns.get((layer, s - LAG_T[layer]), 1)
                    if v % 2 == 0:
                        w = P * ((s - LAG_T[layer]) // PER + 1)
                        dve.wait_ge(probs_turned, v + 1)
                        if v >= 2:
                            dve.wait_ge(pv_done, v - 1)
                        nc.vector.tensor_copy(PTs[:, 0, 0:w], bank[:, 6, 0:w]).then_inc(pt_copied[0], 1)
                    if s < JOBS:
                        T = job(layer, s)[1]
                        w = P * (i + 1)
                        n = use[layer, s]
                        dve.wait_ge(qk_done, J + s + 1)
                        if J + s >= 3:
                            dve.wait_ge(probs_ready, max(J, J + s - 2))
                        nc.vector.tensor_tensor_reduce(out=S2[:, s % 3, 0:w], in0=bank[:, score_bank(n), 0:w], in1=T, scale=-1.0,
                                                       scalar=3.0e38, op0=ALU.add, op1=ALU.min,
                                                       accum_out=nmx[:, s % 3:s % 3 + 1]).then_inc(scores_read, 1)
                    if (layer, s - LAG_M) in turns and map_of(layer, s - LAG_M) == 1:
                        mix(s - LAG_M)
                    for key in CT[layer].get(s, []):
                        n = use[layer, "ct", key]
                        c0 = 4 * key[1]
                        dve.wait_ge(ct_hi, CTN[layer, "ct", key] + 1)
                        ts = slice(P * key[0], P * (key[0] + 1))
                        src = bank[:, score_bank(n), :].rearrange("p (c t) -> p c t", c=4)
                        if (layer, key[1]) == (1, 0):
                            nc.vector.scalar_tensor_tensor(out=Hl[:, c0:c0 + 4, ts], in0=src, scalar=dng[:, 1:2],
                                                           in1=Hh[:, c0:c0 + 4, ts].bitcast(F32), op0=ALU.mult,
                                                           op1=ALU.subtract).then_inc(scores_read, 1)
                        else:
                            nc.vector.tensor_tensor(Hl[:, c0:c0 + 4, ts], src, Hh[:, c0:c0 + 4, ts].bitcast(F32),
                                                    ALU.subtract).then_inc(scores_read, 1)
                    if layer == 0 and i < QT:
                        if r == STEP_CMP["shift"]:
                            dve.wait_ge(sc_made, i + 1)
                            mark(nc.vector.tensor_tensor(Sm[:].rearrange("p (g h) n -> p g h n", g=2),
                                                         spread(bank[:, 2, 0:1], (32, 2), (64, 4), (1, 32)),
                                                         spread(cmask[:, i, 0:1], (0, 2), (0, 4), (1, 32)), ALU.add))
                        if r == STEP_CMP["shift"] + 1:
                            settled()
                            mark(nc.vector.tensor_reduce(cmx[:], Sm[:], AXX, ALU.max))
                        if r == STEP_CMP["shift"] + 2:
                            settled()
                            nc.vector.tensor_tensor(Sm[:], Sm[:], spread(cmx[:, 0:1], (1, 8), (0, 32)),
                                                    ALU.subtract).then_inc(sc_shifted, 1)
                        if r == STEP_CMP["sum"]:
                            dve.wait_ge(pc_ready, i + 1)
                            nc.vector.tensor_reduce(Ls[:, i % 2, 0:8], Pc[:], AXX, ALU.add)
                        if r == STEP_CMP["copy"]:
                            dve.wait_ge(pc_turned, i + 1)
                            nc.vector.tensor_copy(PcT[:], bank[:, 3, 0:2 * P].rearrange("p (g t) -> p g t", g=2)).then_inc(pc_copied, 1)
                    if layer == 0 and s == 2:
                        split_queries(3)
                    if layer == 1 and s in STEP_LATE:
                        place1(LATE[STEP_LATE[s]])
                    for t in (i, i - 1):
                        if 0 <= t < QT:
                            (combine0, combine1)[layer](t, s - PER * t)
                    if layer == 0 and s - 1 in STEP_U:
                        conv_rest(STEP_U[s - 1])

            def project_out(layer, u0, o0, norm):
                for n in range(KC):
                    dve.wait_ge(unit_done, u0 + n + 1)
                    nc.vector.tensor_tensor(XT[:, n, :], XT[:, n, :], bank[:, (o0 + n) % NACC, :], ALU.add).then_inc(xt_ready, 1)
                for k in range(KC):
                    rest_of_gain(norm, k)
                inverse_rms(norm)

            def leave(k):
                dve.wait_ge(fin_turned, k + 1)
                nc.vector.tensor_copy(xout[:, :, k * P:(k + 1) * P],
                                      bank[:, 4 + k % 2, :].rearrange("p (t c) -> p t c", t=QT)).then_inc(fin_copied, 1)

            def ffn(layer):
                u0, o0 = U_GU[layer], O_GU[layer]
                base = count[0]
                with dve.Fori(0, FC // 2) as it:
                    for q in range(2):
                        u, o, m = u0 + 2 * q, o0 + 2 * q, FC * layer + q
                        cols = prm_ff(layer, it, q)
                        y, a, gs = yb[:, q, :], ab[:, q, :], hf[:, q, :]
                        gt, up = bank[:, o % NACC, :], bank[:, (o + 1) % NACC, :]
                        dve.wait_ge(unit_done, u + 1 + it * 4)
                        nc.vector.tensor_tensor(gs, gt, rs[:], ALU.mult).then_inc(tile_read[o % NACC], 1)
                        dve.wait_ge(y_base, m + 1 + it * 2)
                        nc.vector.scalar_tensor_tensor(out=y[:, 1:S], in0=gs[:, 0:S - 1], scalar=cols[1], in1=y[:, 1:S],
                                                       op0=ALU.mult, op1=ALU.add).then_inc(dstep, 1)
                        dve.wait_ge(dstep, base + q + 1 + it * 2)
                        nc.vector.scalar_tensor_tensor(out=y[:, 2:S], in0=gs[:, 0:S - 2], scalar=cols[0], in1=y[:, 2:S],
                                                       op0=ALU.mult, op1=ALU.add).then_inc(y_conv, 1)
                        dve.wait_ge(unit_done, u + 2 + it * 4)
                        nc.vector.tensor_tensor(a, up, rs[:], ALU.mult).then_inc(tile_read[(o + 1) % NACC], 1)
                        dve.wait_ge(tile_read[(o + 1) % NACC], reads(o + 1) + it)
                        dve.wait_ge(y_gelu, m + 1 + it * 2)
                        nc.vector.tensor_tensor(a, y, a, ALU.mult).then_inc(prod, 1)
                        dve.wait_ge(ah_ready, m + 1 + it * 2)
                        nc.vector.tensor_tensor(one(Al, it, q), a, one(Ah, it, q).bitcast(F32), ALU.subtract).then_inc(a_ready, 1)
                count[0] = base + FC
                for n in range(KC):
                    dve.wait_ge(unit_done, U_DN[layer] + 3 * n + 3)
                    nc.vector.tensor_tensor(XT[:, n, :], XT[:, n, :], bank[:, (O_DN[layer] + n) % NACC, :],
                                            ALU.add).then_inc(xt_ready, 1)
                    if layer == 0:
                        rest_of_gain(2, n)
                    else:
                        if n >= 2:
                            dve.wait_ge(fin_turned, n - 1)
                        dve.wait_ge(xt_ready, 4 * KC + n + 1)
                        nc.vector.tensor_scalar(hf[:, n % 2, :], XT[:, n, :], prm[:, PR_FIN + n:PR_FIN + n + 1], None,
                                                ALU.mult).then_inc(fin_ready, 1)
                        if n >= 1:
                            leave(n - 1)

            attention(0)
            project_out(0, U_OUT0, O_OUT0, 1)
            ffn(0)
            dve.wait_ge(small_loaded, 64)
            step(nc.vector.tensor_tensor(lamp[:, 0, :], lamp[:, 0, :], lamp[:, 1, :], ALU.mult))
            step(nc.vector.tensor_tensor(lamp[:, 2, :], lamp[:, 2, :], lamp[:, 3, :], ALU.mult))
            nc.vector.tensor_reduce(lamb[:, 0:2], spread(lamp[:, 0, 0:1], (2 * HD, 2), (1, HD)), AXX,
                                    ALU.add).then_inc(lam_dots, 1)
            dve.wait_ge(rms_ready, 2)
            step(nc.vector.reciprocal(rs1[:], rs[:]))
            dve.wait_ge(lam_exps, 1)
            step(nc.vector.tensor_tensor(lamb[:, 4:5], lamb[:, 3:4], lamb[:, 2:3], ALU.subtract))
            step(nc.vector.tensor_scalar(lamb[:, 4:5], lamb[:, 4:5], -LAM_INIT, None, ALU.add))
            nc.vector.tensor_scalar(dng[:, 1:2], dng[:, 0:1], 1.0 - LAM_INIT, None, ALU.mult).then_inc(gain_ready, 1)
            for n in range(LATE[0]):
                place1(n)
            attention(1)
            project_out(1, U_OUT1, O_OUT1, 3)
            ffn(1)
            leave(KC - 1)
            dve.wait_ge(out_std, 1)
            nc.vector.reciprocal(xs[:, 0, :], xs[:, 1, :]).then_inc(out_inverse, 1)
            dve.wait_ge(out_inverse, 1)
            dve.wait_ge(fin_copied, KC)
            for t in range(QT // 2):
                nc.vector.tensor_scalar(xout[:, t, :], xout[:, t, :], xs[:, 0, t:t + 1], None, ALU.mult).then_inc(out_scaled_dve, 1)


INPUTS = ["x", "rel_bias_table", "mix_norm_g", "ffn_norm_g", "ffn_w_gate", "ffn_w_up", "ffn_conv_w", "ffn_conv_b",
          "ffn_w_down", "ev_w_in", "ev_w_out", "nsa_phi_pos", "nsa_phi_w1", "nsa_phi_w2", "conv_dw_w", "conv_dw_b",
          "conv_ln_g", "conv_ln_b", "od_w_in", "od_w_out", "diff_lambda", "diff_norm_g", "final_norm_g"]


def shape_constants():
    import numpy as np

    onehot = np.zeros((BUCKETS + 1, 2, FROW), np.float32)
    exact = BUCKETS // 2
    for j in range(FROW):
        d = j - (P - 1)
        if d < 0 or d >= S:
            onehot[BUCKETS, :, j] = NEG
            continue
        b = d if d < exact else min(BUCKETS - 1, exact + int(math.log(d / exact) / math.log(2048 / exact) * (BUCKETS - exact)))
        onehot[b, :, j] = 1.0
        m = (d <= 128) + (d % 4 == 0) + (d % 16 == 0)
        onehot[BUCKETS, 1, j] = math.log(m) if m else NEG
    cmask = np.zeros((P, QT, 33), np.float32)
    for i in range(QT):
        for p in range(P):
            for n in range(32):
                if n >= NCMP or 16 * n + 31 > P * i + p:
                    cmask[p, i, n] = NEG
            cmask[p, i, 32] = float(P * i + p >= 31)
    return {"onehot": onehot, "ident": np.eye(P, dtype=np.float32), "cmpmask": cmask}


def kernel(**inputs):
    import numpy as np
    import concourse.bacc as bacc
    from concourse.bass_utils import run_bass_kernel_spmd

    nc = bacc.Bacc("TRN2", target_bir_lowering=False, num_devices=1)
    arrays, args = {}, []
    given = {name: np.ascontiguousarray(inputs[name]) for name in INPUTS}
    given.update(shape_constants())
    for name, a in given.items():
        arrays[f"in_{name}"] = a
        args.append(nc.dram_tensor(f"in_{name}", a.shape, mybir.dt.from_np(a.dtype), kind="ExternalInput").ap())
    args.append(nc.dram_tensor("bias_rows", (20, FROW), F32, kind="Internal").ap())
    args.append(nc.dram_tensor("out_0", (1, S, D), F32, kind="ExternalOutput").ap())
    build(nc, *args)
    r = run_bass_kernel_spmd(nc, [arrays], core_ids=[0])
    return r.results[0]["out_0"]
```
